# Optimizing a Trainium2 kernel written in Bass

```python
import math
import jax, jax.numpy as jnp
from jax import lax
import numpy as np

D_MODEL = 1024
BATCH = 1
SEQ = 1024
DEPTH = 1
DEC_BATCH = 8
DEC_SEQ = 8
PAST_LEN = 8192
PAGE_SIZE = 128

D_CONV = D_MODEL
CONV_W = 3
GLA_HEADS = 4
GLA_DK = D_MODEL // 2
GLA_DV = D_MODEL
DK_HEAD = GLA_DK // GLA_HEADS
DV_HEAD = GLA_DV // GLA_HEADS
GATE_RANK = 16
GATE_NORMALIZER = 16.0
GLA_CHUNK = 64
D_IN = 3 * D_CONV + 2 * GLA_DK + 2 * GLA_DV + GATE_RANK + 2 * D_MODEL
N_EXPERTS = 64
TOP_K = 8
N_GROUPS = 8
TOPK_GROUPS = 4
D_EXPERT = D_MODEL // 4
D_SHARED = D_MODEL // 4
ROUTED_SCALE = 2.5
MOE_BLOCK = 128
EPS = 1e-6

kernel_name = "hybrid_conv_gla_moe_adaln_step"

def _rmsnorm(x, w):
    xf = x.astype(jnp.float32)
    y = xf * lax.rsqrt(jnp.mean(xf * xf, axis=-1, keepdims=True) + EPS)
    return (y * w.astype(jnp.float32)).astype(x.dtype)

def _split_cols(p):
    sizes = [D_CONV, D_CONV, D_CONV, GLA_DK, GLA_DK, GLA_DV, GLA_DV, GATE_RANK, D_MODEL, D_MODEL]
    outs = []
    start = 0
    for s in sizes:
        outs.append(p[..., start:start + s])
        start += s
    return outs

def _gla_chunked(q, k, v, log_a, s0):
    bsz, nh, L, _ = q.shape
    dv = v.shape[-1]
    C = math.gcd(L, GLA_CHUNK)
    n = L // C

    def to_chunks(t):
        return jnp.moveaxis(t.reshape(bsz, nh, n, C, t.shape[-1]), 2, 0)

    causal = jnp.tril(jnp.ones((C, C), dtype=bool))

    def step(S, inp):
        qc, kc, vc, gc = inp
        b = jnp.cumsum(gc, axis=2)
        b_end = b[:, :, -1:, :]
        q_dec = qc * jnp.exp(b)
        o_inter = jnp.einsum('bhcd,bhde->bhce', q_dec, S)
        scores = jnp.einsum('bhcd,bhsd->bhcs', q_dec, kc * jnp.exp(-b))
        scores = jnp.where(causal, scores, 0.0)
        o = o_inter + jnp.einsum('bhcs,bhse->bhce', scores, vc)
        S_new = (jnp.exp(b_end[:, :, 0, :])[..., None] * S
                 + jnp.einsum('bhsd,bhse->bhde', kc * jnp.exp(b_end - b), vc))
        return S_new, o

    S, o = lax.scan(step, s0, (to_chunks(q), to_chunks(k), to_chunks(v), to_chunks(log_a)))
    o = jnp.moveaxis(o, 0, 2).reshape(bsz, nh, L, dv)
    return o, S

def _mixer(h, conv_state, gla_state, w_in, conv_w, w_gk, b_gk, gla_norm_w,
           w_out_conv, w_out_gla, w_o):
    bsz, L, _ = h.shape
    b_gate, c_gate, h_conv, q, k, v, g, z, u_a, u_b = _split_cols(h @ w_in)
    pre = c_gate * h_conv
    padded = jnp.concatenate([conv_state.astype(pre.dtype), pre], axis=1)
    conv = conv_w[0] * padded[:, 0:L]
    for j in range(1, CONV_W):
        conv = conv + conv_w[j] * padded[:, j:j + L]
    y_a = (b_gate * conv) @ w_out_conv
    new_conv = padded[:, L:]
    log_a = jax.nn.log_sigmoid((z @ w_gk + b_gk).astype(jnp.float32)) / GATE_NORMALIZER

    def heads(t, dh):
        return t.reshape(bsz, L, GLA_HEADS, dh).transpose(0, 2, 1, 3).astype(jnp.float32)

    o, S = _gla_chunked(heads(q, DK_HEAD) * (DK_HEAD ** -0.5), heads(k, DK_HEAD),
                        heads(v, DV_HEAD), heads(log_a, DK_HEAD),
                        gla_state.astype(jnp.float32))
    o = _rmsnorm(o, gla_norm_w).transpose(0, 2, 1, 3).reshape(bsz, L, GLA_DV).astype(h.dtype)
    y_b = (o * jax.nn.silu(g)) @ w_out_gla
    merged = jax.nn.sigmoid(u_a) * y_a + jax.nn.sigmoid(u_b) * y_b
    return merged @ w_o, new_conv, S.astype(gla_state.dtype)

def _moe(h, router_w, router_bias, we_gate, we_up, we_down, ws_gate, ws_up, ws_down):
    T, D = h.shape
    E = N_EXPERTS
    scores = jax.nn.sigmoid(h.astype(jnp.float32) @ router_w.astype(jnp.float32))
    choice = scores + router_bias.astype(jnp.float32)
    grp = choice.reshape(T, N_GROUPS, E // N_GROUPS)
    grp_score = lax.top_k(grp, 2)[0].sum(-1)
    _, gidx = lax.top_k(grp_score, TOPK_GROUPS)
    gmask = jnp.any(gidx[..., None] == jnp.arange(N_GROUPS), axis=1)
    emask = jnp.repeat(gmask, E // N_GROUPS, axis=1)
    _, eidx = lax.top_k(jnp.where(emask, choice, -jnp.inf), TOP_K)
    w = jnp.take_along_axis(scores, eidx, axis=1)
    w = w / jnp.sum(w, axis=-1, keepdims=True) * ROUTED_SCALE

    A = T * TOP_K
    flat_e = eidx.reshape(-1)
    flat_tok = jnp.repeat(jnp.arange(T, dtype=jnp.int32), TOP_K)
    order = jnp.argsort(flat_e)
    se, stok, sw = flat_e[order], flat_tok[order], w.reshape(-1)[order]
    counts = jnp.bincount(flat_e, length=E)
    starts = jnp.cumsum(counts) - counts
    padded = (counts + MOE_BLOCK - 1) // MOE_BLOCK * MOE_BLOCK
    pends = jnp.cumsum(padded)
    pstarts = pends - padded
    dest = pstarts[se] + (jnp.arange(A) - starts[se])
    n_blocks = (A + E * (MOE_BLOCK - 1) + MOE_BLOCK - 1) // MOE_BLOCK
    P = n_blocks * MOE_BLOCK
    tok_buf = jnp.full((P,), T, dtype=jnp.int32).at[dest].set(stok)
    w_buf = jnp.zeros((P,), jnp.float32).at[dest].set(sw)
    blk_e = jnp.clip(jnp.searchsorted(pends, jnp.arange(n_blocks) * MOE_BLOCK, side='right'), 0, E - 1)
    hpad = jnp.concatenate([h, jnp.zeros((1, D), h.dtype)], axis=0)

    def run(args):
        tok, e = args
        xb = hpad[tok]
        act = jax.nn.silu(xb @ we_gate[e]) * (xb @ we_up[e])
        return act @ we_down[e]

    out = lax.map(run, (tok_buf.reshape(n_blocks, MOE_BLOCK), blk_e)).reshape(P, D)
    routed = jnp.zeros((T + 1, D), out.dtype).at[tok_buf].add(out * w_buf[:, None].astype(out.dtype))[:T]
    shared = (jax.nn.silu(h @ ws_gate) * (h @ ws_up)) @ ws_down
    return routed + shared

def _forward(x, c, conv_state, gla_state, w_ada, b_ada, norm1_w, w_in, conv_w, w_gk, b_gk,
             gla_norm_w, w_out_conv, w_out_gla, w_o, norm2_w, router_w, router_bias,
             we_gate, we_up, we_down, ws_gate, ws_up, ws_down, final_norm_w):
    bsz, L, D = x.shape
    new_convs, new_glas = [], []
    for l in range(DEPTH):
        mod = jax.nn.silu(c) @ w_ada[l] + b_ada[l]
        sh1, sc1, g1, sh2, sc2, g2 = jnp.split(mod, 6, axis=-1)
        h = _rmsnorm(x, norm1_w[l]) * (1.0 + sc1[:, None]) + sh1[:, None]
        mix, nc, ns = _mixer(h, conv_state[l], gla_state[l], w_in[l], conv_w[l], w_gk[l], b_gk[l],
                             gla_norm_w[l], w_out_conv[l], w_out_gla[l], w_o[l])
        x = x + g1[:, None] * mix
        h = _rmsnorm(x, norm2_w[l]) * (1.0 + sc2[:, None]) + sh2[:, None]
        ffn = _moe(h.reshape(bsz * L, D), router_w[l], router_bias[l], we_gate[l], we_up[l],
                   we_down[l], ws_gate[l], ws_up[l], ws_down[l]).reshape(bsz, L, D)
        x = x + g2[:, None] * ffn
        new_convs.append(nc)
        new_glas.append(ns)
    return _rmsnorm(x, final_norm_w), jnp.stack(new_convs), jnp.stack(new_glas)

def setup_inputs(seed: int = 0) -> dict:
    key = jax.random.key(seed)
    ks = jax.random.split(key, 32)

    def nrm(k, shape, s):
        return jax.random.normal(k, shape, jnp.float32) * s

    D = D_MODEL
    return {
        "x_prompt": nrm(ks[0], (BATCH, SEQ, D), 1.0),
        "x_sample": nrm(ks[1], (DEC_BATCH, DEC_SEQ, D), 1.0),
        "state_conv": nrm(ks[2], (DEPTH, DEC_BATCH, CONV_W - 1, D_CONV), 1.0),
        "state_gla": nrm(ks[3], (DEPTH, DEC_BATCH, GLA_HEADS, DK_HEAD, DV_HEAD), 0.5),
        "c_prompt": nrm(ks[4], (BATCH, D), 1.0),
        "c_sample": nrm(ks[5], (DEC_BATCH, D), 1.0),
        "w_ada": nrm(ks[6], (DEPTH, D, 6 * D), 0.5 * D ** -0.5),
        "b_ada": nrm(ks[7], (DEPTH, 6 * D), 0.02),
        "norm1_w": 1.0 + nrm(ks[8], (DEPTH, D), 0.02),
        "w_in": nrm(ks[9], (DEPTH, D, D_IN), D ** -0.5),
        "conv_w": nrm(ks[10], (DEPTH, CONV_W, D_CONV), CONV_W ** -0.5),
        "w_gk": nrm(ks[11], (DEPTH, GATE_RANK, GLA_DK), GATE_RANK ** -0.5),
        "b_gk": nrm(ks[12], (DEPTH, GLA_DK), 0.02),
        "gla_norm_w": 1.0 + nrm(ks[13], (DEPTH, DV_HEAD), 0.02),
        "w_out_conv": nrm(ks[14], (DEPTH, D_CONV, D), D_CONV ** -0.5),
        "w_out_gla": nrm(ks[15], (DEPTH, GLA_DV, D), GLA_DV ** -0.5),
        "w_o": nrm(ks[16], (DEPTH, D, D), D ** -0.5),
        "norm2_w": 1.0 + nrm(ks[17], (DEPTH, D), 0.02),
        "router_w": nrm(ks[18], (DEPTH, D, N_EXPERTS), D ** -0.5),
        "router_bias": nrm(ks[19], (DEPTH, N_EXPERTS), 0.01),
        "we_gate": nrm(ks[20], (DEPTH, N_EXPERTS, D, D_EXPERT), D ** -0.5),
        "we_up": nrm(ks[21], (DEPTH, N_EXPERTS, D, D_EXPERT), D ** -0.5),
        "we_down": nrm(ks[22], (DEPTH, N_EXPERTS, D_EXPERT, D), D_EXPERT ** -0.5),
        "ws_gate": nrm(ks[23], (DEPTH, D, D_SHARED), D ** -0.5),
        "ws_up": nrm(ks[24], (DEPTH, D, D_SHARED), D ** -0.5),
        "ws_down": nrm(ks[25], (DEPTH, D_SHARED, D), D_SHARED ** -0.5),
        "final_norm_w": 1.0 + nrm(ks[26], (D,), 0.02),
    }

def reference(x_prompt, x_sample, state_conv, state_gla, c_prompt, c_sample, w_ada, b_ada,
              norm1_w, w_in, conv_w, w_gk, b_gk, gla_norm_w, w_out_conv, w_out_gla, w_o,
              norm2_w, router_w, router_bias, we_gate, we_up, we_down, ws_gate, ws_up,
              ws_down, final_norm_w):
    params = (w_ada, b_ada, norm1_w, w_in, conv_w, w_gk, b_gk, gla_norm_w, w_out_conv,
              w_out_gla, w_o, norm2_w, router_w, router_bias, we_gate, we_up, we_down,
              ws_gate, ws_up, ws_down, final_norm_w)
    bp = x_prompt.shape[0]
    conv0 = jnp.zeros((DEPTH, bp, CONV_W - 1, D_CONV), x_prompt.dtype)
    gla0 = jnp.zeros((DEPTH, bp, GLA_HEADS, DK_HEAD, DV_HEAD), x_prompt.dtype)
    y_prompt, conv_p, gla_p = _forward(x_prompt, c_prompt, conv0, gla0, *params)
    y_sample, conv_s, gla_s = _forward(x_sample, c_sample, state_conv, state_gla, *params)
    return (y_prompt, y_sample, conv_p, gla_p, conv_s, gla_s)


_drawn_inputs = setup_inputs


def setup_inputs(seed=0):
    import zlib

    import numpy as np

    out = dict(_drawn_inputs(seed))
    spreads = {}
    factors = {'b_gk': 6.33, 'gla_norm_w': 5.314, 'final_norm_w': 2.775}
    for name, (base, spread) in spreads.items():
        noise = np.random.default_rng([zlib.crc32(name.encode()), seed]).standard_normal(out[name].shape)
        drawn = base * np.exp(spread * noise) if base else spread * noise
        out[name] = __import__('jax').numpy.asarray(drawn.astype(out[name].dtype))
    for name, factor in factors.items():
        out[name] = (out[name] * factor).astype(out[name].dtype)
    return out
```

```python
from contextlib import ExitStack

import numpy as np
import concourse.bass as bass
from concourse import mybir

ALU = mybir.AluOpType
ACT = mybir.ActivationFunctionType
F32 = mybir.dt.float32
I32 = mybir.dt.int32
U32 = mybir.dt.uint32
AX = mybir.AxisListType.X

P = 128
D = 1024
KD = D // P
TP = 1024
NB, LS = 8, 8
TS = NB * LS
T = TP + TS
NT = TP // P
HEADS, DK, DV = 4, 128, 256
CH = 64
RANK = 16
E, GROUPS, TOPG, TOPK = 64, 8, 4, 8
EG = E // GROUPS
FE = 256
SCALE_R = 2.5
EPS = 1e-6
B_ = 128
NBLK = (T * TOPK + E * (B_ - 1) + B_ - 1) // B_
NSLOT = NBLK * B_
PIECES = [(0, 384), (384, 384), (768, 320)]
C_B, C_C, C_H, C_Q, C_K, C_V, C_G, C_Z = 0, D, 2 * D, 3 * D, 3 * D + 512, 4 * D, 5 * D, 6 * D
C_UA, C_UB = 6 * D + RANK, 7 * D + RANK
SW = 384
V_ADA, V_N1, V_N2, V_CONV, V_BGK, V_GNW, V_END = 0, 48, 56, 64, 88, 92, 94
SH1, SC1, G1, SH2, SC2, G2 = range(6)
BIG = 1e30
CW = 3


def tok(t):
    return (t * P, P) if t < NT else (TP, TS)


class Tally:

    def __init__(self, sem):
        self.sem, self.base, self.n, self.outer = sem, 0, 0, None

    def mark(self, ins, by=1):
        ins.then_inc(self.sem, by)
        self.n += by

    def value(self):
        return self.base + self.n

    def loop(self, i, per):
        self.outer, self.per = self.base + self.n, per
        self.base, self.n = i * per + self.outer, 0

    def end(self, count):
        assert self.n == self.per, (self.n, self.per)
        self.base, self.n = self.outer + count * self.per, 0


class Chain(Tally):

    def __init__(self, eng, sem):
        super().__init__(sem)
        self.eng = eng

    def step(self, ins):
        self.mark(ins)
        self.eng.wait_ge(self.sem, self.value())


def flat2(ap):
    return [ap[:, 0:768].rearrange("p (a b) -> p a b", a=2), ap[:, 768:T]]


def slot2(ps):
    return [ps[:, 0:2, 0:384], ps[:, 2, 0:320]]


def slot3(ps):
    return [ps[:, 0:2, 0:384], ps[:, 2, 0:256], ps[:, 2, 256:320].rearrange("p (b t) -> p b t", b=NB)]


def flat3(ap):
    return [ap[:, 0:768].rearrange("p (a b) -> p a b", a=2), ap[:, 768:TP],
            ap[:, TP:T].rearrange("p (b t) -> p b t", b=NB)]


def padded3(ap):
    w = CW - 1
    return [ap[:, w:w + 768].rearrange("p (a b) -> p a b", a=2), ap[:, w + 768:w + TP],
            ap[:, w + TP:w + TP + NB * (LS + w)].rearrange("p (b t) -> p b t", b=NB)[:, :, w:w + LS]]


class Shared:
    pass


def build(nc, a, o):
    ctx = ExitStack()
    with ctx:
        early = []

        def sem(name):
            early.append(nc.alloc_semaphore(name))
            return early[-1]

        def maker(stack):
            return lambda name, shape, dt=F32: stack.enter_context(nc.sbuf_tensor(name, shape, dt))

        sb = maker(ctx)
        acc = [ctx.enter_context(nc.psum_tensor(f"acc{i}", [P, 3, 512], F32)) for i in range(2)]
        side = [ctx.enter_context(nc.psum_tensor(f"side{i}", [P, 512], F32)) for i in range(2)]

        xT_d = nc.dram_tensor("xT_d", [KD, P, T], F32, kind="Internal").ap()
        h2_d = nc.dram_tensor("h2_d", [T, D], F32, kind="Internal").ap()
        base_d = nc.dram_tensor("base_d", [T, D], F32, kind="Internal").ap()
        tok_d = nc.dram_tensor("tok_d", [NSLOT, 1], F32, kind="Internal").ap()
        g2_d = nc.dram_tensor("g2_d", [2, P, D], F32, kind="Internal").ap()
        y_d = nc.dram_tensor("y_d", [NSLOT, D], F32, kind="Internal").ap()

        ident = sb("ident", [P, P])
        ones = sb("ones", [P, P])
        eps = sb("eps", [P, 1])
        vec = sb("vec", [P, V_END])
        mod = sb("mod", [P, 6 * KD, NB + 1])
        amp = sb("amp", [P, 2, KD, NB + 1])

        g = Shared()
        g.dest8 = sb("dest8", [P, NT + 1, TOPK], U32)
        g.w8 = sb("w8", [P, NT + 1, TOPK])
        g.row = sb("row", [1, 2 * P], I32)
        g.idx = sb("idx", [P, NBLK], U32)
        g.nc, g.a, g.o, g.sem, g.maker, g.acc, g.side = nc, a, o, sem, maker, acc, side
        g.xT_d, g.h2_d, g.base_d, g.tok_d, g.y_d, g.g2_d = xT_d, h2_d, base_d, tok_d, y_d, g2_d
        g.ident, g.ones, g.eps, g.vec, g.mod, g.amp = ident, ones, eps, vec, mod, amp

        with ExitStack() as mix:
            sm = maker(mix)
            g.hT = sm("hT", [P, KD, T])
            g.ogT = sm("ogT", [P, KD, T])
            g.stT = sm("stT", [P, KD, 16])
            g.lastT = sm("lastT", [P, KD, 18])
            g.slab = [sm(f"slab{i}", [P, KD, SW]) for i in range(2)]
            with ExitStack() as yc:
                g.ycT = maker(yc)("ycT", [P, KD, T])
                stage1(g)
                stage2(g)
                stage3(g)
            stage4(g)
        nc.clear_and_free_semaphores(early)
        nc.all_engine_barrier()
        stage5(g)
        stage6(g)


class Norm:

    def __init__(self, g, tag, which, src, dst, sq, rst):
        self.g, self.which, self.src, self.dst, self.sq, self.rst = g, which, src, dst, sq, rst
        self.sq_ready = g.sem(f"{tag}_sq_ready")
        self.sq_used = g.sem(f"{tag}_sq_used")
        self.root = g.sem(f"{tag}_root")
        self.inv = g.sem(f"{tag}_inv")
        self.scaled = g.sem(f"{tag}_scaled")
        self.sample1 = g.sem(f"{tag}_sample1")
        self.sample2 = g.sem(f"{tag}_sample2")
        self.prompt = g.sem(f"{tag}_prompt")
        self.shift = (SH1, SH2)[which] * KD

    def act(self, eng, src_ready):
        g = self.g
        for k in range(KD):
            eng.wait_ge(*src_ready(k))
            if k >= 2:
                eng.wait_ge(self.sq_used, k - 1)
            g.nc.scalar.activation(self.sq[k % 2][:, 0:T], self.src[:, k, :], ACT.Square).then_inc(self.sq_ready, 1)
        eng.wait_ge(self.sq_used, KD)
        for d, s in zip(flat2(self.rst[:, 0:T]), slot2(g.acc[1])):
            g.nc.scalar.activation(d, s, ACT.Sqrt, scale=1.0 / D, bias=g.eps[:]).then_inc(self.root, 1)

    def act_prompt(self, eng):
        g = self.g
        for k in range(KD):
            eng.wait_ge(self.scaled, k + 1)
            g.nc.scalar.activation(self.dst[:, k, 0:TP], self.dst[:, k, 0:TP], ACT.Identity,
                                   scale=g.amp[:, self.which, k, 0:1],
                                   bias=g.mod[:, self.shift + k, 0:1]).then_inc(self.prompt, 1)

    def pe(self, eng):
        g = self.g
        for k in range(KD):
            eng.wait_ge(self.sq_ready, k + 1)
            for i, (s, n) in enumerate(PIECES):
                mm = g.nc.tensor.matmul(g.acc[1][:, i, 0:n], g.ones[:], self.sq[k % 2][:, s:s + n],
                                        start=(k == 0), stop=(k == KD - 1))
            mm.then_inc(self.sq_used, 1)

    def dve(self, eng):
        g = self.g
        eng.wait_ge(self.root, 2)
        g.nc.vector.reciprocal(self.rst[:, 0:T], self.rst[:, 0:T]).then_inc(self.inv, 1)
        eng.wait_ge(self.inv, 1)
        for k in range(KD):
            g.nc.vector.tensor_tensor(self.dst[:, k, :], self.src[:, k, :], self.rst[:, 0:T],
                                      ALU.mult).then_inc(self.scaled, 1)

    def dve_sample(self, eng):
        g = self.g
        v = self.dst[:, :, TP:T].rearrange("p k (b t) -> p k b t", b=NB)
        eng.wait_ge(self.scaled, KD)
        sc = g.amp[:, self.which, :, 1:NB + 1].unsqueeze(3).to_broadcast([P, KD, NB, LS])
        sh = g.mod[:, self.shift:self.shift + KD, 1:NB + 1].unsqueeze(3).to_broadcast([P, KD, NB, LS])
        g.nc.vector.tensor_tensor(v, v, sc, ALU.mult).then_inc(self.sample1, 1)
        eng.wait_ge(self.sample1, 1)
        g.nc.vector.tensor_tensor(v, v, sh, ALU.add).then_inc(self.sample2, 1)

    def wait_done(self, eng):
        eng.wait_ge(self.prompt, KD)
        eng.wait_ge(self.sample2, 1)


def stage1(g):
    nc, a, sem = g.nc, g.a, g.sem
    NSLAB = 6 * D // SW
    JS = SW // P
    with ExitStack() as st:
        sb = g.maker(st)
        vrow = sb("vrow", [V_END, P])
        crow = sb("crow", [(NB + 1) * KD, P])
        srow = sb("srow", [16, D])
        xin = [sb(f"xin{i}", [P, D]) for i in range(2)]
        xT = sb("xT", [P, KD, T])
        csig = sb("csig", [P, (NB + 1) * KD])
        cact = sb("cact", [P, KD, NB + 1])
        sq = [sb(f"sq1_{i}", [P, T]) for i in range(2)]
        rst = sb("rst1", [P, T])

        const0 = sem("const0")
        const = sem("const")
        rows_in = sem("rows_in")
        x_in = [sem(f"x_in{i}") for i in range(2)]
        ada_in = [sem(f"ada_in{i}") for i in range(2)]
        ada_used = [sem(f"ada_used{i}") for i in range(2)]
        rowsT = sem("rowsT")
        csig_ready = sem("csig_ready")
        vec_ready = sem("vec_ready")
        cact_ready = sem("cact_ready")
        x_turned = sem("x_turned")
        x_copied = sem("x_copied")
        mod_ready = sem("mod_ready")
        amp_ready = sem("amp_ready")
        xT_out = sem("xT_out")
        norm = Norm(g, "n1", 0, xT, g.hT, sq, rst)
        xp, xs = a["x_prompt"], a["x_sample"]
        blk = st.enter_context(nc.Block())

        @blk.gpsimd
        def _(pool):
            pool.memset(g.ident[:], 0.0).then_inc(const0, 1)
            pool.memset(g.ones[:], 1.0).then_inc(const, 1)
            pool.memset(g.eps[:], EPS).then_inc(const, 1)
            pool.wait_ge(const0, 1)
            pool.affine_select(out=g.ident[:], in_=g.ident[:], compare_op=ALU.not_equal, fill=1.0, base=0,
                               pattern=[[-1, P]], channel_multiplier=1).then_inc(const, 1)

        @blk.sync
        def _(sp):
            rows = [("b_ada", V_ADA, V_N1, a["b_ada"].rearrange("l (r c) -> (l r) c", c=P)),
                    ("n1", V_N1, V_N2, a["norm1_w"].rearrange("l (r c) -> (l r) c", c=P)),
                    ("n2", V_N2, V_CONV, a["norm2_w"].rearrange("l (r c) -> (l r) c", c=P)),
                    ("conv", V_CONV, V_BGK, a["conv_w"].rearrange("l w (r c) -> (l w r) c", c=P)),
                    ("bgk", V_BGK, V_GNW, a["b_gk"].rearrange("l (r c) -> (l r) c", c=P)),
                    ("gnw", V_GNW, V_END, a["gla_norm_w"].rearrange("l (r c) -> (l r) c", c=P))]
            for _, lo, hi, src in rows:
                sp.dma_start(vrow[lo:hi, :], src).then_inc(rows_in, 16)
            sp.dma_start(crow[0:KD, :], a["c_prompt"].rearrange("b (r c) -> (b r) c", c=P)).then_inc(rows_in, 16)
            sp.dma_start(crow[KD:, :], a["c_sample"].rearrange("b (r c) -> (b r) c", c=P)).then_inc(rows_in, 16)
            sp.dma_start(srow[:], a["state_conv"].rearrange("l b w d -> (l b w) d")).then_inc(rows_in, 16)
            with sp.Fori(0, NT // 2) as i:
                for u in range(2):
                    sp.wait_ge(x_turned, i * 2)
                    sp.dma_start(xin[u][:], xp[0, bass.ds(i * (2 * P) + u * P, P), :]).then_inc(x_in[u], 16)
            sp.wait_ge(x_turned, NT - 1)
            sp.dma_start(xin[0][0:TS, :], xs.rearrange("b t d -> (b t) d")).then_inc(x_in[0], 16)
            w = a["w_ada"][0].rearrange("(k p) f -> p k f", p=P)
            with sp.Fori(0, NSLAB // 2) as i:
                for u in range(2):
                    sp.wait_ge(ada_used[u], i)
                    sp.dma_start(g.slab[u][:], w[:, :, bass.ds(i * (2 * SW) + u * SW, SW)]).then_inc(ada_in[u], 16)
            sp.wait_ge(x_copied, NT + 1)
            sp.dma_start(g.xT_d.rearrange("k p t -> p k t"), xT[:]).then_inc(xT_out, 16)
            sp.wait_ge(xT_out, 16)

        @blk.tensor
        def _(pe):
            pe.wait_ge(const, 3)
            pe.wait_ge(rows_in, 16 * 9)
            nc.tensor.transpose(g.side[0][:, 0:V_END], vrow[:], g.ident[0:V_END, 0:V_END])
            nc.tensor.transpose(g.side[0][:, 128:200], crow[:], g.ident[0:72, 0:72])
            for k in range(KD):
                mm = nc.tensor.transpose(g.side[0][:, 256 + 16 * k:272 + 16 * k], srow[:, k * P:(k + 1) * P],
                                         g.ident[0:16, 0:16])
            mm.then_inc(rowsT, 1)

            def turn(u, n):
                out = g.acc[u][:, 0:2, :].rearrange("p a (b c) -> p (a b) c", b=4)
                for k in range(KD):
                    mm = nc.tensor.transpose(out[:, k, 0:n], xin[u][0:n, k * P:(k + 1) * P], g.ident[0:n, 0:n])
                mm.then_inc(x_turned, 1)

            with pe.Fori(0, NT // 2) as i:
                for u in range(2):
                    pe.wait_ge(x_in[u], i * 16 + 16)
                    pe.wait_ge(x_copied, i * 2)
                    turn(u, P)
            pe.wait_ge(x_in[0], 16 * (NT // 2 + 1))
            pe.wait_ge(x_copied, NT - 1)
            turn(0, TS)
            pe.wait_ge(x_copied, NT)
            norm.pe(pe)
            pe.wait_ge(cact_ready, 1)
            with pe.Fori(0, NSLAB // 2) as i:
                for u in range(2):
                    pe.wait_ge(ada_in[u], i * 16 + 16)
                    for j in range(JS):
                        col = i * (2 * JS * (NB + 1)) + (u * JS + j) * (NB + 1)
                        for k in range(KD):
                            mm = nc.tensor.matmul(g.side[1][:, bass.ds(col, NB + 1)], g.slab[u][:, k, j * P:(j + 1) * P],
                                                  cact[:, k, :], start=(k == 0), stop=(k == KD - 1))
                    mm.then_inc(ada_used[u], 1)

        @blk.scalar
        def _(act):
            act.wait_ge(rowsT, 1)
            nc.scalar.activation(csig[:], g.side[0][:, 128:200], ACT.Sigmoid).then_inc(csig_ready, 1)
            norm.act(act, lambda k: (x_copied, NT + 1))
            act.wait_ge(amp_ready, 2)
            norm.act_prompt(act)

        @blk.vector
        def _(dve):
            dve.wait_ge(csig_ready, 1)
            cps = g.side[0][:, 128:200].rearrange("p (b k) -> p k b", b=NB + 1)
            nc.vector.tensor_tensor(cact[:], cps, csig[:].rearrange("p (b k) -> p k b", b=NB + 1),
                                    ALU.mult).then_inc(cact_ready, 1)
            nc.vector.tensor_copy(g.vec[:], g.side[0][:, 0:V_END]).then_inc(vec_ready, 1)
            nc.vector.tensor_copy(g.stT[:], g.side[0][:, 256:384].rearrange("p (k c) -> p k c", k=KD)).then_inc(vec_ready, 1)

            def copy(u, at, n):
                src = g.acc[u][:, 0:2, :].rearrange("p a (b c) -> p (a b) c", b=4)
                nc.vector.tensor_copy(xT[:, :, at], src[:, :, 0:n]).then_inc(x_copied, 1)

            with dve.Fori(0, NT // 2) as i:
                for u in range(2):
                    dve.wait_ge(x_turned, i * 2 + u + 1)
                    copy(u, bass.ds(i * (2 * P) + u * P, P), P)
            dve.wait_ge(x_turned, NT + 1)
            copy(0, slice(TP, T), TS)
            dve.wait_ge(x_copied, NT + 1)
            norm.dve(dve)
            dve.wait_ge(vec_ready, 2)
            for u in range(2):
                dve.wait_ge(ada_used[u], NSLAB // 2)
            nc.vector.tensor_tensor(g.mod[:], g.side[1][:, 0:6 * KD * (NB + 1)].rearrange("p (j b) -> p j b", b=NB + 1),
                                    g.vec[:, V_ADA:V_N1].unsqueeze(2).to_broadcast([P, 6 * KD, NB + 1]),
                                    ALU.add).then_inc(mod_ready, 1)
            dve.wait_ge(mod_ready, 1)
            for w, (seg, v) in enumerate(((SC1, V_N1), (SC2, V_N2))):
                nc.vector.scalar_tensor_tensor(out=g.amp[:, w], in0=g.mod[:, seg * KD:(seg + 1) * KD, :], scalar=1.0,
                                               in1=g.vec[:, v:v + KD].unsqueeze(2).to_broadcast([P, KD, NB + 1]),
                                               op0=ALU.add, op1=ALU.mult).then_inc(amp_ready, 1)
            dve.wait_ge(amp_ready, 2)
            norm.dve_sample(dve)


def head_order():
    steps = [(kind, t) for t in range(NT) for kind in ("score", "first", "second")]
    steps += [("score", NT), ("sample", 0), ("sample", 1), ("sample", 2), ("sample", 3)]
    events, n = [], 0
    for b in range(6):
        for m in range(KD * len(PIECES)):
            events.append(("mm", b, m))
            if m % 4 == 3 and n < len(steps):
                events.append(("gla", n, steps[n]))
                n += 1
        events.append(("block", b, None))
    assert n == len(steps)
    return events, len(steps)


def stage2(g):
    nc, a, sem, o = g.nc, g.a, g.sem, g.o
    w_in = a["w_in"][0].rearrange("(k p) f -> p k f", p=P)
    events, NSTEP = head_order()
    PROD0 = 4
    NBL = 12
    with ExitStack() as st:
        sb = g.maker(st)
        wz = sb("wz", [P, KD, RANK])
        wgk = sb("wgk", [RANK, DK])
        zT = sb("zT", [RANK, T])
        qd = sb("qd", [P, T])
        kd = sb("kd", [P, T])
        eb = sb("eb", [P, T])
        t1 = sb("t1", [P, T + 18])
        t2 = sb("t2", [P, T + 18])
        oT = sb("oT", [P, 2, T])
        kendT = sb("kendT", [P, NT + 1, DK])
        km = sb("km", [TS, NB, DK])
        v = sb("v", [P, NT + 1, DV])
        S = sb("S", [P, 2, DV])
        s0 = sb("s0", [P, NB, DV])
        scm = sb("scm", [P, P])
        rmask = sb("rmask", [P, T])
        maskp = sb("maskp", [P, P])
        masks = sb("masks", [TS, TS])
        seqm = sb("seqm", [TS, NB])

        consts0 = sem("c2_0")
        consts = sem("c2")
        z_in = sem("z_in")
        zT_ready = sem("zT_ready")
        slab_in = [sem(f"slab_in{i}") for i in range(2)]
        wgk_in, s0_in = sem("wgk_in"), sem("s0_in")
        prod = sem("prod")
        free = [sem(f"free{i}") for i in range(2)]
        side_done = sem("side_done")
        side_free = sem("side_free")
        gate_lin = sem("gate_lin")
        scan_ready = sem("scan_ready")
        d_ready = sem("d_ready")
        exps = sem("exps")
        kd_ready = sem("kd_ready")
        sig_ready = sem("sig_ready")
        gla_mm = sem("gla_mm")
        gla_v = sem("gla_v")
        o_copied = sem("o_copied")
        km_ready = sem("km_ready")
        osq_ready = sem("osq_ready")
        oroot = sem("oroot")
        og_done = sem("og_done")
        s_reset = sem("s_reset")
        s_out = sem("s_out")
        dch, ach = sem("dch2"), sem("ach2")
        blk = st.enter_context(nc.Block())

        @blk.gpsimd
        def _(pool):
            pool.memset(rmask[:], 1.0).then_inc(consts0, 1)
            pool.memset(maskp[:], 1.0).then_inc(consts0, 1)
            pool.memset(masks[:], 1.0).then_inc(consts0, 1)
            pool.memset(seqm[:], 1.0).then_inc(consts0, 1)
            pool.wait_ge(consts0, 4)
            pool.memset(rmask[:, 0:TP:CH], 0.0).then_inc(consts, 1)
            pool.memset(rmask[:, TP:T:LS], 0.0).then_inc(consts, 1)
            for k, (m, w, n) in enumerate(((maskp, CH, P), (masks, LS, TS))):
                v3 = m[:].rearrange("p (b t) -> p b t", t=w)
                pool.affine_select(out=v3, in_=v3, compare_op=ALU.is_ge, fill=0.0, base=0,
                                   pattern=[[w, n // w], [1, w]], channel_multiplier=-1).then_inc(consts0, 1)
                pool.wait_ge(consts0, 5 + k)
                pool.affine_select(out=v3, in_=v3, compare_op=ALU.is_ge, fill=0.0, base=0,
                                   pattern=[[-w, n // w], [0, w]], channel_multiplier=1).then_inc(consts, 1)
            pool.affine_select(out=seqm[:], in_=seqm[:], compare_op=ALU.is_ge, fill=0.0, base=0,
                               pattern=[[-LS, NB]], channel_multiplier=1).then_inc(consts0, 1)
            pool.wait_ge(consts0, 7)
            pool.affine_select(out=seqm[:], in_=seqm[:], compare_op=ALU.is_ge, fill=0.0, base=LS - 1,
                               pattern=[[LS, NB]], channel_multiplier=-1).then_inc(consts, 1)
            with pool.Fori(0, HEADS) as h:
                pool.wait_ge(gla_v, h * NSTEP + NSTEP)
                pool.dma_start(o["gla_p"][0, 0, bass.ds(h, 1)].rearrange("h p v -> p (h v)"), S[:, 0, :]).then_inc(s_out, 16)
                pool.dma_start(o["gla_s"][0, :, bass.ds(h, 1)].rearrange("b h p v -> p (b h) v"), s0[:]).then_inc(s_out, 16)
            pool.wait_ge(s_out, 32 * HEADS)

        @blk.sync
        def _(sp):
            sp.dma_start(wz[:], w_in[:, :, C_Z:C_Z + RANK]).then_inc(z_in, 16)
            with sp.Fori(0, HEADS) as h:
                def slab(s, cols):
                    at = 0
                    for c, n in cols:
                        sp.dma_start(g.slab[s % 2][:, :, at:at + n], w_in[:, :, bass.ds(c, n)]).then_inc(slab_in[s % 2], 16)
                        at += n
                sp.wait_ge(prod, h * NBL)
                sp.dma_start(wgk[:], a["w_gk"][0][:, bass.ds(h * DK, DK)]).then_inc(wgk_in, 16)
                slab(0, [(h * DK + C_Q, DK), (h * DK + C_K, DK), (h * DV + C_G, P)])
                sp.wait_ge(prod, h * NBL + (PROD0 - 1))
                slab(1, [(h * DV + (C_G + P), P), (h * DV + C_V, P), (h * DV + (C_V + P), P)])
                sp.wait_ge(s_out, h * 32)
                sp.dma_start(s0[:], a["state_gla"][0, :, bass.ds(h, 1)].rearrange("b h p v -> p (b h) v")).then_inc(s0_in, 16)
                for j in range(2):
                    if j == 0:
                        sp.wait_ge(prod, h * NBL + (PROD0 + 4))
                    else:
                        sp.wait_ge(side_done, h * 8 + 5)
                    slab(2 + j, [(h * (2 * P) + (c + j * P), P) for c in (C_C, C_H, C_B)])

        @blk.tensor
        def _(pe):
            pe.wait_ge(z_in, 16)
            for k in range(KD):
                for i, (s, n) in enumerate(PIECES):
                    mm = nc.tensor.matmul(g.acc[0][0:RANK, i, 0:n], wz[:, k, :], g.hT[:, k, s:s + n],
                                          start=(k == 0), stop=(k == KD - 1))
            mm.then_inc(prod, PROD0)
            pe.wait_ge(zT_ready, 1)

            def product(slot, w, col, m):
                k, i = divmod(m, len(PIECES))
                s, n = PIECES[i]
                return nc.tensor.matmul(g.acc[slot][:, i, 0:n], w[:, k, col:col + P], g.hT[:, k, s:s + n],
                                        start=(k == 0), stop=(k == KD - 1))

            with pe.Fori(0, HEADS) as h:
                def claim(n):
                    pe.wait_ge(free[n % 2], h * (NBL // 2) + n // 2)

                claim(0)
                pe.wait_ge(wgk_in, h * 16 + 16)
                for i, (s, n) in enumerate(PIECES):
                    mm = nc.tensor.matmul(g.acc[0][:, i, 0:n], wgk[:], zT[:, s:s + n], start=True, stop=True)
                mm.then_inc(prod, 1)
                for n, (s, col) in enumerate(((0, 0), (0, P), (0, 2 * P), (1, 0)), 1):
                    pe.wait_ge(slab_in[s], h * 96 + 48)
                    claim(n)
                    for m in range(KD * 3):
                        mm = product(n % 2, g.slab[s], col, m)
                    mm.then_inc(prod, 1)
                for t in range(NT + 1):
                    s, n = tok(t)
                    if t % 2 == 0:
                        pe.wait_ge(side_free, h * 8 + max(0, t // 2 - 1))
                        if t < 4:
                            pe.wait_ge(o_copied, h * (NT + 1))
                            pe.wait_ge(gla_v, h * NSTEP)
                    for k in range(KD):
                        mm = nc.tensor.matmul(g.side[t // 2 % 2][0:n, (t % 2) * DV:(t % 2 + 1) * DV], g.hT[:, k, s:s + n],
                                              g.slab[1][:, k, P:3 * P], start=(k == 0), stop=(k == KD - 1))
                    if t % 2 == 1 or t == NT:
                        mm.then_inc(side_done, 1)
                pe.wait_ge(free[0], h * 6 + 2)
                for r in range(3):
                    if r < 2:
                        pe.wait_ge(side_free, h * 8 + (4, 6)[r])
                    for t in range(4 * r, min(4 * r + 4, NT + 1)):
                        s, n = tok(t)
                        mm = nc.tensor.transpose(g.side[(r + 1) % 2][0:n, (t % 4) * P:(t % 4 + 1) * P], oT[:, 1, s:s + n], g.ident[:])
                    mm.then_inc(side_done, 1)

                def gla_step(i, kind, t):
                    pe.wait_ge(gla_v, h * NSTEP + i)
                    upd, out = g.side[0], g.side[1]
                    s, n = tok(t)
                    if i == 0:
                        pe.wait_ge(side_free, h * 8 + 8)
                        pe.wait_ge(s_reset, h + 1)
                    if kind == "score":
                        mm = nc.tensor.matmul(upd[0:n, 0:n], kd[:, s:s + n], qd[:, s:s + n], start=True, stop=True)
                    elif kind == "first":
                        pe.wait_ge(o_copied, h * (NT + 1) + t)
                        for e in range(2):
                            nc.tensor.matmul(out[:, e * P:(e + 1) * P], v[:, t, e * P:(e + 1) * P], scm[:],
                                             start=(e == 0), stop=False, skip_group_check=True)
                            nc.tensor.matmul(out[:, e * P:e * P + CH], S[:, 0, e * P:(e + 1) * P], qd[:, s:s + CH],
                                             start=False, stop=False, skip_group_check=True)
                        mm = nc.tensor.matmul(upd[:, 0:DV], kendT[0:CH, t, :], v[0:CH, t, :], start=True, stop=True)
                    elif kind == "second":
                        for e in range(2):
                            nc.tensor.matmul(out[:, e * P + CH:(e + 1) * P], S[:, 1, e * P:(e + 1) * P], qd[:, s + CH:s + P],
                                             start=False, stop=(e == 1), skip_group_check=True)
                        mm = nc.tensor.matmul(upd[:, 0:DV], kendT[CH:P, t, :], v[CH:P, t, :], start=True, stop=True)
                    else:
                        if t == 0:
                            pe.wait_ge(o_copied, h * (NT + 1) + NT)
                            pe.wait_ge(s0_in, h * 16 + 16)
                            pe.wait_ge(km_ready, h + 1)
                            for e in range(2):
                                nc.tensor.matmul(out[:, e * P:e * P + TS], v[0:TS, NT, e * P:(e + 1) * P], scm[0:TS, 0:TS],
                                                 start=(e == 0), stop=False, skip_group_check=True)
                                for b in range(NB):
                                    c = e * P + b * LS
                                    nc.tensor.matmul(out[:, c:c + LS], s0[:, b, e * P:(e + 1) * P],
                                                     qd[:, TP + b * LS:TP + (b + 1) * LS], start=False,
                                                     stop=(e == 1 and b == NB - 1), skip_group_check=True)
                        for u in range(2):
                            mm = nc.tensor.matmul(upd[:, u * DV:(u + 1) * DV], km[:, 2 * t + u, :], v[0:TS, NT, :],
                                                  start=True, stop=True)
                    mm.then_inc(gla_mm, 1)

                for kind, x, y in events:
                    if kind == "gla":
                        gla_step(x, *y)
                    elif kind == "mm":
                        n = 5 + x
                        if y == 0:
                            claim(n)
                            pe.wait_ge(slab_in[x // 3], h * 96 + 96)
                        mm = product(n % 2, g.slab[x // 3], (x % 3) * P, y)
                        if y == KD * 3 - 1:
                            mm.then_inc(prod, 1)
                claim(11)
                for e in range(2):
                    pe.wait_ge(osq_ready, h * 2 + e + 1)
                    for i, (s, n) in enumerate(PIECES):
                        mm = nc.tensor.matmul(g.acc[1][:, i, 0:n], g.ones[:], (t1, t2)[e][:, s:s + n],
                                              start=(e == 0), stop=(e == 1))
                mm.then_inc(prod, 1)

        @blk.scalar
        def _(act):
            ch = Chain(act, ach)
            with act.Fori(0, HEADS) as h:
                ch.loop(h, 2)

                def product(n):
                    act.wait_ge(prod, h * NBL + (PROD0 + n + 1))

                product(0)
                act.wait_ge(og_done, h)
                for d, s in zip(flat2(t2[:, 0:T]), slot2(g.acc[0])):
                    x = nc.scalar.activation(d, s, ACT.Identity, bias=g.vec[:, bass.ds(h + V_BGK, 1)])
                x.then_inc(free[0], 1)
                act.wait_ge(free[0], h * (NBL // 2) + 1)
                ch.step(nc.scalar.activation(t1[:, 0:T], t2[:, 0:T], ACT.Abs))
                ch.step(nc.scalar.activation(t1[:, 0:T], t1[:, 0:T], ACT.Exp, scale=-1.0))
                nc.scalar.activation(t1[:, 0:T], t1[:, 0:T], ACT.Ln, bias=1.0).then_inc(gate_lin, 1)
                act.wait_ge(scan_ready, h + 1)
                nc.scalar.activation(eb[:], t1[:, 0:T], ACT.Exp, scale=1.0 / 16).then_inc(exps, 1)
                nc.scalar.activation(t2[:, 0:T], t1[:, 0:T], ACT.Exp, scale=-1.0 / 16).then_inc(exps, 1)
                act.wait_ge(d_ready, h + 1)
                nc.scalar.activation(oT[:, 0, :], oT[:, 0, :], ACT.Exp, scale=1.0 / 16).then_inc(exps, 1)
                for e, (slot, t) in enumerate(((1, t1), (0, t2))):
                    product(3 + e)
                    act.wait_ge(exps, h * 3 + 3) if e == 0 else act.wait_ge(kd_ready, h + 1)
                    for d, s in zip(flat2(t[:, 0:T]), slot2(g.acc[slot])):
                        x = nc.scalar.activation(d, s, ACT.Sigmoid)
                    x.then_inc(sig_ready, 1)
                for kind, x, y in events:
                    if kind == "block" and x % 3 == 0:
                        product(5 + x)
                        dst = g.ycT[:, bass.ds(h * 2 + x // 3, 1), :].rearrange("p k t -> p (k t)")
                        for d, s in zip(flat2(dst), slot2(g.acc[(5 + x) % 2])):
                            i = nc.scalar.activation(d, s, ACT.Copy)
                        i.then_inc(free[(5 + x) % 2], 1)
                    if kind == "gla" and (y[0] == "second" or y == ("sample", 0)):
                        t = y[1] if y[0] == "second" else NT
                        s, n = tok(t)
                        act.wait_ge(gla_mm, h * NSTEP + x + 1)
                        src = g.side[1][:, 0:2 * P].rearrange("p (e c) -> p e c", e=2)[:, :, 0:n]
                        nc.scalar.activation(oT[:, :, s:s + n], src, ACT.Copy).then_inc(o_copied, 1)
                act.wait_ge(free[0], h * 6 + 6)
                act.wait_ge(o_copied, h * (NT + 1) + NT + 1)
                for e in range(2):
                    nc.scalar.activation((t1, t2)[e][:, 0:T], oT[:, e, :], ACT.Square).then_inc(osq_ready, 1)
                product(11)
                for d, s in zip(flat2(t1[:, 0:T]), slot2(g.acc[1])):
                    x = nc.scalar.activation(d, s, ACT.Sqrt, scale=1.0 / DV, bias=g.eps[:])
                x.then_inc(free[1], 1)
                assert ch.n == ch.per

        @blk.vector
        def _(dve):
            V = nc.vector
            ch = Chain(dve, dch)
            dve.wait_ge(prod, PROD0)
            for d, s in zip(flat2(zT[:]), slot2(g.acc[0][0:RANK])):
                x = V.tensor_copy(d, s)
            x.then_inc(zT_ready, 1)
            dve.wait_ge(consts, 5)
            with dve.Fori(0, HEADS) as h:
                ch.loop(h, 12)

                def product(n):
                    dve.wait_ge(prod, h * NBL + (PROD0 + n + 1))

                dve.wait_ge(s_out, h * 32)
                V.memset(S[:, 0, :], 0.0).then_inc(s_reset, 1)
                dve.wait_ge(gate_lin, h + 1)
                ch.step(V.scalar_tensor_tensor(out=t2[:, 0:T], in0=t2[:, 0:T], scalar=0.0, in1=t1[:, 0:T],
                                               op0=ALU.min, op1=ALU.subtract))
                V.tensor_tensor_scan(t1[:, 0:T], rmask[:], t2[:, 0:T], 0.0, ALU.mult, ALU.add).then_inc(scan_ready, 1)
                dve.wait_ge(scan_ready, h + 1)
                for lo, hi, w in ((0, TP, CH), (TP, T, LS)):
                    bv = t1[:, lo:hi].rearrange("p (c t) -> p c t", t=w)
                    x = V.tensor_tensor(oT[:, 0, lo:hi].rearrange("p (c t) -> p c t", t=w),
                                        bv[:, :, w - 1:w].to_broadcast([P, (hi - lo) // w, w]), bv, ALU.subtract)
                x.then_inc(d_ready, 1)
                product(1)
                dve.wait_ge(exps, h * 3 + 1)
                for d, s, e in zip(flat2(qd[:]), slot2(g.acc[1]), flat2(eb[:])):
                    x = V.scalar_tensor_tensor(out=d, in0=s, scalar=DK ** -0.5, in1=e, op0=ALU.mult, op1=ALU.mult)
                x.then_inc(free[1], 1)
                product(2)
                dve.wait_ge(exps, h * 3 + 3)
                for d, s, e in zip(flat2(kd[:]), slot2(g.acc[0]), flat2(t2[:, 0:T])):
                    x = V.tensor_tensor(d, s, e, ALU.mult)
                x.then_inc(kd_ready, 1)
                for d, s, e in zip(flat2(oT[:, 1, :]), slot2(g.acc[0]), flat2(oT[:, 0, :])):
                    x = V.tensor_tensor(d, s, e, ALU.mult)
                x.then_inc(free[0], 1)
                for e, (slot, t) in enumerate(((1, t1), (0, t2))):
                    dve.wait_ge(sig_ready, h * 2 + e + 1)
                    dst = g.ogT[:, bass.ds(h * 2 + e, 1), :].rearrange("p k t -> p (k t)")
                    for d, s, q in zip(flat2(dst), slot2(g.acc[slot]), flat2(t[:, 0:T])):
                        x = V.tensor_tensor(d, s, q, ALU.mult)
                    x.then_inc(free[slot], 1)
                for r in range(5):
                    dve.wait_ge(side_done, h * 8 + r + 1)
                    src = g.side[r % 2][:].rearrange("p (u v) -> p u v", u=2)
                    if r < 4:
                        x = V.tensor_copy(v[:, 2 * r:2 * r + 2, :], src)
                    else:
                        x = V.tensor_copy(v[0:TS, NT, :], src[0:TS, 0, :])
                    x.then_inc(side_free, 1)
                for r in range(3):
                    dve.wait_ge(side_done, h * 8 + 6 + r)
                    src = g.side[(r + 1) % 2][:].rearrange("p (u v) -> p u v", u=4)
                    if r < 2:
                        x = V.tensor_copy(kendT[:, 4 * r:4 * r + 4, :], src)
                    else:
                        x = V.tensor_copy(kendT[0:TS, NT, :], src[0:TS, 0, :])
                    x.then_inc(side_free, 1)
                dve.wait_ge(side_free, h * 8 + 8)
                V.tensor_tensor(km[:], kendT[0:TS, NT:NT + 1, :].to_broadcast([TS, NB, DK]),
                                seqm[:].unsqueeze(2).to_broadcast([TS, NB, DK]), ALU.mult).then_inc(km_ready, 1)
                dve.wait_ge(free[0], h * 6 + 3)
                pads = t2[:, T + 2 - TS:T + 18].rearrange("p (b c) -> p b c", b=NB)

                def gla_step(i, kind, t):
                    dve.wait_ge(gla_mm, h * NSTEP + i + 1)
                    upd = g.side[0]
                    s, n = tok(t)
                    if kind == "score":
                        x = V.tensor_tensor(scm[0:n, 0:n], upd[0:n, 0:n], (maskp if t < NT else masks)[:], ALU.mult)
                    elif kind in ("first", "second"):
                        c = kind == "second"
                        end = s + (c + 1) * CH - 1
                        if i == 1:
                            dve.wait_ge(s_reset, h + 1)
                        else:
                            dve.wait_ge(gla_v, h * NSTEP + i)
                        x = V.scalar_tensor_tensor(out=S[:, 1 - c, :], in0=S[:, int(c), :], scalar=eb[:, end:end + 1],
                                                   in1=upd[:, 0:DV], op0=ALU.mult, op1=ALU.add)
                    else:
                        for u in range(2):
                            b = 2 * t + u
                            end = TP + (b + 1) * LS - 1
                            x = V.scalar_tensor_tensor(out=s0[:, b, :], in0=s0[:, b, :], scalar=eb[:, end:end + 1],
                                                       in1=upd[:, u * DV:(u + 1) * DV], op0=ALU.mult, op1=ALU.add)
                    x.then_inc(gla_v, 1)

                def conv_tap(j, w):
                    return g.vec[:, bass.ds(h * 2 + (V_CONV + w * KD + j), 1)]

                for kind, x, y in events:
                    if kind == "gla":
                        gla_step(x, *y)
                    if kind != "block":
                        continue
                    n, j = 5 + x, x // 3
                    slot = n % 2
                    if x % 3 == 0:
                        V.memset(t2[:, 0:2], 0.0)
                        ch.step(V.tensor_copy(pads[:, :, 0:2], g.stT[:, bass.ds(h * 2 + j, 1), :].rearrange("p k (b w) -> p (k b) w", w=2)))
                    elif x % 3 == 1:
                        product(n)
                        dve.wait_ge(free[(n - 1) % 2], h * 6 + (n - 1) // 2 + 1)
                        dst = g.ycT[:, bass.ds(h * 2 + j, 1), :].rearrange("p k t -> p (k t)")
                        for d, s, c in zip(padded3(t2), slot3(g.acc[slot]), flat3(dst)):
                            i = V.tensor_tensor(d, s, c, ALU.mult)
                        i.then_inc(free[slot], 1)
                        dve.wait_ge(free[slot], h * 6 + n // 2 + 1)
                        W = T + 16
                        V.tensor_copy(g.lastT[:, bass.ds(h * 2 + j, 1), 0:2].rearrange("p k c -> p (k c)"), t2[:, TP:TP + 2])
                        V.tensor_copy(g.lastT[:, bass.ds(h * 2 + j, 1), 2:18].rearrange("p k (b c) -> p (k b) c", b=NB), pads[:, :, LS:LS + 2])
                        ch.step(V.tensor_scalar(t1[:, 0:W], t2[:, 0:W], conv_tap(j, 0), None, ALU.mult))
                        ch.step(V.scalar_tensor_tensor(out=t1[:, 0:W], in0=t2[:, 1:W + 1], scalar=conv_tap(j, 1), in1=t1[:, 0:W],
                                                       op0=ALU.mult, op1=ALU.add))
                        ch.step(V.scalar_tensor_tensor(out=t1[:, 0:W], in0=t2[:, 2:W + 2], scalar=conv_tap(j, 2), in1=t1[:, 0:W],
                                                       op0=ALU.mult, op1=ALU.add))
                    else:
                        product(n)
                        dst = g.ycT[:, bass.ds(h * 2 + j, 1), :].rearrange("p k t -> p (k t)")
                        out3 = [t1[:, 0:768].rearrange("p (a b) -> p a b", a=2), t1[:, 768:TP],
                                t1[:, TP + 2:T + 18].rearrange("p (b t) -> p b t", b=NB)[:, :, 0:LS]]
                        for d, s, c in zip(flat3(dst), slot3(g.acc[slot]), out3):
                            i = V.tensor_tensor(d, s, c, ALU.mult)
                        i.then_inc(free[slot], 1)
                dve.wait_ge(free[1], h * 6 + 6)
                ch.step(V.reciprocal(t1[:, 0:T], t1[:, 0:T]))
                for e in range(2):
                    dst = g.ogT[:, bass.ds(h * 2 + e, 1), :].rearrange("p k t -> p (k t)")
                    ch.step(V.tensor_tensor(oT[:, e, :], oT[:, e, :], t1[:, 0:T], ALU.mult))
                    x = V.scalar_tensor_tensor(out=dst, in0=oT[:, e, :], scalar=g.vec[:, V_GNW + e:V_GNW + e + 1], in1=dst,
                                               op0=ALU.mult, op1=ALU.mult)
                x.then_inc(og_done, 1)
                assert ch.n == ch.per, (ch.n, ch.per)


def stage3(g):
    nc, a, sem, o = g.nc, g.a, g.sem, g.o
    w_in = a["w_in"][0].rearrange("(k p) f -> p k f", p=P)
    w_oc = a["w_out_conv"][0].rearrange("(k p) f -> p k f", p=P)
    w_og = a["w_out_gla"][0].rearrange("(k p) f -> p k f", p=P)
    w_o = a["w_o"][0].rearrange("(k p) f -> p k f", p=P)
    PER = 4
    PROD0, PROD1 = PER, PER + KD * PER
    with ExitStack() as st:
        sb = g.maker(st)
        merged = sb("merged", [P, KD, T])
        t1, t2 = sb("m1", [P, T]), sb("m2", [P, T])
        xb = [sb(f"xb{i}", [P, T]) for i in range(2)]
        xs = sb("xs", [P, 2, TS])
        lrow = sb("lrow", [18, D])
        slab_in = [sem(f"slab3_in{i}") for i in range(2)]
        prod = sem("prod3")
        free = [sem(f"free3_{i}") for i in range(2)]
        merged_done = sem("merged_done")
        y_scaled = sem("y_scaled")
        xb_in = [sem(f"xb_in{i}") for i in range(2)]
        x1_done = [sem(f"x1_done{i}") for i in range(2)]
        lout = sem("lout")
        norm = Norm(g, "n2", 1, g.hT, g.ogT, (t1, t2), xb[0])
        blk = st.enter_context(nc.Block())

        @blk.sync
        def _(sp):
            with sp.Fori(0, KD) as j:
                for u, (w, c) in enumerate(((w_oc, C_UA), (w_og, C_UB))):
                    sp.wait_ge(prod, j * PER + (PROD0 - 2 + 2 * u))
                    sp.dma_start(g.slab[u][:, :, 0:P], w_in[:, :, bass.ds(j * P + c, P)]).then_inc(slab_in[u], 16)
                    sp.dma_start(g.slab[u][:, :, P:2 * P], w[:, :, bass.ds(j * P, P)]).then_inc(slab_in[u], 16)
            with sp.Fori(0, 2) as i:
                for u in range(2):
                    sp.wait_ge(prod, i * PER + (PROD1 - 2 + 2 * u))
                    sp.dma_start(g.slab[u][:, :, 0:2 * P], w_o[:, :, bass.ds(i * (4 * P) + u * 2 * P, 2 * P)]).then_inc(slab_in[u], 16)
                    for r in range(2):
                        sp.wait_ge(x1_done[r], i * 2 + u)
                        sp.dma_start(xb[r][:], g.xT_d[bass.ds(i * 4 + (2 * u + r), 1)].rearrange("k p t -> p (k t)")).then_inc(xb_in[r], 16)

        @blk.gpsimd
        def _(pool):
            pool.wait_ge(free[0], 1)
            pool.dma_start(o["conv_p"].rearrange("l b w d -> (l b w) d"), lrow[0:2, :]).then_inc(lout, 16)
            pool.dma_start(o["conv_s"].rearrange("l b w d -> (l b w) d"), lrow[2:18, :]).then_inc(lout, 16)
            pool.wait_ge(lout, 32)

        @blk.tensor
        def _(pe):
            out = g.acc[0][0:18, 0:2, :].rearrange("p a (b c) -> p (a b) c", b=4)
            for k in range(KD):
                mm = nc.tensor.transpose(out[:, k, :], g.lastT[:, k, :], g.ident[:])
            mm.then_inc(prod, PROD0)

            def block(slot, w, col, src):
                for k in range(KD):
                    for i, (s, n) in enumerate(PIECES):
                        mm = nc.tensor.matmul(g.acc[slot][:, i, 0:n], w[:, k, col:col + P], src[:, k, s:s + n],
                                              start=(k == 0), stop=(k == KD - 1))
                mm.then_inc(prod, 1)

            with pe.Fori(0, KD) as j:
                for u, src in enumerate((g.ycT, g.ogT)):
                    pe.wait_ge(slab_in[u], j * 32 + 32)
                    pe.wait_ge(free[0], j * 2 + (u + 1))
                    block(0, g.slab[u], 0, g.hT)
                    pe.wait_ge(free[1], j * 2 + u)
                    block(1, g.slab[u], P, src)
            pe.wait_ge(merged_done, KD)
            with pe.Fori(0, 2) as i:
                for u in range(2):
                    pe.wait_ge(slab_in[u], i * 16 + (32 * KD + 16))
                    pe.wait_ge(free[0], i * 2 + (2 * KD + 1 + u))
                    block(0, g.slab[u], 0, merged)
                    pe.wait_ge(free[1], i * 2 + (2 * KD + u))
                    block(1, g.slab[u], P, merged)
            norm.pe(pe)

        @blk.scalar
        def _(act):
            with act.Fori(0, KD) as j:
                act.wait_ge(merged_done, j)
                for u, t in enumerate((t1, t2)):
                    act.wait_ge(prod, j * PER + (PROD0 + 2 * u + 1))
                    for d, s in zip(flat2(t[:]), slot2(g.acc[0])):
                        x = nc.scalar.activation(d, s, ACT.Sigmoid)
                    x.then_inc(free[0], 1)
            for r in range(2):
                act.wait_ge(x1_done[r], KD // 2)
            norm.act(act, lambda k: (x1_done[0], KD // 2))
            norm.act_prompt(act)

        @blk.vector
        def _(dve):
            V = nc.vector
            dve.wait_ge(prod, PROD0)
            V.tensor_copy(lrow[:], g.acc[0][0:18, 0:2, :].rearrange("p a c -> p (a c)")).then_inc(free[0], 1)
            with dve.Fori(0, KD) as j:
                for u, t in enumerate((t1, t2)):
                    dve.wait_ge(prod, j * PER + (PROD0 + 2 * u + 2))
                    dve.wait_ge(free[0], j * 2 + (u + 2))
                    for d, s in zip(flat2(t[:]), slot2(g.acc[1])):
                        x = V.tensor_tensor(d, s, d, ALU.mult)
                    x.then_inc(free[1], 1)
                dve.wait_ge(free[1], j * 2 + 2)
                V.tensor_tensor(merged[:, bass.ds(j, 1), :].rearrange("p k t -> p (k t)"), t1[:], t2[:], ALU.add).then_inc(merged_done, 1)
            with dve.Fori(0, 2) as i:
                for u in range(2):
                    for r in range(2):
                        dve.wait_ge(prod, i * PER + (PROD1 + 2 * u + r + 1))
                        dve.wait_ge(xb_in[r], i * 32 + 16 * (u + 1))
                        dve.wait_ge(x1_done[r], i * 2 + u)
                        j = i * 4 + (2 * u + r)
                        gate = g.mod[:, bass.ds(i * 4 + (G1 * KD + 2 * u + r), 1), :]
                        dst = g.hT[:, bass.ds(j, 1), :].rearrange("p k t -> p (k t)")
                        d3, s3, x3 = flat3(dst), slot3(g.acc[r]), flat3(xb[r][:])
                        V.tensor_tensor(xs[:, r, :].rearrange("p (b t) -> p b t", b=NB), s3[2],
                                        gate[:, :, 1:NB + 1].rearrange("p k b -> p (k b)").unsqueeze(2).to_broadcast([P, NB, LS]), ALU.mult)
                        for e in range(2):
                            x = V.scalar_tensor_tensor(out=d3[e], in0=s3[e], scalar=gate[:, :, 0:1].rearrange("p k b -> p (k b)"),
                                                       in1=x3[e], op0=ALU.mult, op1=ALU.add)
                        x.then_inc(free[r], 1)
                        dve.wait_ge(free[r], i * 2 + (2 * KD + 1 - r + u + 1))
                        V.tensor_tensor(d3[2], xs[:, r, :].rearrange("p (b t) -> p b t", b=NB), x3[2], ALU.add).then_inc(x1_done[r], 1)
            for r in range(2):
                dve.wait_ge(x1_done[r], KD // 2)
            norm.dve(dve)
            norm.dve_sample(dve)


def stage4(g):
    nc, a, sem = g.nc, g.a, g.sem
    x1T, h2T = g.hT, g.ogT
    with ExitStack() as st:
        sb = g.maker(st)
        wsd = sb("wsd", [P, 2, D])
        actT = sb("actT", [P, 2, T])
        t1 = sb("sh1", [P, T])
        gx = sb("gx", [P, KD, P + TS])
        g2 = sb("g2", [P, 2, D])
        bt = [sb(f"bt{i}", [P, D]) for i in range(2)]
        ht = [sb(f"ht{i}", [P, D]) for i in range(2)]
        rw = sb("rw", [P, KD, E])
        rb = sb("rb", [P, E])
        below = sb("below", [P, P])
        lower = sb("lower", [P, GROUPS, GROUPS])
        tokid = sb("tokid", [P, NT + 1])
        bnum = sb("bnum", [P, 2])
        zeros = sb("zeros", [P, NBLK])
        sc = sb("sc", [P, E])
        ch_ = sb("choice", [P, E])
        m8 = sb("m8", [P, GROUPS, 8])
        gs = sb("gs", [P, GROUPS])
        cmp = sb("cmp", [P, GROUPS, GROUPS])
        eq = sb("eq", [P, GROUPS, GROUPS])
        gr = sb("gr", [P, GROUPS])
        gmk = sb("gmk", [P, GROUPS])
        goff = sb("goff", [P, GROUPS])
        cm = sb("cm", [P, E])
        v8 = sb("v8", [P, 8])
        mr = sb("mr", [P, E])
        wsum = sb("wsum", [P, 1])
        wrec = sb("wrec", [P, 1])
        sel = sb("sel", [P, NT + 1, E])
        wn = sb("wn", [P, NT + 1, E])
        od = sb("od", [P, NT + 1, E])
        cnt_i = sb("cnt_i", [P, E], I32)
        nb_i = sb("nb_i", [P, E], I32)
        nb = sb("nb", [P, E])
        pend = sb("pend", [P, E])
        pst = sb("pst", [P, E])
        dest = sb("dest", [P, NT + 1, E])
        pick = sb("pick", [P, NT + 1, E])
        d8f = sb("d8f", [P, NT + 1, TOPK])
        be = sb("be", [P, 2])
        trow = [sb(f"trow{i}", [P, P]) for i in range(2)]

        c0, c1, c2 = sem("c4_0"), sem("c4_1"), sem("c4_2")
        w_in = sem("ws_in")
        gx_ready = sem("gx_ready")
        g2_mm, g2_done, g2_out = sem("g2_mm"), sem("g2_done"), sem("g2_out")
        sh_mm = sem("sh_mm")
        sh_sig, sh_v = sem("sh_sig"), sem("sh_v")
        x_mm, y_mm, h_mm, l_mm = sem("x_mm"), sem("y_mm"), sem("h_mm"), sem("l_mm")
        bt_mul, bt_add = sem("bt_mul"), sem("bt_add")
        ht_done = sem("ht_done")
        bt_out, ht_out = [sem(f"bt_out{i}") for i in range(2)], [sem(f"ht_out{i}") for i in range(2)]
        sc_ready, sc_used = sem("sc_ready"), sem("sc_used")
        sel_done = sem("sel_done")
        rank_mm = sem("rank_mm")
        dest_done = sem("dest_done")
        be_done, be_mm, row_done = sem("be_done"), sem("be_mm"), sem("row_done")
        tok_zero, tok_out, tok_in, tok_mm, idx_done = sem("tok_zero"), sem("tok_out"), sem("tok_in"), sem("tok_mm"), sem("idx_done")
        dch = sem("dch4")
        blk = st.enter_context(nc.Block())
        NTT = NT + 1

        @blk.sync
        def _(sp):
            sp.dma_start(g.slab[0][:, :, 0:FE], a["ws_gate"][0].rearrange("(k p) f -> p k f", p=P)).then_inc(w_in, 16)
            sp.dma_start(g.slab[1][:, :, 0:FE], a["ws_up"][0].rearrange("(k p) f -> p k f", p=P)).then_inc(w_in, 16)
            sp.dma_start(wsd[:], a["ws_down"][0].rearrange("(k p) f -> p k f", p=P)).then_inc(w_in, 16)
            sp.dma_start(rw[:], a["router_w"][0].rearrange("(k p) f -> p k f", p=P)).then_inc(w_in, 16)
            sp.dma_start(rb[:], a["router_bias"].to_broadcast([P, E])).then_inc(w_in, 16)
            sp.wait_ge(g2_done, 2)
            sp.dma_start(g.g2_d.rearrange("w p d -> p w d"), g2[:]).then_inc(g2_out, 16)
            for t in range(NTT):
                s, n = tok(t)
                sp.wait_ge(ht_done, 2 * t + 2)
                sp.dma_start(g.h2_d[s:s + n, :], ht[t % 2][0:n, :]).then_inc(ht_out[t % 2], 16)
                sp.wait_ge(bt_add, t + 1)
                sp.dma_start(g.base_d[s:s + n, :], bt[t % 2][0:n, :]).then_inc(bt_out[t % 2], 16)
            sp.wait_ge(tok_out, 16 * NTT * TOPK)
            table = g.tok_d.rearrange("(b s) o -> b (s o)", s=B_)
            sp.dma_start(trow[0][:], table[0:P, :]).then_inc(tok_in, 16)
            sp.dma_start(trow[1][0:NBLK - P, :], table[P:NBLK, :]).then_inc(tok_in, 16)
            sp.wait_ge(g2_out, 16)
            for i in range(2):
                sp.wait_ge(ht_out[i], 16 * (5 - i))
                sp.wait_ge(bt_out[i], 16 * (5 - i))

        @blk.gpsimd
        def _(pool):
            pool.memset(below[:], 1.0).then_inc(c0, 1)
            pool.memset(lower[:], 1.0).then_inc(c0, 1)
            pool.memset(zeros[:], 0.0).then_inc(c0, 1)
            pool.wait_ge(c0, 3)
            pool.affine_select(out=below[:], in_=below[:], compare_op=ALU.is_gt, fill=0.0, base=0,
                               pattern=[[1, P]], channel_multiplier=-1).then_inc(c1, 1)
            pool.affine_select(out=lower[:], in_=lower[:], compare_op=ALU.is_gt, fill=0.0, base=0,
                               pattern=[[1, GROUPS], [-1, GROUPS]], channel_multiplier=0).then_inc(c1, 1)
            pool.iota(tokid[:], pattern=[[P, NTT]], base=0, channel_multiplier=1, allow_small_or_imprecise_dtypes=True).then_inc(c1, 1)
            pool.iota(bnum[:], pattern=[[P, 2]], base=0, channel_multiplier=1, allow_small_or_imprecise_dtypes=True).then_inc(c1, 1)
            pool.dma_start(g.tok_d.rearrange("(p b) o -> p (b o)", p=P), zeros[:]).then_inc(tok_zero, 16)
            pool.wait_ge(tok_zero, 16)
            pool.wait_ge(c1, 4)
            pool.wait_ge(dest_done, 2)
            for t in range(NTT):
                n = tok(t)[1]
                for k in range(TOPK):
                    pool.indirect_dma_start(out=g.tok_d, out_offset=bass.IndirectOffsetOnAxis(ap=g.dest8[0:n, t, k:k + 1], axis=0),
                                            in_=tokid[0:n, t:t + 1], in_offset=None).then_inc(tok_out, 16)
            pool.wait_ge(tok_out, 16 * NTT * TOPK)

        @blk.tensor
        def _(pe):
            M = nc.tensor.matmul
            pe.wait_ge(gx_ready, 2)
            for w, (lo, n) in enumerate(((0, P), (P, TS))):
                out = g.acc[w][0:n, 0:2, :].rearrange("p a (b c) -> p (a b) c", b=4)
                for k in range(KD):
                    mm = nc.tensor.transpose(out[:, k, :], gx[:, k, lo:lo + n], g.ident[:])
                mm.then_inc(g2_mm, 1)
            pe.wait_ge(w_in, 16 * 5)
            pe.wait_ge(g2_done, 2)
            for e in range(2):
                for u in range(2):
                    if e == 1:
                        pe.wait_ge(sh_v, 1 + u)
                    for k in range(KD):
                        for i, (s, n) in enumerate(PIECES):
                            mm = M(g.acc[u][:, i, 0:n], g.slab[u][:, k, e * P:(e + 1) * P], h2T[:, k, s:s + n],
                                   start=(k == 0), stop=(k == KD - 1))
                    mm.then_inc(sh_mm, 1)
            pe.wait_ge(sh_v, 4)
            for t in range(NTT):
                s, n = tok(t)
                pe.wait_ge(bt_add, t)
                out = g.acc[0][0:n, 0:2, :].rearrange("p a (b c) -> p (a b) c", b=4)
                for k in range(KD):
                    mm = nc.tensor.transpose(out[:, k, :], x1T[:, k, s:s + n], g.ident[:])
                mm.then_inc(x_mm, 1)
                pe.wait_ge(bt_mul, t)
                for hf in range(2):
                    for f in range(2):
                        mm = M(g.acc[1][0:n, hf, :], actT[:, f, s:s + n], wsd[:, f, hf * 512:(hf + 1) * 512],
                               start=(f == 0), stop=(f == 1))
                mm.then_inc(y_mm, 1)
                for i in range(2):
                    if t > 0:
                        pe.wait_ge(ht_done, 2 * t - 1 + i)
                    for k in range(4):
                        mm = nc.tensor.transpose(g.side[i][0:n, k * P:(k + 1) * P], h2T[:, 4 * i + k, s:s + n], g.ident[:])
                    mm.then_inc(h_mm, 1)
                pe.wait_ge(sc_ready, t)
                for k in range(KD):
                    mm = M(g.acc[1][0:n, 2, 0:E], h2T[:, k, s:s + n], rw[:, k, :], start=(k == 0), stop=(k == KD - 1))
                mm.then_inc(l_mm, 1)
            pe.wait_ge(sel_done, NTT)
            pe.wait_ge(bt_add, NTT)
            pe.wait_ge(c1, 4)
            for t in range(NTT):
                out = g.acc[0][:, t // NT, (t % NT) * E:(t % NT + 1) * E]
                M(out, below[:], sel[:, t, :], start=True, stop=(t == 0))
                for q in range(t):
                    M(out, g.ones[:], sel[:, q, :], start=False, stop=(q == t - 1))
            for t in range(NTT):
                mm = M(g.acc[0][:, 2, 0:E], g.ones[:], sel[:, t, :], start=(t == 0), stop=(t == NTT - 1))
            mm.then_inc(rank_mm, 1)
            pe.wait_ge(be_done, 2)
            for c in range(2):
                mm = M(g.acc[1][0:1, 0, c * P:(c + 1) * P], be[:, c:c + 1], g.ident[:], start=True, stop=True)
            mm.then_inc(be_mm, 1)
            pe.wait_ge(tok_in, 32)
            nc.tensor.transpose(g.side[0][:, 0:P], trow[0][:], g.ident[:])
            nc.tensor.transpose(g.side[0][:, P:NBLK], trow[1][0:NBLK - P, :], g.ident[0:NBLK - P, 0:NBLK - P]).then_inc(tok_mm, 1)

        @blk.scalar
        def _(act):
            for e in range(2):
                act.wait_ge(sh_mm, 2 * e + 1)
                if e == 1:
                    act.wait_ge(sh_v, 2)
                for d, s in zip(flat2(t1[:]), slot2(g.acc[0])):
                    x = nc.scalar.activation(d, s, ACT.Sigmoid)
                x.then_inc(sh_sig, 1)
            for t in range(NTT):
                s, n = tok(t)
                for i in range(2):
                    act.wait_ge(h_mm, 2 * t + 1 + i)
                    if t >= 2 and i == 0:
                        act.wait_ge(ht_out[t % 2], 16 * (t // 2))
                    nc.scalar.activation(ht[t % 2][0:n, i * 512:(i + 1) * 512], g.side[i][0:n, :], ACT.Copy).then_inc(ht_done, 1)
                act.wait_ge(l_mm, t + 1)
                if t > 0:
                    act.wait_ge(sc_used, t)
                nc.scalar.activation(sc[0:n, :], g.acc[1][0:n, 2, 0:E], ACT.Sigmoid).then_inc(sc_ready, 1)

        @blk.vector
        def _(dve):
            V = nc.vector
            ch = Chain(dve, dch)
            V.tensor_copy(gx[:, :, 0:P], g.mod[:, G2 * KD:, 0:1].to_broadcast([P, KD, P])).then_inc(gx_ready, 1)
            V.tensor_copy(gx[:, :, P:].rearrange("p k (b t) -> p k b t", b=NB),
                          g.mod[:, G2 * KD:, 1:NB + 1].unsqueeze(3).to_broadcast([P, KD, NB, LS])).then_inc(gx_ready, 1)
            V.memset(sel[:, NT, :], 0.0)
            V.memset(wn[:, NT, :], 0.0)
            V.memset(g2[:, 1, :], 0.0)
            ch.step(V.memset(od[:, NT, :], 0.0))
            for w, n in enumerate((P, TS)):
                dve.wait_ge(g2_mm, w + 1)
                V.tensor_copy(g2[0:n, w, :], g.acc[w][0:n, 0:2, :].rearrange("p a c -> p (a c)")).then_inc(g2_done, 1)
            for e in range(2):
                dve.wait_ge(sh_sig, e + 1)
                for d, s in zip(flat2(t1[:]), slot2(g.acc[0])):
                    x = V.tensor_tensor(d, s, d, ALU.mult)
                x.then_inc(sh_v, 1)
                dve.wait_ge(sh_v, 2 * e + 1)
                dve.wait_ge(sh_mm, 2 * e + 2)
                for d, s, q in zip(flat2(actT[:, e, :]), slot2(g.acc[1]), flat2(t1[:])):
                    x = V.tensor_tensor(d, s, q, ALU.mult)
                x.then_inc(sh_v, 1)
            dve.wait_ge(g2_done, 2)
            dve.wait_ge(c1, 4)
            for t in range(NTT):
                s, n = tok(t)
                w = t // NT
                b = bt[t % 2][0:n, :]
                if t >= 2:
                    dve.wait_ge(bt_out[t % 2], 16 * (t // 2))
                dve.wait_ge(y_mm, t + 1)
                V.tensor_tensor(b, g.acc[1][0:n, 0:2, :].rearrange("p a c -> p (a c)"), g2[0:n, w, :], ALU.mult).then_inc(bt_mul, 1)
                dve.wait_ge(bt_mul, t + 1)
                dve.wait_ge(x_mm, t + 1)
                V.tensor_tensor(b, g.acc[0][0:n, 0:2, :].rearrange("p a c -> p (a c)"), b, ALU.add).then_inc(bt_add, 1)
                dve.wait_ge(sc_ready, t + 1)
                ch.step(V.tensor_tensor(ch_[0:n], sc[0:n], rb[0:n], ALU.add))
                for q in range(GROUPS):
                    x = V.max(m8[0:n, q, :], ch_[0:n, q * EG:(q + 1) * EG])
                ch.step(x)
                ch.step(V.tensor_tensor(gs[0:n], m8[0:n, :, 0], m8[0:n, :, 1], ALU.add))
                other = gs[0:n].unsqueeze(1).to_broadcast([n, GROUPS, GROUPS])
                own = gs[0:n].unsqueeze(2).to_broadcast([n, GROUPS, GROUPS])
                V.tensor_tensor(cmp[0:n], other, own, ALU.is_gt)
                ch.step(V.tensor_tensor(eq[0:n], other, own, ALU.is_equal))
                ch.step(V.tensor_tensor(eq[0:n], eq[0:n], lower[0:n], ALU.mult))
                ch.step(V.tensor_tensor(cmp[0:n], cmp[0:n], eq[0:n], ALU.add))
                ch.step(V.tensor_reduce(gr[0:n], cmp[0:n], AX, ALU.add))
                ch.step(V.tensor_scalar(gmk[0:n], gr[0:n], float(TOPG) - 0.5, None, ALU.is_lt))
                ch.step(V.tensor_scalar(goff[0:n], gmk[0:n], BIG, -BIG, ALU.mult, ALU.add))
                c3 = cm[0:n].rearrange("p (g e) -> p g e", g=GROUPS)
                ch.step(V.tensor_tensor(c3, ch_[0:n].rearrange("p (g e) -> p g e", g=GROUPS),
                                        gmk[0:n].unsqueeze(2).to_broadcast([n, GROUPS, EG]), ALU.mult))
                ch.step(V.tensor_tensor(c3, c3, goff[0:n].unsqueeze(2).to_broadcast([n, GROUPS, EG]), ALU.add))
                ch.step(V.max(v8[0:n], cm[0:n]))
                ch.step(V.match_replace(mr[0:n], v8[0:n], cm[0:n], 2 * BIG))
                ch.step(V.tensor_scalar(sel[0:n, t, :], mr[0:n], BIG, None, ALU.is_ge))
                V.tensor_tensor(wn[0:n, t, :], sc[0:n], sel[0:n, t, :], ALU.mult).then_inc(sc_used, 1)
                dve.wait_ge(sc_used, t + 1)
                ch.step(V.tensor_reduce(wsum[0:n], wn[0:n, t, :], AX, ALU.add))
                ch.step(V.reciprocal(wrec[0:n], wsum[0:n]))
                ch.step(V.tensor_scalar(wn[0:n, t, :], wn[0:n, t, :], wrec[0:n], SCALE_R, ALU.mult, ALU.mult))
                ch.step(V.tensor_tensor_scan(od[0:n, t, :], g.ones[0:n, 0:E], sel[0:n, t, :], 0.0, ALU.mult, ALU.add))
                V.tensor_tensor(od[0:n, t, :], od[0:n, t, :], sel[0:n, t, :], ALU.mult).then_inc(sel_done, 1)
            dve.wait_ge(rank_mm, 1)
            dve.wait_ge(sel_done, NTT)
            ch.step(V.tensor_scalar(cnt_i[:], g.acc[0][:, 2, 0:E], float(B_ - 1), None, ALU.add))
            ch.step(V.tensor_scalar(nb_i[:], cnt_i[:], 7, None, ALU.arith_shift_right))
            ch.step(V.tensor_copy(nb[:], nb_i[:]))
            ch.step(V.tensor_tensor_scan(pend[:], g.ones[:, 0:E], nb[:], 0.0, ALU.mult, ALU.add))
            ch.step(V.tensor_tensor(pst[:], pend[:], nb[:], ALU.subtract))
            ch.step(V.tensor_scalar(pst[:], pst[:], float(B_), None, ALU.mult))
            V.tensor_tensor(dest[:, 0:NT, :], g.acc[0][:, 0, :].rearrange("p (t e) -> p t e", t=NT),
                            pst[:].unsqueeze(1).to_broadcast([P, NT, E]), ALU.add)
            ch.step(V.tensor_tensor(dest[:, NT, :], g.acc[0][:, 1, 0:E], pst[:], ALU.add))
            for k in range(TOPK):
                for what, out in ((dest, d8f), (wn, g.w8)):
                    ch.step(V.scalar_tensor_tensor(out=pick[:], in0=od[:], scalar=float(k + 1), in1=what[:],
                                                   op0=ALU.is_equal, op1=ALU.mult))
                    ch.step(V.tensor_reduce(out[:, :, k], pick[:], AX, ALU.add))
            V.tensor_copy(g.dest8[:], d8f[:]).then_inc(dest_done, 2)
            for c in range(2):
                ch.step(V.tensor_scalar(cm[:], pend[:], bnum[:, c:c + 1], None, ALU.is_le))
                ch.step(V.tensor_reduce(be[:, c:c + 1], cm[:], AX, ALU.add))
                V.tensor_scalar(be[:, c:c + 1], be[:, c:c + 1], float(E - 1), None, ALU.min).then_inc(be_done, 1)
            dve.wait_ge(be_mm, 1)
            ch.step(V.tensor_copy(g.row[0:1, 0:2 * P], g.acc[1][0:1, 0, 0:2 * P]))
            V.tensor_copy(g.row[0:1, 2 * P - 1:2 * P], pend[0:1, E - 1:E]).then_inc(row_done, 1)
            dve.wait_ge(tok_mm, 1)
            V.tensor_copy(g.idx[:], g.side[0][:, 0:NBLK]).then_inc(idx_done, 1)


def stage5(g):
    nc, a, sem = g.nc, g.a, g.sem
    with ExitStack() as st:
        sb = g.maker(st)
        wgu = [sb(f"wgu{i}", [P, KD, 2 * FE]) for i in range(2)]
        wd = [sb(f"wd{i}", [P, 2, D]) for i in range(2)]
        xg = [sb(f"xg{i}", [P, D]) for i in range(2)]
        xe = [sb(f"xe{i}", [P, KD, B_]) for i in range(2)]
        sg = [sb(f"sg{i}", [P, FE]) for i in range(2)]
        hh = [sb(f"hh{i}", [P, FE]) for i in range(2)]
        hT = [sb(f"hTe{i}", [P, 2, B_]) for i in range(2)]
        ys = [sb(f"ys{i}", [P, D]) for i in range(2)]

        def pair(name):
            return [sem(f"{name}{i}") for i in range(2)]

        gu_in, wd_in = pair("gu_in"), pair("wd_in")
        x_in = pair("xg_in")
        x_mm, xe_ready = pair("xe_mm"), pair("xe_ready")
        gu_mm = pair("gu_mm")
        sg_ready, hm, h_ready = pair("sg_ready"), pair("hm"), pair("h_ready")
        h_mm, hT_ready = pair("h_mm"), pair("hT_ready")
        y_mm, ys_ready, y_out = pair("ye_mm"), pair("ys_ready"), pair("y_out")
        blk = st.enter_context(nc.Block())
        xps = g.acc[0][:, 0:2, :]
        gps = [g.side[0], g.side[1]]
        hps = g.acc[0][:, 2, :]
        yps = g.acc[1][:, 0:2, :]

        @blk.sync
        def _(sp):
            with sp.Fori(0, NBLK // 2) as i:
                for u in range(2):
                    e = sp.value_load(g.row[0:1, bass.ds(i * 2 + u, 1)], min_val=0, max_val=E - 1)
                    sp.wait_ge(gu_mm[u], i)
                    for w, name in enumerate(("we_gate", "we_up")):
                        sp.dma_start(wgu[u][:, :, w * FE:(w + 1) * FE],
                                     a[name][0][bass.ds(e, 1)].rearrange("e (k p) f -> p (e k) f", p=P)).then_inc(gu_in[u], 16)
                    sp.wait_ge(y_mm[u], i)
                    sp.dma_start(wd[u][:], a["we_down"][0][bass.ds(e, 1)].rearrange("e (k p) f -> p (e k) f", p=P)).then_inc(wd_in[u], 16)

        @blk.gpsimd
        def _(pool):
            for b in range(NBLK):
                u, c = b % 2, b // 2
                if c > 0:
                    pool.wait_ge(x_mm[u], c)
                pool.indirect_dma_start(out=xg[u][:], out_offset=None, in_=g.h2_d,
                                        in_offset=bass.IndirectOffsetOnAxis(ap=g.idx[:, b:b + 1], axis=0)).then_inc(x_in[u], 16)

        @blk.tensor
        def _(pe):
            M = nc.tensor.matmul

            def turn(u, c, cp):
                pe.wait_ge(x_in[u], c * 16 + 16)
                pe.wait_ge(xe_ready[1 - u], cp)
                out = xps.rearrange("p a (b c) -> p (a b) c", b=4)
                for k in range(KD):
                    mm = nc.tensor.transpose(out[:, k, :], xg[u][:, k * P:(k + 1) * P], g.ident[:])
                mm.then_inc(x_mm[u], 1)

            def down(u, c, cp):
                pe.wait_ge(h_ready[u], c + 1)
                pe.wait_ge(hT_ready[1 - u], cp)
                for f in range(2):
                    mm = nc.tensor.transpose(hps[:, f * P:(f + 1) * P], hh[u][:, f * P:(f + 1) * P], g.ident[:])
                mm.then_inc(h_mm[u], 1)
                pe.wait_ge(hT_ready[u], c + 1)
                pe.wait_ge(wd_in[u], c * 16 + 16)
                pe.wait_ge(ys_ready[1 - u], cp)
                for hf in range(2):
                    for f in range(2):
                        mm = M(yps[:, hf, :], hT[u][:, f, :], wd[u][:, f, hf * 512:(hf + 1) * 512], start=(f == 0), stop=(f == 1))
                mm.then_inc(y_mm[u], 1)

            def gate_up(u, c):
                pe.wait_ge(xe_ready[u], c + 1)
                pe.wait_ge(gu_in[u], c * 32 + 32)
                pe.wait_ge(h_ready[u], c)
                for k in range(KD):
                    mm = M(gps[u][:], xe[u][:, k, :], wgu[u][:, k, :], start=(k == 0), stop=(k == KD - 1))
                mm.then_inc(gu_mm[u], 1)

            turn(0, 0, 0)
            gate_up(0, 0)
            with pe.Fori(0, NBLK // 2 - 1) as i:
                turn(1, i, i + 1)
                down(0, i, i)
                gate_up(1, i)
                turn(0, i + 1, i + 1)
                down(1, i, i + 1)
                gate_up(0, i + 1)
            L = NBLK // 2 - 1
            turn(1, L, L + 1)
            down(0, L, L)
            gate_up(1, L)
            down(1, L, L + 1)

        @blk.scalar
        def _(act):
            def copy_x(u, c):
                act.wait_ge(x_mm[u], c + 1)
                act.wait_ge(gu_mm[u], c)
                nc.scalar.activation(xe[u][:].rearrange("p k s -> p (k s)").rearrange("p (a c) -> p a c", a=2), xps,
                                     ACT.Copy).then_inc(xe_ready[u], 1)

            def sigmoid(u, c):
                act.wait_ge(gu_mm[u], c + 1)
                act.wait_ge(h_ready[u], c)
                nc.scalar.activation(sg[u][:], gps[u][:, 0:FE], ACT.Sigmoid).then_inc(sg_ready[u], 1)

            def store(u, c, b):
                act.wait_ge(ys_ready[u], c + 1)
                act.dma_start(g.y_d[bass.ds(b * B_, B_), :] if not isinstance(b, int) else g.y_d[b * B_:(b + 1) * B_, :],
                              ys[u][:]).then_inc(y_out[u], 16)

            copy_x(0, 0)
            sigmoid(0, 0)
            with act.Fori(0, NBLK // 2 - 1) as i:
                copy_x(1, i)
                sigmoid(1, i)
                store(0, i, i * 2)
                copy_x(0, i + 1)
                sigmoid(0, i + 1)
                store(1, i, i * 2 + 1)
            L = NBLK // 2 - 1
            copy_x(1, L)
            sigmoid(1, L)
            store(0, L, 2 * L)
            store(1, L, 2 * L + 1)
            for u in range(2):
                act.wait_ge(y_out[u], 16 * (L + 1))

        @blk.vector
        def _(dve):
            V = nc.vector

            def finish(u, c):
                dve.wait_ge(h_mm[u], c + 1)
                dve.wait_ge(y_mm[u], c)
                V.tensor_copy(hT[u][:], hps[:, 0:2 * B_].rearrange("p (f s) -> p f s", f=2)).then_inc(hT_ready[u], 1)
                dve.wait_ge(y_mm[u], c + 1)
                dve.wait_ge(y_out[u], c * 16)
                V.tensor_copy(ys[u][:].rearrange("p (a c) -> p a c", a=2), yps).then_inc(ys_ready[u], 1)

            def swiglu(u, c):
                dve.wait_ge(sg_ready[u], c + 1)
                dve.wait_ge(h_mm[u], c)
                V.tensor_tensor(sg[u][:], gps[u][:, 0:FE], sg[u][:], ALU.mult).then_inc(hm[u], 1)
                dve.wait_ge(hm[u], c + 1)
                V.tensor_tensor(hh[u][:], gps[u][:, FE:2 * FE], sg[u][:], ALU.mult).then_inc(h_ready[u], 1)

            swiglu(0, 0)
            with dve.Fori(0, NBLK // 2 - 1) as i:
                finish(0, i)
                swiglu(1, i)
                finish(1, i)
                swiglu(0, i + 1)
            L = NBLK // 2 - 1
            finish(0, L)
            swiglu(1, L)
            finish(1, L)



def stage6(g):
    nc, a, sem, o = g.nc, g.a, g.sem, g.o
    NTT = NT + 1
    with ExitStack() as st:
        sb = g.maker(st)
        R = 6
        yg = [sb(f"yg{i}", [P, D]) for i in range(R)]
        base = [sb(f"base{i}", [P, D]) for i in range(2)]
        g2 = sb("g2b", [P, 2, D])
        fw = sb("fw", [P, D])
        acc = [sb(f"ysum{i}", [P, D]) for i in range(2)]
        sqs = sb("sqs", [P, D])
        ss = sb("ss", [P, NTT])
        rt = sb("rt", [P, NTT])
        rc = sb("rc", [P, NTT])
        yo = [sb(f"yo{i}", [P, D]) for i in range(2)]
        c_in = sem("c6_in")
        b_in = [sem(f"b6_in{i}") for i in range(2)]
        y_in = [sem(f"y6_in{i}") for i in range(R)]
        add = sem("add6")
        x2m, x2_ready = sem("x2m"), sem("x2_ready")
        sum_ready, root_ready, inv_ready = sem("sum6"), sem("root6"), sem("inv6")
        yo_ready = sem("yo_ready")
        out_done = [sem(f"out{i}") for i in range(2)]
        blk = st.enter_context(nc.Block())

        @blk.gpsimd
        def _(pool):
            n_ = 0
            for t in range(NTT):
                n = tok(t)[1]
                for k in range(TOPK):
                    if n_ >= R:
                        pool.wait_ge(add, n_ - R + 1)
                    pool.indirect_dma_start(out=yg[n_ % R][0:n, :], out_offset=None, in_=g.y_d,
                                            in_offset=bass.IndirectOffsetOnAxis(ap=g.dest8[0:n, t, k:k + 1], axis=0)
                                            ).then_inc(y_in[n_ % R], 16)
                    n_ += 1

        def store(sp, t):
            s, n = tok(t)
            sp.wait_ge(yo_ready, t + 1)
            dst = o["y_p"][0, s:s + n, :] if t < NT else o["y_s"].rearrange("b t d -> (b t) d")
            sp.dma_start(dst, yo[t % 2][0:n, :]).then_inc(out_done[t % 2], 16)

        @blk.sync
        def _(sp):
            sp.dma_start(fw[:], a["final_norm_w"].rearrange("(o d) -> o d", o=1).to_broadcast([P, D])).then_inc(c_in, 16)
            sp.dma_start(g2[:], g.g2_d.rearrange("w p d -> p w d")).then_inc(c_in, 16)
            for t in range(NTT):
                s, n = tok(t)
                if t >= 2:
                    sp.wait_ge(x2_ready, t - 1)
                sp.dma_start(base[t % 2][0:n, :], g.base_d[s:s + n, :]).then_inc(b_in[t % 2], 16)
                if t >= 1:
                    store(sp, t - 1)
            store(sp, NTT - 1)
            for i in range(2):
                sp.wait_ge(out_done[i], 16 * (5 - i))

        @blk.scalar
        def _(act):
            for t in range(NTT):
                n = tok(t)[1]
                act.wait_ge(x2_ready, t + 1)
                if t > 0:
                    act.wait_ge(root_ready, t)
                nc.scalar.activation(sqs[0:n, :], acc[t % 2][0:n, :], ACT.Square, accum_out=ss[0:n, t:t + 1]).then_inc(sum_ready, 1)
                act.wait_ge(sum_ready, t + 1)
                nc.scalar.activation(rt[0:n, t:t + 1], ss[0:n, t:t + 1], ACT.Sqrt, scale=1.0 / D, bias=g.eps[0:n]).then_inc(root_ready, 1)

        @blk.vector
        def _(dve):
            V = nc.vector
            n_ = 0

            def final(t):
                n = tok(t)[1]
                dve.wait_ge(root_ready, t + 1)
                V.reciprocal(rc[0:n, t:t + 1], rt[0:n, t:t + 1]).then_inc(inv_ready, 1)
                dve.wait_ge(inv_ready, t + 1)
                if t >= 2:
                    dve.wait_ge(out_done[t % 2], 16 * (t // 2))
                V.scalar_tensor_tensor(out=yo[t % 2][0:n, :], in0=acc[t % 2][0:n, :], scalar=rc[0:n, t:t + 1], in1=fw[0:n, :],
                                       op0=ALU.mult, op1=ALU.mult).then_inc(yo_ready, 1)

            dve.wait_ge(c_in, 32)
            for t in range(NTT):
                n = tok(t)[1]
                s = acc[t % 2][0:n, :]
                for k in range(TOPK):
                    dve.wait_ge(y_in[n_ % R], 16 * (n_ // R + 1))
                    row, w = yg[n_ % R][0:n, :], g.w8[0:n, t, k:k + 1]
                    if k == 0:
                        if t >= 2:
                            dve.wait_ge(yo_ready, t - 1)
                        x = V.tensor_scalar(s, row, w, None, ALU.mult)
                    else:
                        dve.wait_ge(add, n_)
                        x = V.scalar_tensor_tensor(out=s, in0=row, scalar=w, in1=s, op0=ALU.mult, op1=ALU.add)
                    x.then_inc(add, 1)
                    n_ += 1
                dve.wait_ge(add, n_)
                V.tensor_tensor(s, s, g2[0:n, t // NT, :], ALU.mult).then_inc(x2m, 1)
                dve.wait_ge(x2m, t + 1)
                dve.wait_ge(b_in[t % 2], 16 * (t // 2 + 1))
                V.tensor_tensor(s, s, base[t % 2][0:n, :], ALU.add).then_inc(x2_ready, 1)
                if t >= 1:
                    final(t - 1)
            final(NTT - 1)


_INS = ["x_prompt", "x_sample", "state_conv", "state_gla", "c_prompt", "c_sample", "w_ada", "b_ada", "norm1_w", "w_in",
        "conv_w", "w_gk", "b_gk", "gla_norm_w", "w_out_conv", "w_out_gla", "w_o", "norm2_w", "router_w", "router_bias",
        "we_gate", "we_up", "we_down", "ws_gate", "ws_up", "ws_down", "final_norm_w"]
_OUTS = [("y_p", (1, TP, D)), ("y_s", (NB, LS, D)), ("conv_p", (1, 1, CW - 1, D)), ("gla_p", (1, 1, HEADS, DK, DV)),
         ("conv_s", (1, NB, CW - 1, D)), ("gla_s", (1, NB, HEADS, DK, DV))]


def kernel(**inputs):
    import concourse.bacc as bacc
    from concourse.bass_utils import run_bass_kernel_spmd

    nc = bacc.Bacc("TRN2", target_bir_lowering=False, num_devices=1)
    arrays = {name: np.ascontiguousarray(inputs[name]) for name in _INS}
    ins = {name: nc.dram_tensor(name, x.shape, F32, kind="ExternalInput").ap() for name, x in arrays.items()}
    outs = {name: nc.dram_tensor(f"out_{name}", shape, F32, kind="ExternalOutput").ap() for name, shape in _OUTS}
    build(nc, ins, outs)
    r = run_bass_kernel_spmd(nc, [arrays], core_ids=[0])
    return tuple(r.results[0][f"out_{name}"] for name, _ in _OUTS)
```

```python
from contextlib import ExitStack

import numpy as np
import concourse.bass as bass
from concourse import mybir

ALU = mybir.AluOpType
ACT = mybir.ActivationFunctionType
F32 = mybir.dt.float32
F32R = mybir.dt.float32r
I32 = mybir.dt.int32
U32 = mybir.dt.uint32
AX = mybir.AxisListType.X

P = 128
D = 1024
KD = D // P
TP = 1024
NB, LS = 8, 8
TS = NB * LS
T = TP + TS
NT = TP // P
HEADS, DK, DV = 4, 128, 256
CH = 64
RANK = 16
E, GROUPS, TOPG, TOPK = 64, 8, 4, 8
EG = E // GROUPS
FE = 256
SCALE_R = 2.5
EPS = 1e-6
B_ = 128
NBLK = (T * TOPK + E * (B_ - 1) + B_ - 1) // B_
NSLOT = NBLK * B_
MINSLOT = -(-T * TOPK // (2 * B_)) * 2 * B_
PIECES = [(0, 384), (384, 384), (768, 320)]
C_B, C_C, C_H, C_Q, C_K, C_V, C_G, C_Z = 0, D, 2 * D, 3 * D, 3 * D + 512, 4 * D, 5 * D, 6 * D
C_UA, C_UB = 6 * D + RANK, 7 * D + RANK
SW = 384
V_ADA, V_N1, V_N2, V_CONV, V_BGK, V_GNW, V_END = 0, 48, 56, 64, 88, 92, 94
SH1, SC1, G1, SH2, SC2, G2 = range(6)
BIG = 1e30
CW = 3


def tok(t):
    return (t * P, P) if t < NT else (TP, TS)


class Tally:

    def __init__(self, sem):
        self.sem, self.base, self.n, self.outer = sem, 0, 0, None

    def mark(self, ins, by=1):
        ins.then_inc(self.sem, by)
        self.n += by

    def value(self):
        return self.base + self.n

    def loop(self, i, per):
        self.outer, self.per = self.base + self.n, per
        self.base, self.n = i * per + self.outer, 0

    def end(self, count):
        assert self.n == self.per, (self.n, self.per)
        self.base, self.n = self.outer + count * self.per, 0


class Chain(Tally):

    def __init__(self, eng, sem):
        super().__init__(sem)
        self.eng = eng

    def step(self, ins):
        self.mark(ins)
        self.eng.wait_ge(self.sem, self.value())


def flat2(ap):
    return [ap[:, 0:768].rearrange("p (a b) -> p a b", a=2), ap[:, 768:T]]


def slot2(ps):
    return [ps[:, 0:2, 0:384], ps[:, 2, 0:320]]


def slot3(ps):
    return [ps[:, 0:2, 0:384], ps[:, 2, 0:256], ps[:, 2, 256:320].rearrange("p (b t) -> p b t", b=NB)]


def flat3(ap):
    return [ap[:, 0:768].rearrange("p (a b) -> p a b", a=2), ap[:, 768:TP],
            ap[:, TP:T].rearrange("p (b t) -> p b t", b=NB)]


def padded3(ap):
    w = CW - 1
    return [ap[:, w:w + 768].rearrange("p (a b) -> p a b", a=2), ap[:, w + 768:w + TP],
            ap[:, w + TP:w + TP + NB * (LS + w)].rearrange("p (b t) -> p b t", b=NB)[:, :, w:w + LS]]


class Shared:
    pass


def build(nc, a, o):
    ctx = ExitStack()
    with ctx:
        early = []

        def sem(name):
            early.append(nc.alloc_semaphore(name))
            return early[-1]

        def maker(stack):
            return lambda name, shape, dt=F32: stack.enter_context(nc.sbuf_tensor(name, shape, dt))

        sb = maker(ctx)
        acc = [ctx.enter_context(nc.psum_tensor(f"acc{i}", [P, 3, 512], F32)) for i in range(2)]
        side = [ctx.enter_context(nc.psum_tensor(f"side{i}", [P, 512], F32)) for i in range(2)]

        xT_d = nc.dram_tensor("xT_d", [KD, P, T], F32, kind="Internal").ap()
        h2_d = nc.dram_tensor("h2_d", [T, D], F32, kind="Internal").ap()
        base_d = nc.dram_tensor("base_d", [T, D], F32, kind="Internal").ap()
        tok_d = nc.dram_tensor("tok_d", [NSLOT, 1], F32, kind="Internal").ap()
        g2_d = nc.dram_tensor("g2_d", [2, P, D], F32, kind="Internal").ap()
        y_d = nc.dram_tensor("y_d", [NSLOT, D], F32, kind="Internal").ap()

        ident = sb("ident", [P, P])
        ones = sb("ones", [P, P])
        eps = sb("eps", [P, 1])
        vec = sb("vec", [P, V_END])
        mod = sb("mod", [P, 6 * KD, NB + 1])
        amp = sb("amp", [P, 2, KD, NB + 1])

        g = Shared()
        g.dest8 = sb("dest8", [P, NT + 1, TOPK], U32)
        g.w8 = sb("w8", [P, NT + 1, TOPK])
        g.row = sb("row", [1, 6 * P + 1], I32)
        g.idx = sb("idx", [P, NBLK], U32)
        g.nc, g.a, g.o, g.sem, g.maker, g.acc, g.side = nc, a, o, sem, maker, acc, side
        g.xT_d, g.h2_d, g.base_d, g.tok_d, g.y_d, g.g2_d = xT_d, h2_d, base_d, tok_d, y_d, g2_d
        g.ident, g.ones, g.eps, g.vec, g.mod, g.amp = ident, ones, eps, vec, mod, amp

        with ExitStack() as mix:
            sm = maker(mix)
            g.hT = sm("hT", [P, KD, T])
            g.ogT = sm("ogT", [P, KD, T])
            g.stT = sm("stT", [P, KD, 16])
            g.lastT = sm("lastT", [P, KD, 18])
            g.slab = [sm(f"slab{i}", [P, KD, SW]) for i in range(2)]
            with ExitStack() as yc:
                g.ycT = maker(yc)("ycT", [P, KD, T])
                stage1(g)
                stage2(g)
                stage3(g)
            stage4(g)
        nc.clear_and_free_semaphores(early)
        nc.all_engine_barrier()
        stage5(g)
        stage6(g)


class Norm:

    def __init__(self, g, tag, which, src, dst, sq, rst):
        self.g, self.which, self.src, self.dst, self.sq, self.rst = g, which, src, dst, sq, rst
        self.sq_ready = g.sem(f"{tag}_sq_ready")
        self.sq_used = g.sem(f"{tag}_sq_used")
        self.root = g.sem(f"{tag}_root")
        self.inv = g.sem(f"{tag}_inv")
        self.scaled = g.sem(f"{tag}_scaled")
        self.sample1 = g.sem(f"{tag}_sample1")
        self.sample2 = g.sem(f"{tag}_sample2")
        self.prompt = g.sem(f"{tag}_prompt")
        self.shift = (SH1, SH2)[which] * KD

    def act(self, eng, src_ready):
        g = self.g
        for k in range(KD):
            eng.wait_ge(*src_ready(k))
            if k >= 2:
                eng.wait_ge(self.sq_used, k - 1)
            g.nc.scalar.activation(self.sq[k % 2][:, 0:T], self.src[:, k, :], ACT.Square).then_inc(self.sq_ready, 1)
        eng.wait_ge(self.sq_used, KD)
        for d, s in zip(flat2(self.rst[:, 0:T]), slot2(g.acc[1])):
            g.nc.scalar.activation(d, s, ACT.Sqrt, scale=1.0 / D, bias=g.eps[:]).then_inc(self.root, 1)

    def act_prompt(self, eng):
        g = self.g
        for k in range(KD):
            eng.wait_ge(self.scaled, k + 1)
            g.nc.scalar.activation(self.dst[:, k, 0:TP], self.dst[:, k, 0:TP], ACT.Identity,
                                   scale=g.amp[:, self.which, k, 0:1],
                                   bias=g.mod[:, self.shift + k, 0:1]).then_inc(self.prompt, 1)

    def pe(self, eng):
        g = self.g
        for k in range(KD):
            eng.wait_ge(self.sq_ready, k + 1)
            for i, (s, n) in enumerate(PIECES):
                mm = g.nc.tensor.matmul(g.acc[1][:, i, 0:n], g.ones[:], self.sq[k % 2][:, s:s + n],
                                        start=(k == 0), stop=(k == KD - 1))
            mm.then_inc(self.sq_used, 1)

    def dve(self, eng):
        g = self.g
        eng.wait_ge(self.root, 2)
        g.nc.vector.reciprocal(self.rst[:, 0:T], self.rst[:, 0:T]).then_inc(self.inv, 1)
        eng.wait_ge(self.inv, 1)
        for k in range(KD):
            g.nc.vector.tensor_tensor(self.dst[:, k, :], self.src[:, k, :], self.rst[:, 0:T],
                                      ALU.mult).then_inc(self.scaled, 1)

    def dve_sample(self, eng):
        g = self.g
        v = self.dst[:, :, TP:T].rearrange("p k (b t) -> p k b t", b=NB)
        eng.wait_ge(self.scaled, KD)
        sc = g.amp[:, self.which, :, 1:NB + 1].unsqueeze(3).to_broadcast([P, KD, NB, LS])
        sh = g.mod[:, self.shift:self.shift + KD, 1:NB + 1].unsqueeze(3).to_broadcast([P, KD, NB, LS])
        g.nc.vector.tensor_tensor(v, v, sc, ALU.mult).then_inc(self.sample1, 1)
        eng.wait_ge(self.sample1, 1)
        g.nc.vector.tensor_tensor(v, v, sh, ALU.add).then_inc(self.sample2, 1)

    def wait_done(self, eng):
        eng.wait_ge(self.prompt, KD)
        eng.wait_ge(self.sample2, 1)


def stage1(g):
    nc, a, sem = g.nc, g.a, g.sem
    NSLAB = 6 * D // SW
    with ExitStack() as st:
        sb = g.maker(st)
        vrow = sb("vrow", [V_END, P])
        crow = sb("crow", [(NB + 1) * KD, P])
        srow = sb("srow", [16, D])
        xin = [sb(f"xin{i}", [P, D]) for i in range(2)]
        xT = sb("xT", [P, KD, T])
        csig = sb("csig", [P, (NB + 1) * KD])
        cact = sb("cact", [P, KD, NB + 1])
        sq = [sb(f"sq1_{i}", [P, T]) for i in range(2)]
        rst = sb("rst1", [P, T])
        modrow = g.ycT[0:NB + 1].rearrange("p k t -> p (k t)")

        const0 = sem("const0")
        const = sem("const")
        rows_in = sem("rows_in")
        x_in = [sem(f"x_in{i}") for i in range(2)]
        ada_in = [sem(f"ada_in{i}") for i in range(2)]
        ada_mm = [sem(f"ada_mm{i}") for i in range(2)]
        ada_row = [sem(f"ada_row{i}") for i in range(2)]
        ada_turned = sem("ada_turned")
        rowsT = sem("rowsT")
        csig_ready = sem("csig_ready")
        vec_ready = sem("vec_ready")
        cact_ready = sem("cact_ready")
        x_turned = sem("x_turned")
        x_copied = sem("x_copied")
        mod_ready = sem("mod_ready")
        amp_ready = sem("amp_ready")
        xT_out = sem("xT_out")
        norm = Norm(g, "n1", 0, xT, g.hT, sq, rst)
        xp, xs = a["x_prompt"], a["x_sample"]
        blk = st.enter_context(nc.Block())

        @blk.gpsimd
        def _(pool):
            pool.memset(g.ident[:], 0.0).then_inc(const0, 1)
            pool.memset(g.ones[:], 1.0).then_inc(const, 1)
            pool.memset(g.eps[:], EPS).then_inc(const, 1)
            pool.wait_ge(const0, 1)
            pool.affine_select(out=g.ident[:], in_=g.ident[:], compare_op=ALU.not_equal, fill=1.0, base=0,
                               pattern=[[-1, P]], channel_multiplier=1).then_inc(const, 1)

        @blk.sync
        def _(sp):
            rows = [("b_ada", V_ADA, V_N1, a["b_ada"].rearrange("l (r c) -> (l r) c", c=P)),
                    ("n1", V_N1, V_N2, a["norm1_w"].rearrange("l (r c) -> (l r) c", c=P)),
                    ("n2", V_N2, V_CONV, a["norm2_w"].rearrange("l (r c) -> (l r) c", c=P)),
                    ("conv", V_CONV, V_BGK, a["conv_w"].rearrange("l w (r c) -> (l w r) c", c=P)),
                    ("bgk", V_BGK, V_GNW, a["b_gk"].rearrange("l (r c) -> (l r) c", c=P)),
                    ("gnw", V_GNW, V_END, a["gla_norm_w"].rearrange("l (r c) -> (l r) c", c=P))]
            for _, lo, hi, src in rows:
                sp.dma_start(vrow[lo:hi, :], src).then_inc(rows_in, 16)
            sp.dma_start(crow[0:KD, :], a["c_prompt"].rearrange("b (r c) -> (b r) c", c=P)).then_inc(rows_in, 16)
            sp.dma_start(crow[KD:, :], a["c_sample"].rearrange("b (r c) -> (b r) c", c=P)).then_inc(rows_in, 16)
            sp.dma_start(srow[:], a["state_conv"].rearrange("l b w d -> (l b w) d")).then_inc(rows_in, 16)
            with sp.Fori(0, NT // 2) as i:
                for u in range(2):
                    sp.wait_ge(x_turned, i * 2 + 1)
                    sp.dma_start(xin[u][:], xp[0, bass.ds(i * (2 * P) + u * P, P), :]).then_inc(x_in[u], 16)
            sp.wait_ge(x_turned, NT)
            sp.dma_start(xin[0][0:TS, :], xs.rearrange("b t d -> (b t) d")).then_inc(x_in[0], 16)
            w = a["w_ada"][0].rearrange("(k p) f -> p k f", p=P)
            with sp.Fori(0, NSLAB // 2) as i:
                for u in range(2):
                    sp.wait_ge(ada_mm[u], i + 1)
                    sp.dma_start(g.slab[u][:], w[:, :, bass.ds(i * (2 * SW) + u * SW, SW)]).then_inc(ada_in[u], 16)
            sp.wait_ge(x_copied, NT + 2)
            sp.dma_start(g.xT_d.rearrange("k p t -> p k t"), xT[:]).then_inc(xT_out, 16)
            sp.wait_ge(xT_out, 16)

        @blk.tensor
        def _(pe):
            pe.sem_inc(x_turned, 1)
            for u in range(2):
                pe.sem_inc(ada_mm[u], 1)
            pe.wait_ge(const, 3)
            pe.wait_ge(rows_in, 16 * 9)
            nc.tensor.transpose(g.side[0][:, 0:V_END], vrow[:], g.ident[0:V_END, 0:V_END])
            nc.tensor.transpose(g.side[0][:, 128:200], crow[:], g.ident[0:72, 0:72])
            for k in range(KD):
                mm = nc.tensor.transpose(g.side[0][:, 256 + 16 * k:272 + 16 * k], srow[:, k * P:(k + 1) * P],
                                         g.ident[0:16, 0:16])
            mm.then_inc(rowsT, 1)

            def turn(u, n):
                out = g.acc[u][:, 0:2, :].rearrange("p a (b c) -> p (a b) c", b=4)
                for k in range(KD):
                    mm = nc.tensor.transpose(out[:, k, 0:n], xin[u][0:n, k * P:(k + 1) * P], g.ident[0:n, 0:n])
                mm.then_inc(x_turned, 1)

            with pe.Fori(0, NT // 2) as i:
                for u in range(2):
                    pe.wait_ge(x_in[u], i * 16 + 16)
                    pe.wait_ge(x_copied, i * 2 + 1)
                    turn(u, P)
            pe.wait_ge(x_in[0], 16 * (NT // 2 + 1))
            pe.wait_ge(x_copied, NT)
            turn(0, TS)
            pe.wait_ge(x_copied, NT + 2)
            norm.pe(pe)
            pe.wait_ge(cact_ready, 1)
            with pe.Fori(0, NSLAB // 2) as i:
                for u in range(2):
                    pe.wait_ge(ada_in[u], i * 16 + 16)
                    pe.wait_ge(ada_row[u], i + 1)
                    for k in range(KD):
                        mm = nc.tensor.matmul(g.acc[0][0:NB + 1, u, 0:SW], cact[:, k, :], g.slab[u][:, k, :],
                                              start=(k == 0), stop=(k == KD - 1))
                    mm.then_inc(ada_mm[u], 1)
            for u in range(2):
                pe.wait_ge(ada_row[u], NSLAB // 2 + 1)
            for j in range(6 * KD):
                mm = nc.tensor.transpose(g.side[1][:, j * (NB + 1):(j + 1) * (NB + 1)], modrow[:, j * P:(j + 1) * P],
                                         g.ident[0:NB + 1, 0:NB + 1])
            mm.then_inc(ada_turned, 1)

        @blk.scalar
        def _(act):
            for u in range(2):
                act.sem_inc(ada_row[u], 1)
            act.wait_ge(rowsT, 1)
            nc.scalar.activation(csig[:], g.side[0][:, 128:200], ACT.Sigmoid).then_inc(csig_ready, 1)
            norm.act(act, lambda k: (x_copied, NT + 2))
            with act.Fori(0, NSLAB // 2) as i:
                for u in range(2):
                    act.wait_ge(ada_mm[u], i + 2)
                    nc.scalar.activation(modrow[:, bass.ds(i * (2 * SW) + u * SW, SW)], g.acc[0][0:NB + 1, u, 0:SW],
                                         ACT.Copy).then_inc(ada_row[u], 1)
            act.wait_ge(amp_ready, 2)
            norm.act_prompt(act)

        @blk.vector
        def _(dve):
            dve.sem_inc(x_copied, 1)
            dve.wait_ge(csig_ready, 1)
            cps = g.side[0][:, 128:200].rearrange("p (b k) -> p k b", b=NB + 1)
            nc.vector.tensor_tensor(cact[:], cps, csig[:].rearrange("p (b k) -> p k b", b=NB + 1),
                                    ALU.mult).then_inc(cact_ready, 1)
            nc.vector.tensor_copy(g.vec[:], g.side[0][:, 0:V_END]).then_inc(vec_ready, 1)
            nc.vector.tensor_copy(g.stT[:], g.side[0][:, 256:384].rearrange("p (k c) -> p k c", k=KD)).then_inc(vec_ready, 1)

            def copy(u, at, n):
                src = g.acc[u][:, 0:2, :].rearrange("p a (b c) -> p (a b) c", b=4)
                nc.vector.tensor_copy(xT[:, :, at], src[:, :, 0:n]).then_inc(x_copied, 1)

            with dve.Fori(0, NT // 2) as i:
                for u in range(2):
                    dve.wait_ge(x_turned, i * 2 + (u + 2))
                    copy(u, bass.ds(i * (2 * P) + u * P, P), P)
            dve.wait_ge(x_turned, NT + 2)
            copy(0, slice(TP, T), TS)
            dve.wait_ge(x_copied, NT + 2)
            norm.dve(dve)
            dve.wait_ge(vec_ready, 2)
            dve.wait_ge(ada_turned, 1)
            nc.vector.tensor_tensor(g.mod[:], g.side[1][:, 0:6 * KD * (NB + 1)].rearrange("p (j b) -> p j b", b=NB + 1),
                                    g.vec[:, V_ADA:V_N1].unsqueeze(2).to_broadcast([P, 6 * KD, NB + 1]),
                                    ALU.add).then_inc(mod_ready, 1)
            dve.wait_ge(mod_ready, 1)
            for w, (seg, v) in enumerate(((SC1, V_N1), (SC2, V_N2))):
                nc.vector.scalar_tensor_tensor(out=g.amp[:, w], in0=g.mod[:, seg * KD:(seg + 1) * KD, :], scalar=1.0,
                                               in1=g.vec[:, v:v + KD].unsqueeze(2).to_broadcast([P, KD, NB + 1]),
                                               op0=ALU.add, op1=ALU.mult).then_inc(amp_ready, 1)
            dve.wait_ge(amp_ready, 2)
            norm.dve_sample(dve)


def head_order():
    steps = [(kind, t) for t in range(NT) for kind in ("score", "first", "second")]
    steps += [("score", NT), ("sample", 0), ("sample", 1), ("sample", 2), ("sample", 3)]
    events, n = [], 0
    for b in range(6):
        for m in range(KD * len(PIECES)):
            events.append(("mm", b, m))
            if m % 4 == 3 and n < len(steps):
                events.append(("gla", n, steps[n]))
                n += 1
        events.append(("block", b, None))
    assert n == len(steps)
    return events, len(steps)


def stage2(g):
    nc, a, sem, o = g.nc, g.a, g.sem, g.o
    w_in = a["w_in"][0].rearrange("(k p) f -> p k f", p=P)
    events, NSTEP = head_order()
    PROD0 = 5
    NBL = 12
    with ExitStack() as st:
        sb = g.maker(st)
        wz = sb("wz", [P, KD, RANK])
        wgk = sb("wgk", [RANK, DK])
        zT = sb("zT", [RANK, T])
        qd = sb("qd", [P, T])
        kd = sb("kd", [P, T])
        eb = sb("eb", [P, T])
        t1 = sb("t1", [P, T + 18])
        t2 = sb("t2", [P, T + 18])
        oT = sb("oT", [P, 2, T])
        kendT = sb("kendT", [P, NT + 1, DK])
        km = sb("km", [TS, NB, DK])
        v = sb("v", [P, NT + 1, DV])
        S = sb("S", [P, 2, DV])
        s0 = sb("s0", [P, NB, DV])
        scm = sb("scm", [P, P])
        rmask = sb("rmask", [P, T])
        maskp = sb("maskp", [P, P])
        masks = sb("masks", [TS, TS])
        seqm = sb("seqm", [TS, NB])

        zero = sb("zero", [P, D // 2])
        zero_ready, y_zero = sem("zero_ready"), sem("y_zero")

        consts0 = sem("c2_0")
        consts = sem("c2")
        z_in = sem("z_in")
        zT_ready = sem("zT_ready")
        slab_in = [sem(f"slab_in{i}") for i in range(2)]
        wgk_in, s0_in = sem("wgk_in"), sem("s0_in")
        prod = sem("prod")
        free = [sem(f"free{i}") for i in range(2)]
        side_done = sem("side_done")
        side_free = sem("side_free")
        gate_lin = sem("gate_lin")
        scan_ready = sem("scan_ready")
        d_ready = sem("d_ready")
        exps = sem("exps")
        kd_ready = sem("kd_ready")
        sig_ready = sem("sig_ready")
        gla_mm = sem("gla_mm")
        gla_v = sem("gla_v")
        o_copied = sem("o_copied")
        km_ready = sem("km_ready")
        osq_ready = sem("osq_ready")
        oroot = sem("oroot")
        og_done = sem("og_done")
        s_reset = sem("s_reset")
        s_out = sem("s_out")
        s_kept = sem("s_kept")
        dch, ach = sem("dch2"), sem("ach2")
        blk = st.enter_context(nc.Block())

        @blk.gpsimd
        def _(pool):
            pool.sem_inc(s_kept, 1)
            pool.memset(rmask[:], 1.0).then_inc(consts0, 1)
            pool.memset(maskp[:], 1.0).then_inc(consts0, 1)
            pool.memset(masks[:], 1.0).then_inc(consts0, 1)
            pool.memset(seqm[:], 1.0).then_inc(consts0, 1)
            pool.wait_ge(consts0, 4)
            pool.memset(rmask[:, 0:TP:CH], 0.0).then_inc(consts, 1)
            pool.memset(rmask[:, TP:T:LS], 0.0).then_inc(consts, 1)
            for k, (m, w, n) in enumerate(((maskp, CH, P), (masks, LS, TS))):
                v3 = m[:].rearrange("p (b t) -> p b t", t=w)
                pool.affine_select(out=v3, in_=v3, compare_op=ALU.is_ge, fill=0.0, base=0,
                                   pattern=[[w, n // w], [1, w]], channel_multiplier=-1).then_inc(consts0, 1)
                pool.wait_ge(consts0, 5 + k)
                pool.affine_select(out=v3, in_=v3, compare_op=ALU.is_ge, fill=0.0, base=0,
                                   pattern=[[-w, n // w], [0, w]], channel_multiplier=1).then_inc(consts, 1)
            pool.affine_select(out=seqm[:], in_=seqm[:], compare_op=ALU.is_ge, fill=0.0, base=0,
                               pattern=[[-LS, NB]], channel_multiplier=1).then_inc(consts0, 1)
            pool.wait_ge(consts0, 7)
            pool.affine_select(out=seqm[:], in_=seqm[:], compare_op=ALU.is_ge, fill=0.0, base=LS - 1,
                               pattern=[[LS, NB]], channel_multiplier=-1).then_inc(consts, 1)
            pool.memset(zero[:], 0.0).then_inc(zero_ready, 1)
            pool.wait_ge(zero_ready, 1)
            with pool.Fori(0, HEADS) as h:
                share = (NSLOT - MINSLOT) // HEADS
                src = zero[:].unsqueeze(1).to_broadcast([P, share * 2 // P, D // 2])
                pool.dma_start(g.y_d[bass.ds(h * share + MINSLOT, share), :].rearrange("(p b) (c d) -> p (b c) d", p=P, c=2), src).then_inc(y_zero, 16)
                pool.wait_ge(gla_v, h * NSTEP + (NSTEP + 1))
                pool.dma_start(o["gla_p"][0, 0, bass.ds(h, 1)].rearrange("h p v -> p (h v)"), S[:, 0, :]).then_inc(s_out, 16)
                pool.dma_start(o["gla_s"][0, :, bass.ds(h, 1)].rearrange("b h p v -> p (b h) v"), s0[:]).then_inc(s_out, 16)
                pool.wait_ge(s_out, h * 32 + 32)
                pool.sem_inc(s_kept, 1)
            pool.wait_ge(y_zero, 16 * HEADS)

        @blk.sync
        def _(sp):
            sp.dma_start(wz[:], w_in[:, :, C_Z:C_Z + RANK]).then_inc(z_in, 16)
            with sp.Fori(0, HEADS) as h:
                def slab(s, cols):
                    at = 0
                    for c, n in cols:
                        sp.dma_start(g.slab[s % 2][:, :, at:at + n], w_in[:, :, bass.ds(c, n)]).then_inc(slab_in[s % 2], 16)
                        at += n
                sp.wait_ge(prod, h * NBL + (PROD0 - 4))
                sp.dma_start(wgk[:], a["w_gk"][0][:, bass.ds(h * DK, DK)]).then_inc(wgk_in, 16)
                slab(0, [(h * DK + C_Q, DK), (h * DK + C_K, DK), (h * DV + C_G, P)])
                sp.wait_ge(prod, h * NBL + (PROD0 - 1))
                slab(1, [(h * DV + (C_G + P), P), (h * DV + C_V, P), (h * DV + (C_V + P), P)])
                sp.wait_ge(s_kept, h + 1)
                sp.dma_start(s0[:], a["state_gla"][0, :, bass.ds(h, 1)].rearrange("b h p v -> p (b h) v")).then_inc(s0_in, 16)
                for j in range(2):
                    if j == 0:
                        sp.wait_ge(prod, h * NBL + (PROD0 + 4))
                    else:
                        sp.wait_ge(side_done, h * 8 + 5)
                    slab(2 + j, [(h * (2 * P) + (c + j * P), P) for c in (C_C, C_H, C_B)])

        @blk.tensor
        def _(pe):
            pe.sem_inc(prod, PROD0 - 1)
            pe.wait_ge(z_in, 16)
            for k in range(KD):
                for i, (s, n) in enumerate(PIECES):
                    mm = nc.tensor.matmul(g.acc[0][0:RANK, i, 0:n], wz[:, k, :], g.hT[:, k, s:s + n],
                                          start=(k == 0), stop=(k == KD - 1))
            mm.then_inc(prod, 1)
            pe.wait_ge(zT_ready, 1)

            def product(slot, w, col, m):
                k, i = divmod(m, len(PIECES))
                s, n = PIECES[i]
                return nc.tensor.matmul(g.acc[slot][:, i, 0:n], w[:, k, col:col + P], g.hT[:, k, s:s + n],
                                        start=(k == 0), stop=(k == KD - 1))

            with pe.Fori(0, HEADS) as h:
                def claim(n):
                    pe.wait_ge(free[n % 2], h * (NBL // 2) + (n // 2 + 1))

                claim(0)
                pe.wait_ge(wgk_in, h * 16 + 16)
                for i, (s, n) in enumerate(PIECES):
                    mm = nc.tensor.matmul(g.acc[0][:, i, 0:n], wgk[:], zT[:, s:s + n], start=True, stop=True)
                mm.then_inc(prod, 1)
                for n, (s, col) in enumerate(((0, 0), (0, P), (0, 2 * P), (1, 0)), 1):
                    pe.wait_ge(slab_in[s], h * 96 + 48)
                    claim(n)
                    for m in range(KD * 3):
                        mm = product(n % 2, g.slab[s], col, m)
                    mm.then_inc(prod, 1)
                for t in range(NT + 1):
                    s, n = tok(t)
                    if t % 2 == 0:
                        pe.wait_ge(side_free, h * 8 + max(1, t // 2))
                        if t < 4:
                            pe.wait_ge(o_copied, h * (NT + 1) + 1)
                            pe.wait_ge(gla_v, h * NSTEP + 1)
                    for k in range(KD):
                        mm = nc.tensor.matmul(g.side[t // 2 % 2][0:n, (t % 2) * DV:(t % 2 + 1) * DV], g.hT[:, k, s:s + n],
                                              g.slab[1][:, k, P:3 * P], start=(k == 0), stop=(k == KD - 1))
                    if t % 2 == 1 or t == NT:
                        mm.then_inc(side_done, 1)
                pe.wait_ge(free[0], h * 6 + 3)
                for r in range(3):
                    if r < 2:
                        pe.wait_ge(side_free, h * 8 + (5, 7)[r])
                    for t in range(4 * r, min(4 * r + 4, NT + 1)):
                        s, n = tok(t)
                        mm = nc.tensor.transpose(g.side[(r + 1) % 2][0:n, (t % 4) * P:(t % 4 + 1) * P], oT[:, 1, s:s + n], g.ident[:])
                    mm.then_inc(side_done, 1)

                def gla_step(i, kind, t):
                    pe.wait_ge(gla_v, h * NSTEP + (i + 1))
                    upd, out = g.side[0], g.side[1]
                    s, n = tok(t)
                    if i == 0:
                        pe.wait_ge(side_free, h * 8 + 9)
                        pe.wait_ge(s_reset, h + 1)
                    if kind == "score":
                        mm = nc.tensor.matmul(upd[0:n, 0:n], kd[:, s:s + n], qd[:, s:s + n], start=True, stop=True)
                    elif kind == "first":
                        pe.wait_ge(o_copied, h * (NT + 1) + (t + 1))
                        for e in range(2):
                            nc.tensor.matmul(out[:, e * P:(e + 1) * P], v[:, t, e * P:(e + 1) * P], scm[:],
                                             start=(e == 0), stop=False, skip_group_check=True)
                            nc.tensor.matmul(out[:, e * P:e * P + CH], S[:, 0, e * P:(e + 1) * P], qd[:, s:s + CH],
                                             start=False, stop=False, skip_group_check=True)
                        mm = nc.tensor.matmul(upd[:, 0:DV], kendT[0:CH, t, :], v[0:CH, t, :], start=True, stop=True)
                    elif kind == "second":
                        for e in range(2):
                            nc.tensor.matmul(out[:, e * P + CH:(e + 1) * P], S[:, 1, e * P:(e + 1) * P], qd[:, s + CH:s + P],
                                             start=False, stop=(e == 1), skip_group_check=True)
                        mm = nc.tensor.matmul(upd[:, 0:DV], kendT[CH:P, t, :], v[CH:P, t, :], start=True, stop=True)
                    else:
                        if t == 0:
                            pe.wait_ge(o_copied, h * (NT + 1) + (NT + 1))
                            pe.wait_ge(s0_in, h * 16 + 16)
                            pe.wait_ge(km_ready, h + 1)
                            for e in range(2):
                                nc.tensor.matmul(out[:, e * P:e * P + TS], v[0:TS, NT, e * P:(e + 1) * P], scm[0:TS, 0:TS],
                                                 start=(e == 0), stop=False, skip_group_check=True)
                                for b in range(NB):
                                    c = e * P + b * LS
                                    nc.tensor.matmul(out[:, c:c + LS], s0[:, b, e * P:(e + 1) * P],
                                                     qd[:, TP + b * LS:TP + (b + 1) * LS], start=False,
                                                     stop=(e == 1 and b == NB - 1), skip_group_check=True)
                        for u in range(2):
                            mm = nc.tensor.matmul(upd[:, u * DV:(u + 1) * DV], km[:, 2 * t + u, :], v[0:TS, NT, :],
                                                  start=True, stop=True)
                    mm.then_inc(gla_mm, 1)

                for kind, x, y in events:
                    if kind == "gla":
                        gla_step(x, *y)
                    elif kind == "mm":
                        n = 5 + x
                        if y == 0:
                            claim(n)
                            pe.wait_ge(slab_in[x // 3], h * 96 + 96)
                        mm = product(n % 2, g.slab[x // 3], (x % 3) * P, y)
                        if y == KD * 3 - 1:
                            mm.then_inc(prod, 1)
                claim(11)
                for e in range(2):
                    pe.wait_ge(osq_ready, h * 2 + e + 1)
                    for i, (s, n) in enumerate(PIECES):
                        mm = nc.tensor.matmul(g.acc[1][:, i, 0:n], g.ones[:], (t1, t2)[e][:, s:s + n],
                                              start=(e == 0), stop=(e == 1))
                mm.then_inc(prod, 1)

        @blk.scalar
        def _(act):
            ch = Chain(act, ach)
            act.sem_inc(o_copied, 1)
            with act.Fori(0, HEADS) as h:
                ch.loop(h, 2)

                def product(n):
                    act.wait_ge(prod, h * NBL + (PROD0 + n + 1))

                product(0)
                act.wait_ge(og_done, h + 1)
                for d, s in zip(flat2(t2[:, 0:T]), slot2(g.acc[0])):
                    x = nc.scalar.activation(d, s, ACT.Identity, bias=g.vec[:, bass.ds(h + V_BGK, 1)])
                x.then_inc(free[0], 1)
                act.wait_ge(free[0], h * (NBL // 2) + 2)
                ch.step(nc.scalar.activation(t1[:, 0:T], t2[:, 0:T], ACT.Abs))
                ch.step(nc.scalar.activation(t1[:, 0:T], t1[:, 0:T], ACT.Exp, scale=-1.0))
                nc.scalar.activation(t1[:, 0:T], t1[:, 0:T], ACT.Ln, bias=1.0).then_inc(gate_lin, 1)
                act.wait_ge(scan_ready, h + 1)
                nc.scalar.activation(eb[:], t1[:, 0:T], ACT.Exp, scale=1.0 / 16).then_inc(exps, 1)
                nc.scalar.activation(t2[:, 0:T], t1[:, 0:T], ACT.Exp, scale=-1.0 / 16).then_inc(exps, 1)
                act.wait_ge(d_ready, h + 1)
                nc.scalar.activation(oT[:, 0, :], oT[:, 0, :], ACT.Exp, scale=1.0 / 16).then_inc(exps, 1)
                for e, (slot, t) in enumerate(((1, t1), (0, t2))):
                    product(3 + e)
                    act.wait_ge(exps, h * 3 + 3) if e == 0 else act.wait_ge(kd_ready, h + 1)
                    for d, s in zip(flat2(t[:, 0:T]), slot2(g.acc[slot])):
                        x = nc.scalar.activation(d, s, ACT.Sigmoid)
                    x.then_inc(sig_ready, 1)
                for kind, x, y in events:
                    if kind == "block" and x % 3 == 0:
                        product(5 + x)
                        dst = g.ycT[:, bass.ds(h * 2 + x // 3, 1), :].rearrange("p k t -> p (k t)")
                        for d, s in zip(flat2(dst), slot2(g.acc[(5 + x) % 2])):
                            i = nc.scalar.activation(d, s, ACT.Copy)
                        i.then_inc(free[(5 + x) % 2], 1)
                    if kind == "gla" and (y[0] == "second" or y == ("sample", 0)):
                        t = y[1] if y[0] == "second" else NT
                        s, n = tok(t)
                        act.wait_ge(gla_mm, h * NSTEP + x + 1)
                        src = g.side[1][:, 0:2 * P].rearrange("p (e c) -> p e c", e=2)[:, :, 0:n]
                        nc.scalar.activation(oT[:, :, s:s + n], src, ACT.Copy).then_inc(o_copied, 1)
                act.wait_ge(free[0], h * 6 + 7)
                act.wait_ge(o_copied, h * (NT + 1) + (NT + 2))
                for e in range(2):
                    nc.scalar.activation((t1, t2)[e][:, 0:T], oT[:, e, :], ACT.Square).then_inc(osq_ready, 1)
                product(11)
                for d, s in zip(flat2(t1[:, 0:T]), slot2(g.acc[1])):
                    x = nc.scalar.activation(d, s, ACT.Sqrt, scale=1.0 / DV, bias=g.eps[:])
                x.then_inc(free[1], 1)
                assert ch.n == ch.per

        @blk.vector
        def _(dve):
            V = nc.vector
            ch = Chain(dve, dch)
            for s in (*free, side_free, gla_v, og_done):
                dve.sem_inc(s, 1)
            dve.wait_ge(prod, PROD0)
            for d, s in zip(flat2(zT[:]), slot2(g.acc[0][0:RANK])):
                x = V.tensor_copy(d, s)
            x.then_inc(zT_ready, 1)
            dve.wait_ge(consts, 5)
            with dve.Fori(0, HEADS) as h:
                ch.loop(h, 12)

                def product(n):
                    dve.wait_ge(prod, h * NBL + (PROD0 + n + 1))

                dve.wait_ge(s_kept, h + 1)
                V.memset(S[:, 0, :], 0.0).then_inc(s_reset, 1)
                dve.wait_ge(gate_lin, h + 1)
                ch.step(V.scalar_tensor_tensor(out=t2[:, 0:T], in0=t2[:, 0:T], scalar=0.0, in1=t1[:, 0:T],
                                               op0=ALU.min, op1=ALU.subtract))
                V.tensor_tensor_scan(t1[:, 0:T], rmask[:], t2[:, 0:T], 0.0, ALU.mult, ALU.add).then_inc(scan_ready, 1)
                dve.wait_ge(scan_ready, h + 1)
                for lo, hi, w in ((0, TP, CH), (TP, T, LS)):
                    bv = t1[:, lo:hi].rearrange("p (c t) -> p c t", t=w)
                    x = V.tensor_tensor(oT[:, 0, lo:hi].rearrange("p (c t) -> p c t", t=w),
                                        bv[:, :, w - 1:w].to_broadcast([P, (hi - lo) // w, w]), bv, ALU.subtract)
                x.then_inc(d_ready, 1)
                product(1)
                dve.wait_ge(exps, h * 3 + 1)
                for d, s, e in zip(flat2(qd[:]), slot2(g.acc[1]), flat2(eb[:])):
                    x = V.scalar_tensor_tensor(out=d, in0=s, scalar=DK ** -0.5, in1=e, op0=ALU.mult, op1=ALU.mult)
                x.then_inc(free[1], 1)
                product(2)
                dve.wait_ge(exps, h * 3 + 3)
                for d, s, e in zip(flat2(kd[:]), slot2(g.acc[0]), flat2(t2[:, 0:T])):
                    x = V.tensor_tensor(d, s, e, ALU.mult)
                x.then_inc(kd_ready, 1)
                for d, s, e in zip(flat2(oT[:, 1, :]), slot2(g.acc[0]), flat2(oT[:, 0, :])):
                    x = V.tensor_tensor(d, s, e, ALU.mult)
                x.then_inc(free[0], 1)
                for e, (slot, t) in enumerate(((1, t1), (0, t2))):
                    dve.wait_ge(sig_ready, h * 2 + e + 1)
                    dst = g.ogT[:, bass.ds(h * 2 + e, 1), :].rearrange("p k t -> p (k t)")
                    for d, s, q in zip(flat2(dst), slot2(g.acc[slot]), flat2(t[:, 0:T])):
                        x = V.tensor_tensor(d, s, q, ALU.mult)
                    x.then_inc(free[slot], 1)
                for r in range(5):
                    dve.wait_ge(side_done, h * 8 + r + 1)
                    src = g.side[r % 2][:].rearrange("p (u v) -> p u v", u=2)
                    if r < 4:
                        x = V.tensor_copy(v[:, 2 * r:2 * r + 2, :], src)
                    else:
                        x = V.tensor_copy(v[0:TS, NT, :], src[0:TS, 0, :])
                    x.then_inc(side_free, 1)
                for r in range(3):
                    dve.wait_ge(side_done, h * 8 + 6 + r)
                    src = g.side[(r + 1) % 2][:].rearrange("p (u v) -> p u v", u=4)
                    if r < 2:
                        x = V.tensor_copy(kendT[:, 4 * r:4 * r + 4, :], src)
                    else:
                        x = V.tensor_copy(kendT[0:TS, NT, :], src[0:TS, 0, :])
                    x.then_inc(side_free, 1)
                dve.wait_ge(side_free, h * 8 + 9)
                V.tensor_tensor(km[:], kendT[0:TS, NT:NT + 1, :].to_broadcast([TS, NB, DK]),
                                seqm[:].unsqueeze(2).to_broadcast([TS, NB, DK]), ALU.mult).then_inc(km_ready, 1)
                dve.wait_ge(free[0], h * 6 + 4)
                pads = t2[:, T + 2 - TS:T + 18].rearrange("p (b c) -> p b c", b=NB)

                def gla_step(i, kind, t):
                    dve.wait_ge(gla_mm, h * NSTEP + i + 1)
                    upd = g.side[0]
                    s, n = tok(t)
                    if kind == "score":
                        x = V.tensor_tensor(scm[0:n, 0:n], upd[0:n, 0:n], (maskp if t < NT else masks)[:], ALU.mult)
                    elif kind in ("first", "second"):
                        c = kind == "second"
                        end = s + (c + 1) * CH - 1
                        if i == 1:
                            dve.wait_ge(s_reset, h + 1)
                        else:
                            dve.wait_ge(gla_v, h * NSTEP + (i + 1))
                        x = V.scalar_tensor_tensor(out=S[:, 1 - c, :], in0=S[:, int(c), :], scalar=eb[:, end:end + 1],
                                                   in1=upd[:, 0:DV], op0=ALU.mult, op1=ALU.add)
                    else:
                        for u in range(2):
                            b = 2 * t + u
                            end = TP + (b + 1) * LS - 1
                            x = V.scalar_tensor_tensor(out=s0[:, b, :], in0=s0[:, b, :], scalar=eb[:, end:end + 1],
                                                       in1=upd[:, u * DV:(u + 1) * DV], op0=ALU.mult, op1=ALU.add)
                    x.then_inc(gla_v, 1)

                def conv_tap(j, w):
                    return g.vec[:, bass.ds(h * 2 + (V_CONV + w * KD + j), 1)]

                for kind, x, y in events:
                    if kind == "gla":
                        gla_step(x, *y)
                    if kind != "block":
                        continue
                    n, j = 5 + x, x // 3
                    slot = n % 2
                    if x % 3 == 0:
                        V.memset(t2[:, 0:2], 0.0)
                        ch.step(V.tensor_copy(pads[:, :, 0:2], g.stT[:, bass.ds(h * 2 + j, 1), :].rearrange("p k (b w) -> p (k b) w", w=2)))
                    elif x % 3 == 1:
                        product(n)
                        dve.wait_ge(free[(n - 1) % 2], h * 6 + ((n - 1) // 2 + 2))
                        dst = g.ycT[:, bass.ds(h * 2 + j, 1), :].rearrange("p k t -> p (k t)")
                        for d, s, c in zip(padded3(t2), slot3(g.acc[slot]), flat3(dst)):
                            i = V.tensor_tensor(d, s, c, ALU.mult)
                        i.then_inc(free[slot], 1)
                        dve.wait_ge(free[slot], h * 6 + (n // 2 + 2))
                        W = T + 16
                        V.tensor_copy(g.lastT[:, bass.ds(h * 2 + j, 1), 0:2].rearrange("p k c -> p (k c)"), t2[:, TP:TP + 2])
                        V.tensor_copy(g.lastT[:, bass.ds(h * 2 + j, 1), 2:18].rearrange("p k (b c) -> p (k b) c", b=NB), pads[:, :, LS:LS + 2])
                        ch.step(V.tensor_scalar(t1[:, 0:W], t2[:, 0:W], conv_tap(j, 0), None, ALU.mult))
                        ch.step(V.scalar_tensor_tensor(out=t1[:, 0:W], in0=t2[:, 1:W + 1], scalar=conv_tap(j, 1), in1=t1[:, 0:W],
                                                       op0=ALU.mult, op1=ALU.add))
                        ch.step(V.scalar_tensor_tensor(out=t1[:, 0:W], in0=t2[:, 2:W + 2], scalar=conv_tap(j, 2), in1=t1[:, 0:W],
                                                       op0=ALU.mult, op1=ALU.add))
                    else:
                        product(n)
                        dst = g.ycT[:, bass.ds(h * 2 + j, 1), :].rearrange("p k t -> p (k t)")
                        out3 = [t1[:, 0:768].rearrange("p (a b) -> p a b", a=2), t1[:, 768:TP],
                                t1[:, TP + 2:T + 18].rearrange("p (b t) -> p b t", b=NB)[:, :, 0:LS]]
                        for d, s, c in zip(flat3(dst), slot3(g.acc[slot]), out3):
                            i = V.tensor_tensor(d, s, c, ALU.mult)
                        i.then_inc(free[slot], 1)
                dve.wait_ge(free[1], h * 6 + 7)
                ch.step(V.reciprocal(t1[:, 0:T], t1[:, 0:T]))
                for e in range(2):
                    dst = g.ogT[:, bass.ds(h * 2 + e, 1), :].rearrange("p k t -> p (k t)")
                    ch.step(V.tensor_tensor(oT[:, e, :], oT[:, e, :], t1[:, 0:T], ALU.mult))
                    x = V.scalar_tensor_tensor(out=dst, in0=oT[:, e, :], scalar=g.vec[:, V_GNW + e:V_GNW + e + 1], in1=dst,
                                               op0=ALU.mult, op1=ALU.mult)
                x.then_inc(og_done, 1)
                assert ch.n == ch.per, (ch.n, ch.per)


def stage3(g):
    nc, a, sem, o = g.nc, g.a, g.sem, g.o
    w_in = a["w_in"][0].rearrange("(k p) f -> p k f", p=P)
    w_oc = a["w_out_conv"][0].rearrange("(k p) f -> p k f", p=P)
    w_og = a["w_out_gla"][0].rearrange("(k p) f -> p k f", p=P)
    w_o = a["w_o"][0].rearrange("(k p) f -> p k f", p=P)
    PER = 4
    PROD0, PROD1 = PER, PER + KD * PER
    with ExitStack() as st:
        sb = g.maker(st)
        merged = sb("merged", [P, KD, T])
        t1, t2 = sb("m1", [P, T]), sb("m2", [P, T])
        xb = [sb(f"xb{i}", [P, T]) for i in range(2)]
        xs = sb("xs", [P, 2, TS])
        lrow = sb("lrow", [18, D])
        slab_in = [sem(f"slab3_in{i}") for i in range(2)]
        prod = sem("prod3")
        free = [sem(f"free3_{i}") for i in range(2)]
        merged_done = sem("merged_done")
        y_scaled = sem("y_scaled")
        xb_in = [sem(f"xb_in{i}") for i in range(2)]
        x1_done = [sem(f"x1_done{i}") for i in range(2)]
        lout = sem("lout")
        norm = Norm(g, "n2", 1, g.hT, g.ogT, (t1, t2), xb[0])
        blk = st.enter_context(nc.Block())

        @blk.sync
        def _(sp):
            with sp.Fori(0, KD) as j:
                for u, (w, c) in enumerate(((w_oc, C_UA), (w_og, C_UB))):
                    sp.wait_ge(prod, j * PER + (PROD0 - 2 + 2 * u))
                    sp.dma_start(g.slab[u][:, :, 0:P], w_in[:, :, bass.ds(j * P + c, P)]).then_inc(slab_in[u], 16)
                    sp.dma_start(g.slab[u][:, :, P:2 * P], w[:, :, bass.ds(j * P, P)]).then_inc(slab_in[u], 16)
            with sp.Fori(0, 2) as i:
                for u in range(2):
                    sp.wait_ge(prod, i * PER + (PROD1 - 2 + 2 * u))
                    sp.dma_start(g.slab[u][:, :, 0:2 * P], w_o[:, :, bass.ds(i * (4 * P) + u * 2 * P, 2 * P)]).then_inc(slab_in[u], 16)
                    for r in range(2):
                        sp.wait_ge(x1_done[r], i * 2 + (u + 1))
                        sp.dma_start(xb[r][:], g.xT_d[bass.ds(i * 4 + (2 * u + r), 1)].rearrange("k p t -> p (k t)")).then_inc(xb_in[r], 16)

        @blk.gpsimd
        def _(pool):
            pool.wait_ge(free[0], 2)
            pool.dma_start(o["conv_p"].rearrange("l b w d -> (l b w) d"), lrow[0:2, :]).then_inc(lout, 16)
            pool.dma_start(o["conv_s"].rearrange("l b w d -> (l b w) d"), lrow[2:18, :]).then_inc(lout, 16)
            pool.wait_ge(lout, 32)

        @blk.tensor
        def _(pe):
            out = g.acc[0][0:18, 0:2, :].rearrange("p a (b c) -> p (a b) c", b=4)
            for k in range(KD):
                mm = nc.tensor.transpose(out[:, k, :], g.lastT[:, k, :], g.ident[:])
            mm.then_inc(prod, PROD0)

            def block(slot, w, col, src):
                for k in range(KD):
                    for i, (s, n) in enumerate(PIECES):
                        mm = nc.tensor.matmul(g.acc[slot][:, i, 0:n], w[:, k, col:col + P], src[:, k, s:s + n],
                                              start=(k == 0), stop=(k == KD - 1))
                mm.then_inc(prod, 1)

            with pe.Fori(0, KD) as j:
                for u, src in enumerate((g.ycT, g.ogT)):
                    pe.wait_ge(slab_in[u], j * 32 + 32)
                    pe.wait_ge(free[0], j * 2 + (u + 2))
                    block(0, g.slab[u], 0, g.hT)
                    pe.wait_ge(free[1], j * 2 + (u + 1))
                    block(1, g.slab[u], P, src)
            pe.wait_ge(merged_done, KD + 1)
            with pe.Fori(0, 2) as i:
                for u in range(2):
                    pe.wait_ge(slab_in[u], i * 16 + (32 * KD + 16))
                    pe.wait_ge(free[0], i * 2 + (2 * KD + 2 + u))
                    block(0, g.slab[u], 0, merged)
                    pe.wait_ge(free[1], i * 2 + (2 * KD + 1 + u))
                    block(1, g.slab[u], P, merged)
            norm.pe(pe)

        @blk.scalar
        def _(act):
            with act.Fori(0, KD) as j:
                act.wait_ge(merged_done, j + 1)
                for u, t in enumerate((t1, t2)):
                    act.wait_ge(prod, j * PER + (PROD0 + 2 * u + 1))
                    for d, s in zip(flat2(t[:]), slot2(g.acc[0])):
                        x = nc.scalar.activation(d, s, ACT.Sigmoid)
                    x.then_inc(free[0], 1)
            for r in range(2):
                act.wait_ge(x1_done[r], KD // 2 + 1)
            norm.act(act, lambda k: (x1_done[0], KD // 2 + 1))
            norm.act_prompt(act)

        @blk.vector
        def _(dve):
            V = nc.vector
            for s in (merged_done, *free, *x1_done):
                dve.sem_inc(s, 1)
            dve.wait_ge(prod, PROD0)
            V.tensor_copy(lrow[:], g.acc[0][0:18, 0:2, :].rearrange("p a c -> p (a c)")).then_inc(free[0], 1)
            with dve.Fori(0, KD) as j:
                for u, t in enumerate((t1, t2)):
                    dve.wait_ge(prod, j * PER + (PROD0 + 2 * u + 2))
                    dve.wait_ge(free[0], j * 2 + (u + 3))
                    for d, s in zip(flat2(t[:]), slot2(g.acc[1])):
                        x = V.tensor_tensor(d, s, d, ALU.mult)
                    x.then_inc(free[1], 1)
                dve.wait_ge(free[1], j * 2 + 3)
                V.tensor_tensor(merged[:, bass.ds(j, 1), :].rearrange("p k t -> p (k t)"), t1[:], t2[:], ALU.add).then_inc(merged_done, 1)
            with dve.Fori(0, 2) as i:
                for u in range(2):
                    for r in range(2):
                        dve.wait_ge(prod, i * PER + (PROD1 + 2 * u + r + 1))
                        dve.wait_ge(xb_in[r], i * 32 + 16 * (u + 1))
                        dve.wait_ge(x1_done[r], i * 2 + (u + 1))
                        j = i * 4 + (2 * u + r)
                        gate = g.mod[:, bass.ds(i * 4 + (G1 * KD + 2 * u + r), 1), :]
                        dst = g.hT[:, bass.ds(j, 1), :].rearrange("p k t -> p (k t)")
                        d3, s3, x3 = flat3(dst), slot3(g.acc[r]), flat3(xb[r][:])
                        V.tensor_tensor(xs[:, r, :].rearrange("p (b t) -> p b t", b=NB), s3[2],
                                        gate[:, :, 1:NB + 1].rearrange("p k b -> p (k b)").unsqueeze(2).to_broadcast([P, NB, LS]), ALU.mult)
                        for e in range(2):
                            x = V.scalar_tensor_tensor(out=d3[e], in0=s3[e], scalar=gate[:, :, 0:1].rearrange("p k b -> p (k b)"),
                                                       in1=x3[e], op0=ALU.mult, op1=ALU.add)
                        x.then_inc(free[r], 1)
                        dve.wait_ge(free[r], i * 2 + (2 * KD + 1 - r + u + 2))
                        V.tensor_tensor(d3[2], xs[:, r, :].rearrange("p (b t) -> p b t", b=NB), x3[2], ALU.add).then_inc(x1_done[r], 1)
            for r in range(2):
                dve.wait_ge(x1_done[r], KD // 2 + 1)
            norm.dve(dve)
            norm.dve_sample(dve)


def stage4(g):
    nc, a, sem = g.nc, g.a, g.sem
    x1T, h2T = g.hT, g.ogT
    with ExitStack() as st:
        sb = g.maker(st)
        wsd = sb("wsd", [P, 2, D])
        actT = sb("actT", [P, 2, T])
        t1 = sb("sh1", [P, T])
        gx = sb("gx", [P, KD, P + TS])
        g2 = sb("g2", [P, 2, D])
        bt = [sb(f"bt{i}", [P, D]) for i in range(2)]
        ht = [sb(f"ht{i}", [P, D]) for i in range(2)]
        rw = sb("rw", [P, KD, E])
        rb = sb("rb", [P, E])
        below = sb("below", [P, P])
        lower = sb("lower", [P, GROUPS, GROUPS])
        tokid = sb("tokid", [P, NT + 1])
        bnum = sb("bnum", [P, 2])
        zeros = sb("zeros", [P, NBLK])
        sc = sb("sc", [P, NT + 1, E])
        ch_ = sb("choice", [P, E])
        m8 = sb("m8", [P, GROUPS, 8])
        gs = sb("gs", [P, GROUPS])
        cmp = sb("cmp", [P, GROUPS, GROUPS])
        eq = sb("eq", [P, GROUPS, GROUPS])
        gr = sb("gr", [P, GROUPS])
        gmk = sb("gmk", [P, GROUPS])
        goff = sb("goff", [P, GROUPS])
        cm = sb("cm", [P, E])
        v8 = sb("v8", [P, 8])
        mr = sb("mr", [P, E])
        wsum = sb("wsum", [P, 1])
        wrec = sb("wrec", [P, 1])
        sel = sb("sel", [P, NT + 1, E])
        wn = sb("wn", [P, NT + 1, E])
        od = sb("od", [P, NT + 1, E])
        cnt_i = sb("cnt_i", [P, E], I32)
        nb_i = sb("nb_i", [P, E], I32)
        nb = sb("nb", [P, E])
        pend = sb("pend", [P, E])
        pst = sb("pst", [P, E])
        dest = sb("dest", [P, NT + 1, E])
        pick = sb("pick", [P, NT + 1, E])
        d8f = sb("d8f", [P, NT + 1, TOPK])
        be = sb("be", [P, 6])
        used = sb("used", [P, E])
        gi = sb("gi", [P, 2], I32)
        gp = sb("gp", [P, 2])
        trow = [sb(f"trow{i}", [P, P]) for i in range(2)]

        c0, c1, c2 = sem("c4_0"), sem("c4_1"), sem("c4_2")
        w_in = sem("ws_in")
        gx_ready = sem("gx_ready")
        g2_mm, g2_done, g2_out = sem("g2_mm"), sem("g2_done"), sem("g2_out")
        sh_mm = sem("sh_mm")
        sh_sig, sh_v = sem("sh_sig"), sem("sh_v")
        x_mm, y_mm, h_mm, l_mm = sem("x_mm"), sem("y_mm"), sem("h_mm"), sem("l_mm")
        bt_mul, bt_add = sem("bt_mul"), sem("bt_add")
        ht_done = sem("ht_done")
        bt_out, ht_out = [sem(f"bt_out{i}") for i in range(2)], [sem(f"ht_out{i}") for i in range(2)]
        sc_ready, sc_used = sem("sc_ready"), sem("sc_used")
        sel_done = sem("sel_done")
        rank_mm = sem("rank_mm")
        dest_done = sem("dest_done")
        be_done, be_mm, row_done = sem("be_done"), sem("be_mm"), sem("row_done")
        tok_zero, tok_out, tok_in, tok_mm, idx_done = sem("tok_zero"), sem("tok_out"), sem("tok_in"), sem("tok_mm"), sem("idx_done")
        dch = sem("dch4")
        blk = st.enter_context(nc.Block())
        NTT = NT + 1

        @blk.sync
        def _(sp):
            sp.dma_start(g.slab[0][:, :, 0:FE], a["ws_gate"][0].rearrange("(k p) f -> p k f", p=P)).then_inc(w_in, 16)
            sp.dma_start(g.slab[1][:, :, 0:FE], a["ws_up"][0].rearrange("(k p) f -> p k f", p=P)).then_inc(w_in, 16)
            sp.dma_start(wsd[:], a["ws_down"][0].rearrange("(k p) f -> p k f", p=P)).then_inc(w_in, 16)
            sp.dma_start(rw[:], a["router_w"][0].rearrange("(k p) f -> p k f", p=P)).then_inc(w_in, 16)
            sp.dma_start(rb[:], a["router_bias"].to_broadcast([P, E])).then_inc(w_in, 16)
            sp.wait_ge(g2_done, 2)
            sp.dma_start(g.g2_d.rearrange("w p d -> p w d"), g2[:]).then_inc(g2_out, 16)
            for t in range(NTT):
                s, n = tok(t)
                sp.wait_ge(ht_done, 2 * t + 2)
                sp.dma_start(g.h2_d[s:s + n, :], ht[t % 2][0:n, :]).then_inc(ht_out[t % 2], 16)
            for t in range(NTT):
                s, n = tok(t)
                sp.wait_ge(bt_add, t + 1)
                sp.dma_start(g.base_d[s:s + n, :], bt[t % 2][0:n, :]).then_inc(bt_out[t % 2], 16)
            sp.wait_ge(tok_out, 16 * NTT * TOPK)
            table = g.tok_d.rearrange("(b s) o -> b (s o)", s=B_)
            sp.dma_start(trow[0][:], table[0:P, :]).then_inc(tok_in, 16)
            sp.dma_start(trow[1][0:NBLK - P, :], table[P:NBLK, :]).then_inc(tok_in, 16)
            sp.wait_ge(g2_out, 16)
            for i in range(2):
                sp.wait_ge(ht_out[i], 16 * (5 - i))
                sp.wait_ge(bt_out[i], 16 * (5 - i))

        @blk.gpsimd
        def _(pool):
            pool.memset(below[:], 1.0).then_inc(c0, 1)
            pool.memset(lower[:], 1.0).then_inc(c0, 1)
            pool.memset(zeros[:], 0.0).then_inc(c0, 1)
            pool.wait_ge(c0, 3)
            pool.affine_select(out=below[:], in_=below[:], compare_op=ALU.is_gt, fill=0.0, base=0,
                               pattern=[[1, P]], channel_multiplier=-1).then_inc(c1, 1)
            pool.affine_select(out=lower[:], in_=lower[:], compare_op=ALU.is_gt, fill=0.0, base=0,
                               pattern=[[1, GROUPS], [-1, GROUPS]], channel_multiplier=0).then_inc(c1, 1)
            pool.iota(tokid[:], pattern=[[P, NTT]], base=0, channel_multiplier=1, allow_small_or_imprecise_dtypes=True).then_inc(c1, 1)
            pool.iota(bnum[:], pattern=[[P, 2]], base=0, channel_multiplier=1, allow_small_or_imprecise_dtypes=True).then_inc(c1, 1)
            pool.dma_start(g.tok_d.rearrange("(p b) o -> p (b o)", p=P), zeros[:]).then_inc(tok_zero, 16)
            pool.wait_ge(tok_zero, 16)
            pool.wait_ge(c1, 4)
            pool.wait_ge(dest_done, 2)
            for t in range(NTT):
                n = tok(t)[1]
                for k in range(TOPK):
                    pool.indirect_dma_start(out=g.tok_d, out_offset=bass.IndirectOffsetOnAxis(ap=g.dest8[0:n, t, k:k + 1], axis=0),
                                            in_=tokid[0:n, t:t + 1], in_offset=None).then_inc(tok_out, 16)
            pool.wait_ge(tok_out, 16 * NTT * TOPK)

        @blk.tensor
        def _(pe):
            M = nc.tensor.matmul
            pe.wait_ge(gx_ready, 2)
            for w, (lo, n) in enumerate(((0, P), (P, TS))):
                out = g.acc[w][0:n, 0:2, :].rearrange("p a (b c) -> p (a b) c", b=4)
                for k in range(KD):
                    mm = nc.tensor.transpose(out[:, k, :], gx[:, k, lo:lo + n], g.ident[:])
                mm.then_inc(g2_mm, 1)
            pe.wait_ge(w_in, 16 * 5)
            for t in range(NTT):
                s, n = tok(t)
                for i in range(2):
                    if t > 0:
                        pe.wait_ge(ht_done, 2 * t - 1 + i)
                    for k in range(4):
                        mm = nc.tensor.transpose(g.side[i][0:n, k * P:(k + 1) * P], h2T[:, 4 * i + k, s:s + n], g.ident[:])
                    mm.then_inc(h_mm, 1)
                if t > 0:
                    pe.wait_ge(sc_ready, t)
                else:
                    pe.wait_ge(g2_done, 2)
                for k in range(KD):
                    mm = M(g.acc[1][0:n, 2, 0:E], h2T[:, k, s:s + n], rw[:, k, :], start=(k == 0), stop=(k == KD - 1))
                mm.then_inc(l_mm, 1)
            pe.wait_ge(sc_ready, NTT)

            def shared(e):
                for u in range(2):
                    for k in range(KD):
                        for i, (s, n) in enumerate(PIECES):
                            mm = M(g.acc[u][:, i, 0:n], g.slab[u][:, k, e * P:(e + 1) * P], h2T[:, k, s:s + n],
                                   start=(k == 0), stop=(k == KD - 1))
                    mm.then_inc(sh_mm, 1)

            shared(0)
            pe.wait_ge(sel_done, NTT)
            pe.wait_ge(ht_done, 2 * NTT)
            pe.wait_ge(c1, 4)
            for t in range(NTT):
                out = g.side[t // NT][:, (t % NT) * E:(t % NT + 1) * E]
                M(out, below[:], sel[:, t, :], start=True, stop=(t == 0))
                for q in range(t):
                    M(out, g.ones[:], sel[:, q, :], start=False, stop=(q == t - 1))
            for t in range(NTT):
                mm = M(g.side[1][:, E:2 * E], g.ones[:], sel[:, t, :], start=(t == 0), stop=(t == NTT - 1))
            mm.then_inc(rank_mm, 1)
            pe.wait_ge(sh_v, 2)
            shared(1)
            pe.wait_ge(be_done, 2)
            for c in range(6):
                mm = M(g.side[c // 3][0:1, c % 3 * P:(c % 3 + 1) * P], be[:, c:c + 1], g.ident[:], start=True, stop=True)
            mm.then_inc(be_mm, 1)
            pe.wait_ge(sh_v, 4)
            for t in range(NTT):
                s, n = tok(t)
                if t > 0:
                    pe.wait_ge(bt_add, t)
                out = g.acc[0][0:n, 0:2, :].rearrange("p a (b c) -> p (a b) c", b=4)
                for k in range(KD):
                    mm = nc.tensor.transpose(out[:, k, :], x1T[:, k, s:s + n], g.ident[:])
                mm.then_inc(x_mm, 1)
                if t > 0:
                    pe.wait_ge(bt_mul, t)
                for hf in range(2):
                    for f in range(2):
                        mm = M(g.acc[1][0:n, hf, :], actT[:, f, s:s + n], wsd[:, f, hf * 512:(hf + 1) * 512],
                               start=(f == 0), stop=(f == 1))
                mm.then_inc(y_mm, 1)
            pe.wait_ge(tok_in, 32)
            pe.wait_ge(row_done, 1)
            nc.tensor.transpose(g.side[0][:, 0:P], trow[0][:], g.ident[:])
            nc.tensor.transpose(g.side[0][:, P:NBLK], trow[1][0:NBLK - P, :], g.ident[0:NBLK - P, 0:NBLK - P]).then_inc(tok_mm, 1)

        @blk.scalar
        def _(act):
            for t in range(NTT):
                s, n = tok(t)
                for i in range(2):
                    act.wait_ge(h_mm, 2 * t + 1 + i)
                    if t >= 2 and i == 0:
                        act.wait_ge(ht_out[t % 2], 16 * (t // 2))
                    nc.scalar.activation(ht[t % 2][0:n, i * 512:(i + 1) * 512], g.side[i][0:n, :], ACT.Copy).then_inc(ht_done, 1)
                act.wait_ge(l_mm, t + 1)
                nc.scalar.activation(sc[0:n, t, :], g.acc[1][0:n, 2, 0:E], ACT.Sigmoid).then_inc(sc_ready, 1)
            for e in range(2):
                act.wait_ge(sh_mm, 2 * e + 1)
                if e == 1:
                    act.wait_ge(sh_v, 2)
                for d, s in zip(flat2(t1[:]), slot2(g.acc[0])):
                    x = nc.scalar.activation(d, s, ACT.Sigmoid)
                x.then_inc(sh_sig, 1)

        @blk.vector
        def _(dve):
            V = nc.vector
            ch = Chain(dve, dch)
            V.tensor_copy(gx[:, :, 0:P], g.mod[:, G2 * KD:, 0:1].to_broadcast([P, KD, P])).then_inc(gx_ready, 1)
            V.tensor_copy(gx[:, :, P:].rearrange("p k (b t) -> p k b t", b=NB),
                          g.mod[:, G2 * KD:, 1:NB + 1].unsqueeze(3).to_broadcast([P, KD, NB, LS])).then_inc(gx_ready, 1)
            V.memset(sel[:, NT, :], 0.0)
            V.memset(wn[:, NT, :], 0.0)
            V.memset(g2[:, 1, :], 0.0)
            ch.step(V.memset(od[:, NT, :], 0.0))
            for w, n in enumerate((P, TS)):
                dve.wait_ge(g2_mm, w + 1)
                V.tensor_copy(g2[0:n, w, :], g.acc[w][0:n, 0:2, :].rearrange("p a c -> p (a c)")).then_inc(g2_done, 1)

            def shared(e):
                dve.wait_ge(sh_sig, e + 1)
                for d, s in zip(flat2(t1[:]), slot2(g.acc[0])):
                    x = V.tensor_tensor(d, s, d, ALU.mult)
                x.then_inc(sh_v, 1)
                dve.wait_ge(sh_v, 2 * e + 1)
                dve.wait_ge(sh_mm, 2 * e + 2)
                for d, s, q in zip(flat2(actT[:, e, :]), slot2(g.acc[1]), flat2(t1[:])):
                    x = V.tensor_tensor(d, s, q, ALU.mult)
                x.then_inc(sh_v, 1)

            dve.wait_ge(g2_done, 2)
            dve.wait_ge(c1, 4)
            for t in range(NTT):
                n = tok(t)[1]
                dve.wait_ge(sc_ready, t + 1)
                ch.step(V.tensor_tensor(ch_[0:n], sc[0:n, t, :], rb[0:n], ALU.add))
                for q in range(GROUPS):
                    x = V.max(m8[0:n, q, :], ch_[0:n, q * EG:(q + 1) * EG])
                ch.step(x)
                ch.step(V.tensor_tensor(gs[0:n], m8[0:n, :, 0], m8[0:n, :, 1], ALU.add))
                other = gs[0:n].unsqueeze(1).to_broadcast([n, GROUPS, GROUPS])
                own = gs[0:n].unsqueeze(2).to_broadcast([n, GROUPS, GROUPS])
                V.tensor_tensor(cmp[0:n], other, own, ALU.is_gt)
                ch.step(V.tensor_tensor(eq[0:n], other, own, ALU.is_equal))
                ch.step(V.tensor_tensor(eq[0:n], eq[0:n], lower[0:n], ALU.mult))
                ch.step(V.tensor_tensor(cmp[0:n], cmp[0:n], eq[0:n], ALU.add))
                ch.step(V.tensor_reduce(gr[0:n], cmp[0:n], AX, ALU.add))
                ch.step(V.tensor_scalar(gmk[0:n], gr[0:n], float(TOPG) - 0.5, None, ALU.is_lt))
                ch.step(V.tensor_scalar(goff[0:n], gmk[0:n], BIG, -BIG, ALU.mult, ALU.add))
                c3 = cm[0:n].rearrange("p (g e) -> p g e", g=GROUPS)
                ch.step(V.tensor_tensor(c3, ch_[0:n].rearrange("p (g e) -> p g e", g=GROUPS),
                                        gmk[0:n].unsqueeze(2).to_broadcast([n, GROUPS, EG]), ALU.mult))
                ch.step(V.tensor_tensor(c3, c3, goff[0:n].unsqueeze(2).to_broadcast([n, GROUPS, EG]), ALU.add))
                ch.step(V.max(v8[0:n], cm[0:n]))
                ch.step(V.match_replace(mr[0:n], v8[0:n], cm[0:n], 2 * BIG))
                ch.step(V.tensor_scalar(sel[0:n, t, :], mr[0:n], BIG, None, ALU.is_ge))
                V.tensor_tensor(wn[0:n, t, :], sc[0:n, t, :], sel[0:n, t, :], ALU.mult).then_inc(sc_used, 1)
                dve.wait_ge(sc_used, t + 1)
                ch.step(V.tensor_reduce(wsum[0:n], wn[0:n, t, :], AX, ALU.add))
                ch.step(V.reciprocal(wrec[0:n], wsum[0:n]))
                ch.step(V.tensor_scalar(wn[0:n, t, :], wn[0:n, t, :], wrec[0:n], SCALE_R, ALU.mult, ALU.mult))
                ch.step(V.tensor_tensor_scan(od[0:n, t, :], g.ones[0:n, 0:E], sel[0:n, t, :], 0.0, ALU.mult, ALU.add))
                V.tensor_tensor(od[0:n, t, :], od[0:n, t, :], sel[0:n, t, :], ALU.mult).then_inc(sel_done, 1)
            shared(0)
            dve.wait_ge(rank_mm, 1)
            dve.wait_ge(sel_done, NTT)
            ch.step(V.tensor_scalar(cnt_i[:], g.side[1][:, E:2 * E], float(B_ - 1), None, ALU.add))
            ch.step(V.tensor_scalar(nb_i[:], cnt_i[:], 7, None, ALU.arith_shift_right))
            ch.step(V.tensor_copy(nb[:], nb_i[:]))
            ch.step(V.tensor_tensor_scan(pend[:], g.ones[:, 0:E], nb[:], 0.0, ALU.mult, ALU.add))
            ch.step(V.tensor_tensor(pst[:], pend[:], nb[:], ALU.subtract))
            ch.step(V.tensor_scalar(pst[:], pst[:], float(B_), None, ALU.mult))
            V.tensor_tensor(dest[:, 0:NT, :], g.side[0][:].rearrange("p (t e) -> p t e", t=NT),
                            pst[:].unsqueeze(1).to_broadcast([P, NT, E]), ALU.add)
            ch.step(V.tensor_tensor(dest[:, NT, :], g.side[1][:, 0:E], pst[:], ALU.add))
            for what, out in ((dest, d8f), (wn, g.w8)):
                for k in range(TOPK):
                    ch.step(V.scalar_tensor_tensor(out=pick[:], in0=od[:], scalar=float(k + 1), in1=what[:],
                                                   op0=ALU.is_equal, op1=ALU.mult))
                    ch.step(V.tensor_reduce(out[:, :, k], pick[:], AX, ALU.add))
                if out is d8f:
                    V.tensor_copy(g.dest8[:], d8f[:]).then_inc(dest_done, 2)
            ch.step(V.tensor_scalar(used[:], nb[:], 0.5, None, ALU.is_ge))
            ch.step(V.tensor_tensor(pst[:], pend[:], nb[:], ALU.subtract))
            for c in range(2):
                b = bnum[:, c:c + 1]
                ch.step(V.tensor_scalar(cm[:], pend[:], b, None, ALU.is_le))
                ch.step(V.tensor_reduce(be[:, c:c + 1], cm[:], AX, ALU.add))
                ch.step(V.tensor_scalar(be[:, c:c + 1], be[:, c:c + 1], float(E - 1), None, ALU.min))
                ch.step(V.scalar_tensor_tensor(out=cm[:], in0=pst[:], scalar=b, in1=used[:], op0=ALU.is_le, op1=ALU.mult))
                ch.step(V.tensor_reduce(be[:, 2 + c:3 + c], cm[:], AX, ALU.add))
                ch.step(V.tensor_scalar(be[:, 2 + c:3 + c], be[:, 2 + c:3 + c], -1.0, None, ALU.add))
                ch.step(V.scalar_tensor_tensor(out=cm[:], in0=pst[:], scalar=b, in1=used[:], op0=ALU.is_equal, op1=ALU.mult))
                ch.step(V.tensor_reduce(be[:, 4 + c:5 + c], cm[:], AX, ALU.add))
            ch.step(V.tensor_copy(gi[:], be[:, 2:4]))
            ch.step(V.tensor_scalar(gi[:], gi[:], 1, None, ALU.bitwise_and))
            ch.step(V.tensor_copy(gp[:], gi[:]))
            ch.step(V.scalar_tensor_tensor(out=be[:, 4:6], in0=gp[:], scalar=1.0, in1=be[:, 4:6], op0=ALU.add, op1=ALU.mult))
            V.scalar_tensor_tensor(out=be[:, 4:6], in0=be[:, 2:4], scalar=4.0, in1=be[:, 4:6], op0=ALU.mult, op1=ALU.add).then_inc(be_done, 2)
            ch.step(V.tensor_scalar(cnt_i[0:1, 0:1], pend[0:1, E - 1:E], 1.0, None, ALU.add))
            ch.step(V.tensor_scalar(g.row[0:1, 6 * P:6 * P + 1], cnt_i[0:1, 0:1], 1, None, ALU.arith_shift_right))
            dve.wait_ge(be_mm, 1)
            for i in range(2):
                x = V.tensor_copy(g.row[0:1, i * 3 * P:(i + 1) * 3 * P], g.side[i][0:1, 0:3 * P])
            x.then_inc(row_done, 1)
            shared(1)
            for t in range(NTT):
                n = tok(t)[1]
                b = bt[t % 2][0:n, :]
                if t >= 2:
                    dve.wait_ge(bt_out[t % 2], 16 * (t // 2))
                dve.wait_ge(y_mm, t + 1)
                V.tensor_tensor(b, g.acc[1][0:n, 0:2, :].rearrange("p a c -> p (a c)"), g2[0:n, t // NT, :], ALU.mult).then_inc(bt_mul, 1)
                dve.wait_ge(bt_mul, t + 1)
                dve.wait_ge(x_mm, t + 1)
                V.tensor_tensor(b, g.acc[0][0:n, 0:2, :].rearrange("p a c -> p (a c)"), b, ALU.add).then_inc(bt_add, 1)
            dve.wait_ge(tok_mm, 1)
            V.tensor_copy(g.idx[:], g.side[0][:, 0:NBLK]).then_inc(idx_done, 1)


def stage5(g):
    nc, a, sem = g.nc, g.a, g.sem
    with ExitStack() as st:
        sb = g.maker(st)
        raw = [sb(f"raw{i}", [P, KD, 2 * FE]) for i in range(2)]
        rawd = [sb(f"rawd{i}", [P, 2, D]) for i in range(2)]
        wgu = [sb(f"wgu{x}", [P, 2, KD, 2 * FE], F32R) for x in "hl"]
        wd = [sb(f"wd{x}", [P, 2, 2, D], F32R) for x in "hl"]
        xg = [sb(f"xg{i}", [P, D]) for i in range(2)]
        xe = [[sb(f"xe{i}{x}", [P, KD, B_], F32R) for x in "hl"] for i in range(2)]
        sg = [sb(f"sg{i}", [P, FE]) for i in range(2)]
        hh = [sb(f"hh{i}", [P, FE]) for i in range(2)]
        hT = [[sb(f"hTe{i}{x}", [P, 2, B_], F32R) for x in "hl"] for i in range(2)]
        ys = [sb(f"ys{i}", [P, D]) for i in range(2)]

        def pair(name):
            return [sem(f"{name}{i}") for i in range(2)]

        raw_in, rawd_in = pair("raw_in"), pair("rawd_in")
        gu_hi, d_hi = sem("gu_hi"), sem("d_hi")
        gu_lo, d_lo = sem("gu_lo"), sem("d_lo")
        GU0, D0 = 4, 2
        x_in = pair("xg_in")
        x_mm, xhi, xlo = pair("xe_mm"), pair("xhi"), pair("xlo")
        gu_mm = pair("gu_mm")
        sg_ready, hm, h_ready = pair("sg_ready"), pair("hm"), pair("h_ready")
        h_mm, hhi, hlo = pair("h_mm"), pair("hhi"), pair("hlo")
        y_mm, ys_ready, y_out = pair("ye_mm"), pair("ys_ready"), pair("y_out")
        blk = st.enter_context(nc.Block())
        xps = g.acc[0][:, 0:2, :]
        gps = [g.side[0], g.side[1]]
        hps = g.acc[0][:, 2, :]
        yps = g.acc[1][:, 0:2, :]
        NPAIR = NBLK // 2
        LEAST = -(-T * TOPK // (2 * B_))

        def expert(eng, b):
            return eng.value_load(g.row[0:1, bass.ds(b, 1)], min_val=0, max_val=E - 1)

        def word(eng, b):
            return eng.value_load(g.row[0:1, bass.ds(b + 4 * P, 1)], min_val=0, max_val=4 * E - 2)

        def pairs_in_use(eng):
            return eng.value_load(g.row[0:1, 6 * P:6 * P + 1], min_val=LEAST, max_val=NPAIR)

        def if_first(eng, w, part):
            for p in range(2):
                with eng.If(w % 4 == p + 1):
                    part(p, w >> 2)


        @blk.sync
        def _(sp):
            with sp.Fori(0, NBLK) as b:
                def load(p, gr):
                    e = expert(sp, b)
                    sp.wait_ge(gu_lo, gr * 2 + (GU0 - 2))
                    for w, name in enumerate(("we_gate", "we_up")):
                        sp.dma_start(raw[p][:, :, w * FE:(w + 1) * FE],
                                     a[name][0][bass.ds(e, 1)].rearrange("e (k p) f -> p (e k) f", p=P)).then_inc(raw_in[p], 16)
                    sp.wait_ge(d_lo, gr + (D0 - 1))
                    sp.dma_start(rawd[p][:], a["we_down"][0][bass.ds(e, 1)].rearrange("e (k p) f -> p (e k) f", p=P)).then_inc(rawd_in[p], 16)

                if_first(sp, word(sp, b), load)

        @blk.gpsimd
        def _(pool):
            used = pairs_in_use(pool)

            def gather(c):
                for u in range(2):
                    pool.wait_ge(x_mm[u], c + 1)
                    b = 2 * c + u
                    pool.indirect_dma_start(out=xg[u][:], out_offset=None, in_=g.h2_d,
                                            in_offset=bass.IndirectOffsetOnAxis(ap=g.idx[:, b:b + 1], axis=0)).then_inc(x_in[u], 16)

            for c in range(NPAIR):
                if c < LEAST:
                    gather(c)
                else:
                    with pool.If(used > c):
                        gather(c)
            for u in range(2):
                pool.wait_ge(y_out[u], used * 16 + 16)

        @blk.tensor
        def _(pe):
            M = nc.tensor.matmul

            def turn(u, c):
                pe.wait_ge(x_in[u], c * 16 + 16)
                pe.wait_ge(xlo[1 - u], c + (u + 1))
                out = xps.rearrange("p a (b c) -> p (a b) c", b=4)
                for k in range(KD):
                    mm = nc.tensor.transpose(out[:, k, :], xg[u][:, k * P:(k + 1) * P], g.ident[:])
                mm.then_inc(x_mm[u], 1)

            def three(out, x, w, first, last):
                M(out, x[1], w[0], start=first, stop=False)
                M(out, x[0], w[1], start=False, stop=False)
                return M(out, x[0], w[0], start=False, stop=last)

            def gate_up_half(u, parity, ks):
                for k in ks:
                    ws = [w[:, bass.ds(parity, 1), k, :].rearrange("p g n -> p (g n)") for w in wgu]
                    mm = three(gps[u][:], [x[:, k, :] for x in xe[u]], ws, k == 0, k == KD - 1)
                return mm

            def gate_up_begin(u, c, w):
                pe.wait_ge(xlo[u], c + 2)
                pe.wait_ge(gu_lo, (w >> 2) * 2 + (GU0 + 2))
                pe.wait_ge(h_ready[u], c + 1)
                gate_up_half(u, (w >> 2) % 2, range(KD // 2))

            def gate_up_end(u, w):
                gate_up_half(u, (w >> 2) % 2, range(KD // 2, KD)).then_inc(gu_mm[u], 1)

            def turn_h(u, c):
                pe.wait_ge(h_ready[u], c + 2)
                pe.wait_ge(hlo[1 - u], c + (u + 1))
                for f in range(2):
                    mm = nc.tensor.transpose(hps[:, f * P:(f + 1) * P], hh[u][:, f * P:(f + 1) * P], g.ident[:])
                mm.then_inc(h_mm[u], 1)

            def down(u, c, w):
                pe.wait_ge(hlo[u], c + 2)
                pe.wait_ge(d_lo, (w >> 2) + (D0 + 1))
                pe.wait_ge(ys_ready[1 - u], c + (u + 1))
                for hf in range(2):
                    for f in range(2):
                        ws = [x[:, bass.ds((w >> 2) % 2, 1), f, hf * 512:(hf + 1) * 512].rearrange("p g n -> p (g n)") for x in wd]
                        mm = three(yps[:, hf, :], [x[:, f, :] for x in hT[u]], ws, f == 0, f == 1)
                mm.then_inc(y_mm[u], 1)

            used = pairs_in_use(pe)
            turn(0, 0)
            turn(1, 0)
            w0 = word(pe, 0)
            gate_up_begin(0, 0, w0)
            gate_up_end(0, w0)
            with pe.Fori(0, NPAIR - 1) as i:
                with pe.If(used > i + 1):
                    w = [word(pe, i * 2 + d) for d in range(3)]
                    for u in range(2):
                        turn(u, i + 1)
                        gate_up_begin(1 - u, i + u, w[u + 1])
                        turn_h(u, i)
                        gate_up_end(1 - u, w[u + 1])
                        down(u, i, w[u])
            L = used - 1
            w = [word(pe, L * 2 + d) for d in range(2)]
            gate_up_begin(1, L, w[1])
            turn_h(0, L)
            gate_up_end(1, w[1])
            down(0, L, w[0])
            turn_h(1, L)
            down(1, L, w[1])

        H = KD // 2

        @blk.scalar
        def _(act):
            A = nc.scalar.activation
            for u in range(2):
                act.sem_inc(xhi[u], 1)
                act.sem_inc(ys_ready[u], 1)
                act.sem_inc(y_out[u], 16)

            def split_gu(q, w):
                def part(p, gr):
                    if q == 0:
                        act.wait_ge(raw_in[p], (gr >> 1) * 32 + 32)
                    A(wgu[0][:, p, q * H:(q + 1) * H, :], raw[p][:, q * H:(q + 1) * H, :], ACT.Copy).then_inc(gu_hi, 1)
                if_first(act, w, part)

            def split_d(w):
                def part(p, gr):
                    act.wait_ge(rawd_in[p], (gr >> 1) * 16 + 16)
                    A(wd[0][:, p], rawd[p][:], ACT.Copy).then_inc(d_hi, 1)
                if_first(act, w, part)

            def split_x(u, c):
                act.wait_ge(x_mm[u], c + 2)
                act.wait_ge(gu_mm[u], c + 1)
                A(xe[u][0][:].rearrange("p k s -> p (k s)").rearrange("p (a c) -> p a c", a=2), xps, ACT.Copy).then_inc(xhi[u], 1)

            def sigmoid(u, c):
                act.wait_ge(gu_mm[u], c + 2)
                act.wait_ge(h_ready[u], c + 1)
                A(sg[u][:], gps[u][:, 0:FE], ACT.Sigmoid).then_inc(sg_ready[u], 1)

            def split_h(u, c):
                act.wait_ge(h_mm[u], c + 2)
                act.wait_ge(y_mm[u], c + 1)
                A(hT[u][0][:], hps[:, 0:2 * B_].rearrange("p (f s) -> p f s", f=2), ACT.Copy).then_inc(hhi[u], 1)

            def store(u, c, b):
                act.wait_ge(y_mm[u], c + 2)
                act.wait_ge(y_out[u], c * 16 + 16)
                A(ys[u][:].rearrange("p (a c) -> p a c", a=2), yps, ACT.Copy).then_inc(ys_ready[u], 1)
                act.wait_ge(ys_ready[u], c + 2)
                act.dma_start(g.y_d[bass.ds(b * B_, B_), :], ys[u][:]).then_inc(y_out[u], 16)

            used = pairs_in_use(act)
            w = [word(act, b) for b in range(2)]
            split_x(0, 0)
            split_gu(0, w[0])
            split_gu(1, w[0])
            split_x(1, 0)
            split_gu(0, w[1])
            split_gu(1, w[1])
            split_d(w[0])
            sigmoid(0, 0)
            with act.Fori(0, NPAIR - 1) as i:
                with act.If(used > i + 1):
                    w = [word(act, i * 2 + (1 + d)) for d in range(3)]
                    for u in range(2):
                        split_x(u, i + 1)
                        split_gu(0, w[u + 1])
                        split_h(u, i)
                        split_gu(1, w[u + 1])
                        split_d(w[u])
                        sigmoid(1 - u, i + u)
                        store(u, i, i * 2 + u)
            L = used - 1
            split_h(0, L)
            split_d(word(act, L * 2 + 1))
            sigmoid(1, L)
            store(0, L, L * 2)
            split_h(1, L)
            store(1, L, L * 2 + 1)

        @blk.vector
        def _(dve):
            V = nc.vector
            for u in range(2):
                dve.sem_inc(xlo[u], 1)
                dve.sem_inc(hlo[u], 1)
                dve.sem_inc(h_ready[u], 1)
                dve.sem_inc(x_mm[u], 1)
                dve.sem_inc(gu_mm[u], 1)
                dve.sem_inc(h_mm[u], 1)
                dve.sem_inc(y_mm[u], 1)
            dve.sem_inc(gu_lo, GU0)
            dve.sem_inc(d_lo, D0)

            def split_gu(q, w):
                def part(p, gr):
                    dve.wait_ge(gu_hi, gr * 2 + (q + 1))
                    V.tensor_tensor(wgu[1][:, p, q * H:(q + 1) * H, :], raw[p][:, q * H:(q + 1) * H, :],
                                    wgu[0][:, p, q * H:(q + 1) * H, :].bitcast(F32), ALU.subtract).then_inc(gu_lo, 1)
                if_first(dve, w, part)

            def split_d(w):
                def part(p, gr):
                    dve.wait_ge(d_hi, gr + 1)
                    V.tensor_tensor(wd[1][:, p], rawd[p][:], wd[0][:, p].bitcast(F32), ALU.subtract).then_inc(d_lo, 1)
                if_first(dve, w, part)

            def split_x(u, c):
                dve.wait_ge(xhi[u], c + 2)
                V.tensor_tensor(xe[u][1][:].rearrange("p k s -> p (k s)").rearrange("p (a c) -> p a c", a=2), xps,
                                xe[u][0][:].bitcast(F32).rearrange("p k s -> p (k s)").rearrange("p (a c) -> p a c", a=2),
                                ALU.subtract).then_inc(xlo[u], 1)

            def split_h(u, c):
                dve.wait_ge(hhi[u], c + 1)
                V.tensor_tensor(hT[u][1][:], hps[:, 0:2 * B_].rearrange("p (f s) -> p f s", f=2), hT[u][0][:].bitcast(F32),
                                ALU.subtract).then_inc(hlo[u], 1)

            def swiglu(u, c):
                dve.wait_ge(sg_ready[u], c + 1)
                dve.wait_ge(h_mm[u], c + 1)
                V.tensor_tensor(sg[u][:], gps[u][:, 0:FE], sg[u][:], ALU.mult).then_inc(hm[u], 1)
                dve.wait_ge(hm[u], c + 1)
                V.tensor_tensor(hh[u][:], gps[u][:, FE:2 * FE], sg[u][:], ALU.mult).then_inc(h_ready[u], 1)

            used = pairs_in_use(dve)
            w = [word(dve, b) for b in range(2)]
            split_x(0, 0)
            split_gu(0, w[0])
            split_gu(1, w[0])
            split_x(1, 0)
            split_gu(0, w[1])
            split_gu(1, w[1])
            swiglu(0, 0)
            with dve.Fori(0, NPAIR - 1) as i:
                with dve.If(used > i + 1):
                    w = [word(dve, i * 2 + d) for d in range(4)]
                    for u in range(2):
                        split_d(w[u])
                        split_x(u, i + 1)
                        split_h(u, i)
                        split_gu(0, w[u + 2])
                        split_gu(1, w[u + 2])
                        swiglu(1 - u, i + u)
            L = used - 1
            w = [word(dve, L * 2 + d) for d in range(2)]
            split_d(w[0])
            split_h(0, L)
            swiglu(1, L)
            split_d(w[1])
            split_h(1, L)


def stage6(g):
    nc, a, sem, o = g.nc, g.a, g.sem, g.o
    NTT = NT + 1
    with ExitStack() as st:
        sb = g.maker(st)
        R = 6
        yg = [sb(f"yg{i}", [P, D]) for i in range(R)]
        base = [sb(f"base{i}", [P, D]) for i in range(2)]
        g2 = sb("g2b", [P, 2, D])
        fw = sb("fw", [P, D])
        acc = [sb(f"ysum{i}", [P, D]) for i in range(2)]
        sqs = sb("sqs", [P, D])
        ss = sb("ss", [P, NTT])
        rt = sb("rt", [P, NTT])
        rc = sb("rc", [P, NTT])
        yo = [sb(f"yo{i}", [P, D]) for i in range(2)]
        c_in = sem("c6_in")
        b_in = [sem(f"b6_in{i}") for i in range(2)]
        y_in = [sem(f"y6_in{i}") for i in range(R)]
        add = sem("add6")
        x2m, x2_ready = sem("x2m"), sem("x2_ready")
        sum_ready, root_ready, inv_ready = sem("sum6"), sem("root6"), sem("inv6")
        yo_ready = sem("yo_ready")
        out_done = [sem(f"out{i}") for i in range(2)]
        blk = st.enter_context(nc.Block())

        @blk.gpsimd
        def _(pool):
            n_ = 0
            for t in range(NTT):
                n = tok(t)[1]
                for k in range(TOPK):
                    if n_ >= R:
                        pool.wait_ge(add, n_ - R + 1)
                    pool.indirect_dma_start(out=yg[n_ % R][0:n, :], out_offset=None, in_=g.y_d,
                                            in_offset=bass.IndirectOffsetOnAxis(ap=g.dest8[0:n, t, k:k + 1], axis=0)
                                            ).then_inc(y_in[n_ % R], 16)
                    n_ += 1

        def store(sp, t):
            s, n = tok(t)
            sp.wait_ge(yo_ready, t + 1)
            dst = o["y_p"][0, s:s + n, :] if t < NT else o["y_s"].rearrange("b t d -> (b t) d")
            sp.dma_start(dst, yo[t % 2][0:n, :]).then_inc(out_done[t % 2], 16)

        @blk.sync
        def _(sp):
            sp.dma_start(fw[:], a["final_norm_w"].rearrange("(o d) -> o d", o=1).to_broadcast([P, D])).then_inc(c_in, 16)
            sp.dma_start(g2[:], g.g2_d.rearrange("w p d -> p w d")).then_inc(c_in, 16)
            for t in range(NTT):
                s, n = tok(t)
                if t >= 2:
                    sp.wait_ge(x2_ready, t - 1)
                sp.dma_start(base[t % 2][0:n, :], g.base_d[s:s + n, :]).then_inc(b_in[t % 2], 16)
                if t >= 1:
                    store(sp, t - 1)
            store(sp, NTT - 1)
            for i in range(2):
                sp.wait_ge(out_done[i], 16 * (5 - i))

        @blk.scalar
        def _(act):
            for t in range(NTT):
                n = tok(t)[1]
                act.wait_ge(x2_ready, t + 1)
                if t > 0:
                    act.wait_ge(root_ready, t)
                nc.scalar.activation(sqs[0:n, :], acc[t % 2][0:n, :], ACT.Square, accum_out=ss[0:n, t:t + 1]).then_inc(sum_ready, 1)
                act.wait_ge(sum_ready, t + 1)
                nc.scalar.activation(rt[0:n, t:t + 1], ss[0:n, t:t + 1], ACT.Sqrt, scale=1.0 / D, bias=g.eps[0:n]).then_inc(root_ready, 1)

        @blk.vector
        def _(dve):
            V = nc.vector
            n_ = 0

            def final(t):
                n = tok(t)[1]
                dve.wait_ge(root_ready, t + 1)
                V.reciprocal(rc[0:n, t:t + 1], rt[0:n, t:t + 1]).then_inc(inv_ready, 1)
                dve.wait_ge(inv_ready, t + 1)
                if t >= 2:
                    dve.wait_ge(out_done[t % 2], 16 * (t // 2))
                V.scalar_tensor_tensor(out=yo[t % 2][0:n, :], in0=acc[t % 2][0:n, :], scalar=rc[0:n, t:t + 1], in1=fw[0:n, :],
                                       op0=ALU.mult, op1=ALU.mult).then_inc(yo_ready, 1)

            dve.wait_ge(c_in, 32)
            for t in range(NTT):
                n = tok(t)[1]
                s = acc[t % 2][0:n, :]
                for k in range(TOPK):
                    dve.wait_ge(y_in[n_ % R], 16 * (n_ // R + 1))
                    row, w = yg[n_ % R][0:n, :], g.w8[0:n, t, k:k + 1]
                    if k == 0:
                        if t >= 2:
                            dve.wait_ge(yo_ready, t - 1)
                        x = V.tensor_scalar(s, row, w, None, ALU.mult)
                    else:
                        dve.wait_ge(add, n_)
                        x = V.scalar_tensor_tensor(out=s, in0=row, scalar=w, in1=s, op0=ALU.mult, op1=ALU.add)
                    x.then_inc(add, 1)
                    n_ += 1
                dve.wait_ge(add, n_)
                V.tensor_tensor(s, s, g2[0:n, t // NT, :], ALU.mult).then_inc(x2m, 1)
                dve.wait_ge(x2m, t + 1)
                dve.wait_ge(b_in[t % 2], 16 * (t // 2 + 1))
                V.tensor_tensor(s, s, base[t % 2][0:n, :], ALU.add).then_inc(x2_ready, 1)
                if t >= 1:
                    final(t - 1)
            final(NTT - 1)


_INS = ["x_prompt", "x_sample", "state_conv", "state_gla", "c_prompt", "c_sample", "w_ada", "b_ada", "norm1_w", "w_in",
        "conv_w", "w_gk", "b_gk", "gla_norm_w", "w_out_conv", "w_out_gla", "w_o", "norm2_w", "router_w", "router_bias",
        "we_gate", "we_up", "we_down", "ws_gate", "ws_up", "ws_down", "final_norm_w"]
_OUTS = [("y_p", (1, TP, D)), ("y_s", (NB, LS, D)), ("conv_p", (1, 1, CW - 1, D)), ("gla_p", (1, 1, HEADS, DK, DV)),
         ("conv_s", (1, NB, CW - 1, D)), ("gla_s", (1, NB, HEADS, DK, DV))]


def kernel(**inputs):
    import concourse.bacc as bacc
    from concourse.bass_utils import run_bass_kernel_spmd

    nc = bacc.Bacc("TRN2", target_bir_lowering=False, num_devices=1)
    arrays = {name: np.ascontiguousarray(inputs[name]) for name in _INS}
    ins = {name: nc.dram_tensor(name, x.shape, F32, kind="ExternalInput").ap() for name, x in arrays.items()}
    outs = {name: nc.dram_tensor(f"out_{name}", shape, F32, kind="ExternalOutput").ap() for name, shape in _OUTS}
    build(nc, ins, outs)
    r = run_bass_kernel_spmd(nc, [arrays], core_ids=[0])
    return tuple(r.results[0][f"out_{name}"] for name, _ in _OUTS)
```

```python
from contextlib import ExitStack

import numpy as np
import concourse.bass as bass
from concourse import mybir

ALU = mybir.AluOpType
ACT = mybir.ActivationFunctionType
F32 = mybir.dt.float32
F32R = mybir.dt.float32r
I32 = mybir.dt.int32
U32 = mybir.dt.uint32
AX = mybir.AxisListType.X

P = 128
D = 1024
KD = D // P
TP = 1024
NB, LS = 8, 8
TS = NB * LS
T = TP + TS
NT = TP // P
HEADS, DK, DV = 4, 128, 256
CH = 64
RANK = 16
E, GROUPS, TOPG, TOPK = 64, 8, 4, 8
EG = E // GROUPS
FE = 256
SCALE_R = 2.5
EPS = 1e-6
B_ = 128
NBLK = (T * TOPK + E * (B_ - 1) + B_ - 1) // B_
NSLOT = NBLK * B_
MINSLOT = -(-T * TOPK // (2 * B_)) * 2 * B_
PIECES = [(0, 384), (384, 384), (768, 320)]
C_B, C_C, C_H, C_Q, C_K, C_V, C_G, C_Z = 0, D, 2 * D, 3 * D, 3 * D + 512, 4 * D, 5 * D, 6 * D
C_UA, C_UB = 6 * D + RANK, 7 * D + RANK
SW = 384
V_ADA, V_N1, V_N2, V_CONV, V_BGK, V_GNW, V_END = 0, 48, 56, 64, 88, 92, 94
SH1, SC1, G1, SH2, SC2, G2 = range(6)
BIG = 1e30
CW = 3


def tok(t):
    return (t * P, P) if t < NT else (TP, TS)


class Tally:

    def __init__(self, sem):
        self.sem, self.base, self.n, self.outer = sem, 0, 0, None

    def mark(self, ins, by=1):
        ins.then_inc(self.sem, by)
        self.n += by

    def value(self):
        return self.base + self.n

    def loop(self, i, per):
        self.outer, self.per = self.base + self.n, per
        self.base, self.n = i * per + self.outer, 0

    def end(self, count):
        assert self.n == self.per, (self.n, self.per)
        self.base, self.n = self.outer + count * self.per, 0


class Chain(Tally):

    def __init__(self, eng, sem):
        super().__init__(sem)
        self.eng = eng

    def step(self, ins):
        self.mark(ins)
        self.eng.wait_ge(self.sem, self.value())


def flat2(ap):
    return [ap[:, 0:768].rearrange("p (a b) -> p a b", a=2), ap[:, 768:T]]


def slot2(ps):
    return [ps[:, 0:2, 0:384], ps[:, 2, 0:320]]


def slot3(ps):
    return [ps[:, 0:2, 0:384], ps[:, 2, 0:256], ps[:, 2, 256:320].rearrange("p (b t) -> p b t", b=NB)]


def flat3(ap):
    return [ap[:, 0:768].rearrange("p (a b) -> p a b", a=2), ap[:, 768:TP],
            ap[:, TP:T].rearrange("p (b t) -> p b t", b=NB)]


def padded3(ap):
    w = CW - 1
    return [ap[:, w:w + 768].rearrange("p (a b) -> p a b", a=2), ap[:, w + 768:w + TP],
            ap[:, w + TP:w + TP + NB * (LS + w)].rearrange("p (b t) -> p b t", b=NB)[:, :, w:w + LS]]


class Shared:
    pass


def build(nc, a, o):
    ctx = ExitStack()
    with ctx:
        early = []

        def sem(name):
            early.append(nc.alloc_semaphore(name))
            return early[-1]

        def maker(stack):
            return lambda name, shape, dt=F32: stack.enter_context(nc.sbuf_tensor(name, shape, dt))

        sb = maker(ctx)
        acc = [ctx.enter_context(nc.psum_tensor(f"acc{i}", [P, 3, 512], F32)) for i in range(2)]
        side = [ctx.enter_context(nc.psum_tensor(f"side{i}", [P, 512], F32)) for i in range(2)]

        xT_d = nc.dram_tensor("xT_d", [KD, P, T], F32, kind="Internal").ap()
        yc_d = nc.dram_tensor("yc_d", [KD, P, T], F32, kind="Internal").ap()
        og_d = nc.dram_tensor("og_d", [KD, P, T], F32, kind="Internal").ap()
        h2_d = nc.dram_tensor("h2_d", [T, D], F32, kind="Internal").ap()
        base_d = nc.dram_tensor("base_d", [T, D], F32, kind="Internal").ap()
        tok_d = nc.dram_tensor("tok_d", [NSLOT, 1], F32, kind="Internal").ap()
        g2_d = nc.dram_tensor("g2_d", [2, P, D], F32, kind="Internal").ap()
        y_d = nc.dram_tensor("y_d", [NSLOT, D], F32, kind="Internal").ap()

        ident = sb("ident", [P, P])
        ones = sb("ones", [P, P])
        eps = sb("eps", [P, 1])
        vec = sb("vec", [P, V_END])
        mod = sb("mod", [P, 6 * KD, NB + 1])
        amp = sb("amp", [P, 2, KD, NB + 1])

        g = Shared()
        g.dest8 = sb("dest8", [P, NT + 1, TOPK], U32)
        g.w8 = sb("w8", [P, NT + 1, TOPK])
        g.row = sb("row", [1, 6 * P + 1], I32)
        g.idx = sb("idx", [P, NBLK], U32)
        g.nc, g.a, g.o, g.sem, g.maker, g.acc, g.side = nc, a, o, sem, maker, acc, side
        g.yc_d, g.og_d = yc_d, og_d
        g.xT_d, g.h2_d, g.base_d, g.tok_d, g.y_d, g.g2_d = xT_d, h2_d, base_d, tok_d, y_d, g2_d
        g.ident, g.ones, g.eps, g.vec, g.mod, g.amp = ident, ones, eps, vec, mod, amp

        with ExitStack() as mix:
            sm = maker(mix)
            g.hT = sm("hT", [P, KD, T])
            g.stT = sm("stT", [P, KD, 16])
            g.lastT = sm("lastT", [P, KD, 18])
            with ExitStack() as first:
                sf = maker(first)
                g.ogT = sf("ogT", [P, KD, T])
                g.ycT = sf("ycT", [P, KD, T])
                g.slab = [sf(f"slab{i}", [P, KD, SW]) for i in range(2)]
                stage1(g)
                stage2(g)
            stage3(g)
            g.h2T = sm("h2T", [P, KD, T])
            second_norm(g)
            stage4(g)
        nc.clear_and_free_semaphores(early)
        nc.all_engine_barrier()
        stage5(g)
        stage6(g)


class Norm:

    def __init__(self, g, tag, which, src, dst, sq, rst):
        self.g, self.which, self.src, self.dst, self.sq, self.rst = g, which, src, dst, sq, rst
        self.sq_ready = g.sem(f"{tag}_sq_ready")
        self.sq_used = g.sem(f"{tag}_sq_used")
        self.root = g.sem(f"{tag}_root")
        self.inv = g.sem(f"{tag}_inv")
        self.scaled = g.sem(f"{tag}_scaled")
        self.sample1 = g.sem(f"{tag}_sample1")
        self.sample2 = g.sem(f"{tag}_sample2")
        self.prompt = g.sem(f"{tag}_prompt")
        self.shift = (SH1, SH2)[which] * KD

    def act(self, eng, src_ready):
        g = self.g
        for k in range(KD):
            if src_ready:
                eng.wait_ge(*src_ready(k))
            if k >= 2:
                eng.wait_ge(self.sq_used, k - 1)
            g.nc.scalar.activation(self.sq[k % 2][:, 0:T], self.src[:, k, :], ACT.Square).then_inc(self.sq_ready, 1)
        eng.wait_ge(self.sq_used, KD)
        for d, s in zip(flat2(self.rst[:, 0:T]), slot2(g.acc[1])):
            g.nc.scalar.activation(d, s, ACT.Sqrt, scale=1.0 / D, bias=g.eps[:]).then_inc(self.root, 1)

    def act_prompt(self, eng):
        g = self.g
        for k in range(KD):
            eng.wait_ge(self.scaled, k + 1)
            g.nc.scalar.activation(self.dst[:, k, 0:TP], self.dst[:, k, 0:TP], ACT.Identity,
                                   scale=g.amp[:, self.which, k, 0:1],
                                   bias=g.mod[:, self.shift + k, 0:1]).then_inc(self.prompt, 1)

    def pe(self, eng):
        g = self.g
        for k in range(KD):
            eng.wait_ge(self.sq_ready, k + 1)
            for i, (s, n) in enumerate(PIECES):
                mm = g.nc.tensor.matmul(g.acc[1][:, i, 0:n], g.ones[:], self.sq[k % 2][:, s:s + n],
                                        start=(k == 0), stop=(k == KD - 1))
            mm.then_inc(self.sq_used, 1)

    def dve(self, eng):
        g = self.g
        eng.wait_ge(self.root, 2)
        g.nc.vector.reciprocal(self.rst[:, 0:T], self.rst[:, 0:T]).then_inc(self.inv, 1)
        eng.wait_ge(self.inv, 1)
        for k in range(KD):
            g.nc.vector.tensor_tensor(self.dst[:, k, :], self.src[:, k, :], self.rst[:, 0:T],
                                      ALU.mult).then_inc(self.scaled, 1)

    def dve_sample(self, eng):
        g = self.g
        v = self.dst[:, :, TP:T].rearrange("p k (b t) -> p k b t", b=NB)
        eng.wait_ge(self.scaled, KD)
        sc = g.amp[:, self.which, :, 1:NB + 1].unsqueeze(3).to_broadcast([P, KD, NB, LS])
        sh = g.mod[:, self.shift:self.shift + KD, 1:NB + 1].unsqueeze(3).to_broadcast([P, KD, NB, LS])
        g.nc.vector.tensor_tensor(v, v, sc, ALU.mult).then_inc(self.sample1, 1)
        eng.wait_ge(self.sample1, 1)
        g.nc.vector.tensor_tensor(v, v, sh, ALU.add).then_inc(self.sample2, 1)

    def wait_done(self, eng):
        eng.wait_ge(self.prompt, KD)
        eng.wait_ge(self.sample2, 1)


def stage1(g):
    nc, a, sem = g.nc, g.a, g.sem
    NSLAB = 6 * D // SW
    with ExitStack() as st:
        sb = g.maker(st)
        vrow = sb("vrow", [V_END, P])
        crow = sb("crow", [(NB + 1) * KD, P])
        srow = sb("srow", [16, D])
        xin = [sb(f"xin{i}", [P, D]) for i in range(2)]
        xT = sb("xT", [P, KD, T])
        csig = sb("csig", [P, (NB + 1) * KD])
        cact = sb("cact", [P, KD, NB + 1])
        sq = [sb(f"sq1_{i}", [P, T]) for i in range(2)]
        rst = sb("rst1", [P, T])
        modrow = g.ycT[0:NB + 1].rearrange("p k t -> p (k t)")

        const0 = sem("const0")
        const = sem("const")
        rows_in = sem("rows_in")
        x_in = [sem(f"x_in{i}") for i in range(2)]
        ada_in = [sem(f"ada_in{i}") for i in range(2)]
        ada_mm = [sem(f"ada_mm{i}") for i in range(2)]
        ada_row = [sem(f"ada_row{i}") for i in range(2)]
        ada_turned = sem("ada_turned")
        rowsT = sem("rowsT")
        csig_ready = sem("csig_ready")
        vec_ready = sem("vec_ready")
        cact_ready = sem("cact_ready")
        x_turned = sem("x_turned")
        x_copied = sem("x_copied")
        mod_ready = sem("mod_ready")
        amp_ready = sem("amp_ready")
        xT_out = sem("xT_out")
        norm = Norm(g, "n1", 0, xT, g.hT, sq, rst)
        xp, xs = a["x_prompt"], a["x_sample"]
        blk = st.enter_context(nc.Block())

        @blk.gpsimd
        def _(pool):
            pool.memset(g.ident[:], 0.0).then_inc(const0, 1)
            pool.memset(g.ones[:], 1.0).then_inc(const, 1)
            pool.memset(g.eps[:], EPS).then_inc(const, 1)
            pool.wait_ge(const0, 1)
            pool.affine_select(out=g.ident[:], in_=g.ident[:], compare_op=ALU.not_equal, fill=1.0, base=0,
                               pattern=[[-1, P]], channel_multiplier=1).then_inc(const, 1)

        @blk.sync
        def _(sp):
            rows = [("b_ada", V_ADA, V_N1, a["b_ada"].rearrange("l (r c) -> (l r) c", c=P)),
                    ("n1", V_N1, V_N2, a["norm1_w"].rearrange("l (r c) -> (l r) c", c=P)),
                    ("n2", V_N2, V_CONV, a["norm2_w"].rearrange("l (r c) -> (l r) c", c=P)),
                    ("conv", V_CONV, V_BGK, a["conv_w"].rearrange("l w (r c) -> (l w r) c", c=P)),
                    ("bgk", V_BGK, V_GNW, a["b_gk"].rearrange("l (r c) -> (l r) c", c=P)),
                    ("gnw", V_GNW, V_END, a["gla_norm_w"].rearrange("l (r c) -> (l r) c", c=P))]
            for _, lo, hi, src in rows:
                sp.dma_start(vrow[lo:hi, :], src).then_inc(rows_in, 16)
            sp.dma_start(crow[0:KD, :], a["c_prompt"].rearrange("b (r c) -> (b r) c", c=P)).then_inc(rows_in, 16)
            sp.dma_start(crow[KD:, :], a["c_sample"].rearrange("b (r c) -> (b r) c", c=P)).then_inc(rows_in, 16)
            sp.dma_start(srow[:], a["state_conv"].rearrange("l b w d -> (l b w) d")).then_inc(rows_in, 16)
            w = a["w_ada"][0].rearrange("(k p) f -> p k f", p=P)

            def ada(i):
                for u in range(2):
                    sp.wait_ge(ada_mm[u], i + 1)
                    sp.dma_start(g.slab[u][:], w[:, :, bass.ds(i * (2 * SW) + u * SW, SW)]).then_inc(ada_in[u], 16)

            with sp.Fori(0, NT // 2) as i:
                for u in range(2):
                    sp.wait_ge(x_turned, i * 2 + 1)
                    sp.dma_start(xin[u][:], xp[0, bass.ds(i * (2 * P) + u * P, P), :]).then_inc(x_in[u], 16)
                ada(i)
            sp.wait_ge(x_turned, NT)
            sp.dma_start(xin[0][0:TS, :], xs.rearrange("b t d -> (b t) d")).then_inc(x_in[0], 16)
            with sp.Fori(NT // 2, NSLAB // 2) as i:
                ada(i)
            sp.wait_ge(x_copied, NT + 2)
            sp.dma_start(g.xT_d.rearrange("k p t -> p k t"), xT[:]).then_inc(xT_out, 16)
            sp.wait_ge(xT_out, 16)

        @blk.tensor
        def _(pe):
            pe.sem_inc(x_turned, 1)
            for u in range(2):
                pe.sem_inc(ada_mm[u], 1)
            pe.wait_ge(const, 3)
            pe.wait_ge(rows_in, 16 * 9)
            nc.tensor.transpose(g.side[0][:, 0:V_END], vrow[:], g.ident[0:V_END, 0:V_END])
            nc.tensor.transpose(g.side[0][:, 128:200], crow[:], g.ident[0:72, 0:72])
            for k in range(KD):
                mm = nc.tensor.transpose(g.side[0][:, 256 + 16 * k:272 + 16 * k], srow[:, k * P:(k + 1) * P],
                                         g.ident[0:16, 0:16])
            mm.then_inc(rowsT, 1)

            def turn(u, n):
                out = g.acc[u][:, 0:2, :].rearrange("p a (b c) -> p (a b) c", b=4)
                for k in range(KD):
                    mm = nc.tensor.transpose(out[:, k, 0:n], xin[u][0:n, k * P:(k + 1) * P], g.ident[0:n, 0:n])
                mm.then_inc(x_turned, 1)

            def ada(i):
                for u in range(2):
                    pe.wait_ge(ada_in[u], i * 16 + 16)
                    pe.wait_ge(ada_row[u], i + 1)
                    for k in range(KD):
                        mm = nc.tensor.matmul(g.side[u][0:NB + 1, 0:SW], cact[:, k, :], g.slab[u][:, k, :],
                                              start=(k == 0), stop=(k == KD - 1))
                    mm.then_inc(ada_mm[u], 1)

            pe.wait_ge(cact_ready, 1)
            pe.wait_ge(vec_ready, 2)
            with pe.Fori(0, NT // 2) as i:
                for u in range(2):
                    pe.wait_ge(x_in[u], i * 16 + 16)
                    pe.wait_ge(x_copied, i * 2 + 1)
                    turn(u, P)
                ada(i)
            pe.wait_ge(x_in[0], 16 * (NT // 2 + 1))
            pe.wait_ge(x_copied, NT)
            turn(0, TS)
            FIRST = NT // 2 + 1
            with pe.Fori(NT // 2, FIRST) as i:
                ada(i)
            pe.wait_ge(x_copied, NT + 2)
            norm.pe(pe)
            with pe.Fori(FIRST, NSLAB // 2) as i:
                ada(i)
            for u in range(2):
                pe.wait_ge(ada_row[u], NSLAB // 2 + 1)
            for j in range(6 * KD):
                mm = nc.tensor.transpose(g.side[1][:, j * (NB + 1):(j + 1) * (NB + 1)], modrow[:, j * P:(j + 1) * P],
                                         g.ident[0:NB + 1, 0:NB + 1])
            mm.then_inc(ada_turned, 1)

        @blk.scalar
        def _(act):
            for u in range(2):
                act.sem_inc(ada_row[u], 1)
            act.wait_ge(rowsT, 1)
            nc.scalar.activation(csig[:], g.side[0][:, 128:200], ACT.Sigmoid).then_inc(csig_ready, 1)

            def ada(i):
                for u in range(2):
                    act.wait_ge(ada_mm[u], i + 2)
                    nc.scalar.activation(modrow[:, bass.ds(i * (2 * SW) + u * SW, SW)], g.side[u][0:NB + 1, 0:SW],
                                         ACT.Copy).then_inc(ada_row[u], 1)

            with act.Fori(0, NT // 2) as i:
                ada(i)
            norm.act(act, lambda k: (x_copied, NT + 2))
            with act.Fori(NT // 2, NSLAB // 2) as i:
                ada(i)
            act.wait_ge(amp_ready, 2)
            norm.act_prompt(act)

        @blk.vector
        def _(dve):
            dve.sem_inc(x_copied, 1)
            dve.wait_ge(csig_ready, 1)
            cps = g.side[0][:, 128:200].rearrange("p (b k) -> p k b", b=NB + 1)
            nc.vector.tensor_tensor(cact[:], cps, csig[:].rearrange("p (b k) -> p k b", b=NB + 1),
                                    ALU.mult).then_inc(cact_ready, 1)
            nc.vector.tensor_copy(g.vec[:], g.side[0][:, 0:V_END]).then_inc(vec_ready, 1)
            nc.vector.tensor_copy(g.stT[:], g.side[0][:, 256:384].rearrange("p (k c) -> p k c", k=KD)).then_inc(vec_ready, 1)

            def copy(u, at, n):
                src = g.acc[u][:, 0:2, :].rearrange("p a (b c) -> p (a b) c", b=4)
                nc.vector.tensor_copy(xT[:, :, at], src[:, :, 0:n]).then_inc(x_copied, 1)

            with dve.Fori(0, NT // 2) as i:
                for u in range(2):
                    dve.wait_ge(x_turned, i * 2 + (u + 2))
                    copy(u, bass.ds(i * (2 * P) + u * P, P), P)
            dve.wait_ge(x_turned, NT + 2)
            copy(0, slice(TP, T), TS)
            dve.wait_ge(x_copied, NT + 2)
            norm.dve(dve)
            dve.wait_ge(vec_ready, 2)
            dve.wait_ge(ada_turned, 1)
            nc.vector.tensor_tensor(g.mod[:], g.side[1][:, 0:6 * KD * (NB + 1)].rearrange("p (j b) -> p j b", b=NB + 1),
                                    g.vec[:, V_ADA:V_N1].unsqueeze(2).to_broadcast([P, 6 * KD, NB + 1]),
                                    ALU.add).then_inc(mod_ready, 1)
            dve.wait_ge(mod_ready, 1)
            for w, (seg, v) in enumerate(((SC1, V_N1), (SC2, V_N2))):
                nc.vector.scalar_tensor_tensor(out=g.amp[:, w], in0=g.mod[:, seg * KD:(seg + 1) * KD, :], scalar=1.0,
                                               in1=g.vec[:, v:v + KD].unsqueeze(2).to_broadcast([P, KD, NB + 1]),
                                               op0=ALU.add, op1=ALU.mult).then_inc(amp_ready, 1)
            dve.wait_ge(amp_ready, 2)
            norm.dve_sample(dve)


def head_order():
    steps = [(kind, t) for t in range(NT) for kind in ("score", "first", "second")]
    steps += [("score", NT), ("sample", 0), ("sample", 1), ("sample", 2), ("sample", 3)]
    events, n = [], 0
    for b in range(6):
        for m in range(KD * len(PIECES)):
            events.append(("mm", b, m))
            if m % 4 == 3 and n < len(steps):
                events.append(("gla", n, steps[n]))
                n += 1
        events.append(("block", b, None))
    assert n == len(steps)
    return events, len(steps)


def stage2(g):
    nc, a, sem, o = g.nc, g.a, g.sem, g.o
    w_in = a["w_in"][0].rearrange("(k p) f -> p k f", p=P)
    events, NSTEP = head_order()
    PROD0 = 5
    NBL = 12
    with ExitStack() as st:
        sb = g.maker(st)
        wz = sb("wz", [P, KD, RANK])
        wgk = sb("wgk", [RANK, DK])
        zT = sb("zT", [RANK, T])
        qd = sb("qd", [P, T])
        kd = sb("kd", [P, T])
        eb = sb("eb", [P, T])
        t1 = sb("t1", [P, T + 18])
        t2 = sb("t2", [P, T + 18])
        oT = sb("oT", [P, 2, T])
        kendT = sb("kendT", [P, NT + 1, DK])
        km = sb("km", [TS, NB, DK])
        v = sb("v", [P, NT + 1, DV])
        S = sb("S", [P, 2, DV])
        s0 = sb("s0", [P, NB, DV])
        scm = sb("scm", [P, P])
        rmask = sb("rmask", [P, T])
        maskp = sb("maskp", [P, P])
        masks = sb("masks", [TS, TS])
        seqm = sb("seqm", [TS, NB])

        zero = sb("zero", [P, D // 2])
        zero_ready, y_zero = sem("zero_ready"), sem("y_zero")

        consts0 = sem("c2_0")
        consts = sem("c2")
        z_in = sem("z_in")
        zT_ready = sem("zT_ready")
        slab_in = [sem(f"slab_in{i}") for i in range(2)]
        wgk_in, s0_in = sem("wgk_in"), sem("s0_in")
        prod = sem("prod")
        free = [sem(f"free{i}") for i in range(2)]
        side_done = sem("side_done")
        side_free = sem("side_free")
        gate_lin = sem("gate_lin")
        scan_ready = sem("scan_ready")
        d_ready = sem("d_ready")
        exps = sem("exps")
        kd_ready = sem("kd_ready")
        sig_ready = sem("sig_ready")
        gla_mm = sem("gla_mm")
        gla_v = sem("gla_v")
        o_copied = sem("o_copied")
        km_ready = sem("km_ready")
        osq_ready = sem("osq_ready")
        og_done = sem("og_done")
        s_reset = sem("s_reset")
        s_out = sem("s_out")
        kept_out = sem("kept_out")
        s_kept = sem("s_kept")
        dch, ach = sem("dch2"), sem("ach2")
        blk = st.enter_context(nc.Block())

        @blk.gpsimd
        def _(pool):
            pool.sem_inc(s_kept, 1)
            pool.memset(rmask[:], 1.0).then_inc(consts0, 1)
            pool.memset(maskp[:], 1.0).then_inc(consts0, 1)
            pool.memset(masks[:], 1.0).then_inc(consts0, 1)
            pool.memset(seqm[:], 1.0).then_inc(consts0, 1)
            pool.wait_ge(consts0, 4)
            pool.memset(rmask[:, 0:TP:CH], 0.0).then_inc(consts, 1)
            pool.memset(rmask[:, TP:T:LS], 0.0).then_inc(consts, 1)
            for k, (m, w, n) in enumerate(((maskp, CH, P), (masks, LS, TS))):
                v3 = m[:].rearrange("p (b t) -> p b t", t=w)
                pool.affine_select(out=v3, in_=v3, compare_op=ALU.is_ge, fill=0.0, base=0,
                                   pattern=[[w, n // w], [1, w]], channel_multiplier=-1).then_inc(consts0, 1)
                pool.wait_ge(consts0, 5 + k)
                pool.affine_select(out=v3, in_=v3, compare_op=ALU.is_ge, fill=0.0, base=0,
                                   pattern=[[-w, n // w], [0, w]], channel_multiplier=1).then_inc(consts, 1)
            pool.affine_select(out=seqm[:], in_=seqm[:], compare_op=ALU.is_ge, fill=0.0, base=0,
                               pattern=[[-LS, NB]], channel_multiplier=1).then_inc(consts0, 1)
            pool.wait_ge(consts0, 7)
            pool.affine_select(out=seqm[:], in_=seqm[:], compare_op=ALU.is_ge, fill=0.0, base=LS - 1,
                               pattern=[[LS, NB]], channel_multiplier=-1).then_inc(consts, 1)
            pool.memset(zero[:], 0.0).then_inc(zero_ready, 1)
            pool.wait_ge(zero_ready, 1)
            with pool.Fori(0, HEADS) as h:
                share = (NSLOT - MINSLOT) // HEADS
                src = zero[:].unsqueeze(1).to_broadcast([P, share * 2 // P, D // 2])
                pool.dma_start(g.y_d[bass.ds(h * share + MINSLOT, share), :].rearrange("(p b) (c d) -> p (b c) d", p=P, c=2), src).then_inc(y_zero, 16)
                pool.wait_ge(free[0], h * 6 + 7)
                pool.dma_start(g.yc_d[bass.ds(h * 2, 2)].rearrange("k p t -> p k t"), g.ycT[:, bass.ds(h * 2, 2), :]).then_inc(kept_out, 16)
                pool.wait_ge(gla_v, h * NSTEP + (NSTEP + 1))
                pool.dma_start(o["gla_p"][0, 0, bass.ds(h, 1)].rearrange("h p v -> p (h v)"), S[:, 0, :]).then_inc(s_out, 16)
                pool.dma_start(o["gla_s"][0, :, bass.ds(h, 1)].rearrange("b h p v -> p (b h) v"), s0[:]).then_inc(s_out, 16)
                pool.wait_ge(s_out, h * 32 + 32)
                pool.sem_inc(s_kept, 1)
                pool.wait_ge(og_done, h + 2)
                pool.dma_start(g.og_d[bass.ds(h * 2, 2)].rearrange("k p t -> p k t"), g.ogT[:, bass.ds(h * 2, 2), :]).then_inc(kept_out, 16)
            pool.wait_ge(kept_out, 32 * HEADS)
            pool.wait_ge(y_zero, 16 * HEADS)

        @blk.sync
        def _(sp):
            sp.dma_start(wz[:], w_in[:, :, C_Z:C_Z + RANK]).then_inc(z_in, 16)
            with sp.Fori(0, HEADS) as h:
                def slab(s, cols):
                    at = 0
                    for c, n in cols:
                        sp.dma_start(g.slab[s % 2][:, :, at:at + n], w_in[:, :, bass.ds(c, n)]).then_inc(slab_in[s % 2], 16)
                        at += n
                sp.wait_ge(prod, h * NBL + (PROD0 - 4))
                sp.dma_start(wgk[:], a["w_gk"][0][:, bass.ds(h * DK, DK)]).then_inc(wgk_in, 16)
                slab(0, [(h * DK + C_Q, DK), (h * DK + C_K, DK), (h * DV + C_G, P)])
                sp.wait_ge(prod, h * NBL + (PROD0 - 1))
                slab(1, [(h * DV + (C_G + P), P), (h * DV + C_V, P), (h * DV + (C_V + P), P)])
                sp.wait_ge(s_kept, h + 1)
                sp.dma_start(s0[:], a["state_gla"][0, :, bass.ds(h, 1)].rearrange("b h p v -> p (b h) v")).then_inc(s0_in, 16)
                for j in range(2):
                    if j == 0:
                        sp.wait_ge(prod, h * NBL + (PROD0 + 4))
                    else:
                        sp.wait_ge(side_done, h * 8 + 5)
                    slab(2 + j, [(h * (2 * P) + (c + j * P), P) for c in (C_C, C_H, C_B)])

        @blk.tensor
        def _(pe):
            pe.sem_inc(prod, PROD0 - 1)
            pe.wait_ge(z_in, 16)
            for k in range(KD):
                for i, (s, n) in enumerate(PIECES):
                    mm = nc.tensor.matmul(g.acc[0][0:RANK, i, 0:n], wz[:, k, :], g.hT[:, k, s:s + n],
                                          start=(k == 0), stop=(k == KD - 1))
            mm.then_inc(prod, 1)
            pe.wait_ge(zT_ready, 1)

            def product(slot, w, col, m):
                k, i = divmod(m, len(PIECES))
                s, n = PIECES[i]
                return nc.tensor.matmul(g.acc[slot][:, i, 0:n], w[:, k, col:col + P], g.hT[:, k, s:s + n],
                                        start=(k == 0), stop=(k == KD - 1))

            with pe.Fori(0, HEADS) as h:
                def claim(n):
                    pe.wait_ge(free[n % 2], h * (NBL // 2) + (n // 2 + 1))

                claim(0)
                pe.wait_ge(wgk_in, h * 16 + 16)
                for i, (s, n) in enumerate(PIECES):
                    mm = nc.tensor.matmul(g.acc[0][:, i, 0:n], wgk[:], zT[:, s:s + n], start=True, stop=True)
                mm.then_inc(prod, 1)
                for n, (s, col) in enumerate(((0, 0), (0, P), (0, 2 * P), (1, 0)), 1):
                    pe.wait_ge(slab_in[s], h * 96 + 48)
                    claim(n)
                    for m in range(KD * 3):
                        mm = product(n % 2, g.slab[s], col, m)
                    mm.then_inc(prod, 1)
                for t in range(NT + 1):
                    s, n = tok(t)
                    if t % 2 == 0:
                        pe.wait_ge(side_free, h * 8 + max(1, t // 2))
                        if t < 4:
                            pe.wait_ge(o_copied, h * (NT + 1) + 1)
                            pe.wait_ge(gla_v, h * NSTEP + 1)
                    for k in range(KD):
                        mm = nc.tensor.matmul(g.side[t // 2 % 2][0:n, (t % 2) * DV:(t % 2 + 1) * DV], g.hT[:, k, s:s + n],
                                              g.slab[1][:, k, P:3 * P], start=(k == 0), stop=(k == KD - 1))
                    if t % 2 == 1 or t == NT:
                        mm.then_inc(side_done, 1)
                pe.wait_ge(free[0], h * 6 + 3)
                for r in range(3):
                    if r < 2:
                        pe.wait_ge(side_free, h * 8 + (5, 7)[r])
                    for t in range(4 * r, min(4 * r + 4, NT + 1)):
                        s, n = tok(t)
                        mm = nc.tensor.transpose(g.side[(r + 1) % 2][0:n, (t % 4) * P:(t % 4 + 1) * P], oT[:, 1, s:s + n], g.ident[:])
                    mm.then_inc(side_done, 1)

                def gla_step(i, kind, t):
                    pe.wait_ge(gla_v, h * NSTEP + (i + 1))
                    upd, out = g.side[0], g.side[1]
                    s, n = tok(t)
                    if i == 0:
                        pe.wait_ge(side_free, h * 8 + 9)
                        pe.wait_ge(s_reset, h + 1)
                    if kind == "score":
                        mm = nc.tensor.matmul(upd[0:n, 0:n], kd[:, s:s + n], qd[:, s:s + n], start=True, stop=True)
                    elif kind == "first":
                        pe.wait_ge(o_copied, h * (NT + 1) + (t + 1))
                        for e in range(2):
                            nc.tensor.matmul(out[:, e * P:(e + 1) * P], v[:, t, e * P:(e + 1) * P], scm[:],
                                             start=(e == 0), stop=False, skip_group_check=True)
                            nc.tensor.matmul(out[:, e * P:e * P + CH], S[:, 0, e * P:(e + 1) * P], qd[:, s:s + CH],
                                             start=False, stop=False, skip_group_check=True)
                        mm = nc.tensor.matmul(upd[:, 0:DV], kendT[0:CH, t, :], v[0:CH, t, :], start=True, stop=True)
                    elif kind == "second":
                        for e in range(2):
                            nc.tensor.matmul(out[:, e * P + CH:(e + 1) * P], S[:, 1, e * P:(e + 1) * P], qd[:, s + CH:s + P],
                                             start=False, stop=(e == 1), skip_group_check=True)
                        mm = nc.tensor.matmul(upd[:, 0:DV], kendT[CH:P, t, :], v[CH:P, t, :], start=True, stop=True)
                    else:
                        if t == 0:
                            pe.wait_ge(o_copied, h * (NT + 1) + (NT + 1))
                            pe.wait_ge(s0_in, h * 16 + 16)
                            pe.wait_ge(km_ready, h + 1)
                            for e in range(2):
                                nc.tensor.matmul(out[:, e * P:e * P + TS], v[0:TS, NT, e * P:(e + 1) * P], scm[0:TS, 0:TS],
                                                 start=(e == 0), stop=False, skip_group_check=True)
                                for b in range(NB):
                                    c = e * P + b * LS
                                    nc.tensor.matmul(out[:, c:c + LS], s0[:, b, e * P:(e + 1) * P],
                                                     qd[:, TP + b * LS:TP + (b + 1) * LS], start=False,
                                                     stop=(e == 1 and b == NB - 1), skip_group_check=True)
                        for u in range(2):
                            mm = nc.tensor.matmul(upd[:, u * DV:(u + 1) * DV], km[:, 2 * t + u, :], v[0:TS, NT, :],
                                                  start=True, stop=True)
                    mm.then_inc(gla_mm, 1)

                for kind, x, y in events:
                    if kind == "gla":
                        gla_step(x, *y)
                    elif kind == "mm":
                        n = 5 + x
                        if y == 0:
                            claim(n)
                            pe.wait_ge(slab_in[x // 3], h * 96 + 96)
                        mm = product(n % 2, g.slab[x // 3], (x % 3) * P, y)
                        if y == KD * 3 - 1:
                            mm.then_inc(prod, 1)
                claim(11)
                for e in range(2):
                    pe.wait_ge(osq_ready, h * 2 + e + 1)
                    for i, (s, n) in enumerate(PIECES):
                        mm = nc.tensor.matmul(g.acc[1][:, i, 0:n], g.ones[:], (t1, t2)[e][:, s:s + n],
                                              start=(e == 0), stop=(e == 1))
                mm.then_inc(prod, 1)

        @blk.scalar
        def _(act):
            ch = Chain(act, ach)
            act.sem_inc(o_copied, 1)
            with act.Fori(0, HEADS) as h:
                ch.loop(h, 2)

                def product(n):
                    act.wait_ge(prod, h * NBL + (PROD0 + n + 1))

                product(0)
                act.wait_ge(og_done, h + 1)
                for d, s in zip(flat2(t2[:, 0:T]), slot2(g.acc[0])):
                    x = nc.scalar.activation(d, s, ACT.Identity, bias=g.vec[:, bass.ds(h + V_BGK, 1)])
                x.then_inc(free[0], 1)
                act.wait_ge(free[0], h * (NBL // 2) + 2)
                ch.step(nc.scalar.activation(t1[:, 0:T], t2[:, 0:T], ACT.Abs))
                ch.step(nc.scalar.activation(t1[:, 0:T], t1[:, 0:T], ACT.Exp, scale=-1.0))
                nc.scalar.activation(t1[:, 0:T], t1[:, 0:T], ACT.Ln, bias=1.0).then_inc(gate_lin, 1)
                act.wait_ge(scan_ready, h + 1)
                nc.scalar.activation(eb[:], t1[:, 0:T], ACT.Exp, scale=1.0 / 16).then_inc(exps, 1)
                nc.scalar.activation(t2[:, 0:T], t1[:, 0:T], ACT.Exp, scale=-1.0 / 16).then_inc(exps, 1)
                act.wait_ge(d_ready, h + 1)
                nc.scalar.activation(oT[:, 0, :], oT[:, 0, :], ACT.Exp, scale=1.0 / 16).then_inc(exps, 1)
                for e, (slot, t) in enumerate(((1, t1), (0, t2))):
                    product(3 + e)
                    act.wait_ge(exps, h * 3 + 3) if e == 0 else act.wait_ge(kd_ready, h + 1)
                    for d, s in zip(flat2(t[:, 0:T]), slot2(g.acc[slot])):
                        x = nc.scalar.activation(d, s, ACT.Sigmoid)
                    x.then_inc(sig_ready, 1)
                for kind, x, y in events:
                    if kind == "block" and x % 3 == 0:
                        product(5 + x)
                        dst = g.ycT[:, bass.ds(h * 2 + x // 3, 1), :].rearrange("p k t -> p (k t)")
                        for d, s in zip(flat2(dst), slot2(g.acc[(5 + x) % 2])):
                            i = nc.scalar.activation(d, s, ACT.Copy)
                        i.then_inc(free[(5 + x) % 2], 1)
                    if kind == "gla" and (y[0] == "second" or y == ("sample", 0)):
                        t = y[1] if y[0] == "second" else NT
                        s, n = tok(t)
                        act.wait_ge(gla_mm, h * NSTEP + x + 1)
                        src = g.side[1][:, 0:2 * P].rearrange("p (e c) -> p e c", e=2)[:, :, 0:n]
                        nc.scalar.activation(oT[:, :, s:s + n], src, ACT.Copy).then_inc(o_copied, 1)
                act.wait_ge(free[0], h * 6 + 7)
                act.wait_ge(o_copied, h * (NT + 1) + (NT + 2))
                for e in range(2):
                    nc.scalar.activation((t1, t2)[e][:, 0:T], oT[:, e, :], ACT.Square).then_inc(osq_ready, 1)
                product(11)
                for d, s in zip(flat2(t1[:, 0:T]), slot2(g.acc[1])):
                    x = nc.scalar.activation(d, s, ACT.Sqrt, scale=1.0 / DV, bias=g.eps[:])
                x.then_inc(free[1], 1)
                assert ch.n == ch.per

        @blk.vector
        def _(dve):
            V = nc.vector
            ch = Chain(dve, dch)
            for s in (*free, side_free, gla_v, og_done):
                dve.sem_inc(s, 1)
            dve.wait_ge(prod, PROD0)
            for d, s in zip(flat2(zT[:]), slot2(g.acc[0][0:RANK])):
                x = V.tensor_copy(d, s)
            x.then_inc(zT_ready, 1)
            dve.wait_ge(consts, 5)
            with dve.Fori(0, HEADS) as h:
                ch.loop(h, 12)

                def product(n):
                    dve.wait_ge(prod, h * NBL + (PROD0 + n + 1))

                dve.wait_ge(s_kept, h + 1)
                V.memset(S[:, 0, :], 0.0).then_inc(s_reset, 1)
                dve.wait_ge(gate_lin, h + 1)
                ch.step(V.scalar_tensor_tensor(out=t2[:, 0:T], in0=t2[:, 0:T], scalar=0.0, in1=t1[:, 0:T],
                                               op0=ALU.min, op1=ALU.subtract))
                V.tensor_tensor_scan(t1[:, 0:T], rmask[:], t2[:, 0:T], 0.0, ALU.mult, ALU.add).then_inc(scan_ready, 1)
                dve.wait_ge(scan_ready, h + 1)
                for lo, hi, w in ((0, TP, CH), (TP, T, LS)):
                    bv = t1[:, lo:hi].rearrange("p (c t) -> p c t", t=w)
                    x = V.tensor_tensor(oT[:, 0, lo:hi].rearrange("p (c t) -> p c t", t=w),
                                        bv[:, :, w - 1:w].to_broadcast([P, (hi - lo) // w, w]), bv, ALU.subtract)
                x.then_inc(d_ready, 1)
                product(1)
                dve.wait_ge(exps, h * 3 + 1)
                for d, s, e in zip(flat2(qd[:]), slot2(g.acc[1]), flat2(eb[:])):
                    x = V.scalar_tensor_tensor(out=d, in0=s, scalar=DK ** -0.5, in1=e, op0=ALU.mult, op1=ALU.mult)
                x.then_inc(free[1], 1)
                product(2)
                dve.wait_ge(exps, h * 3 + 3)
                for d, s, e in zip(flat2(kd[:]), slot2(g.acc[0]), flat2(t2[:, 0:T])):
                    x = V.tensor_tensor(d, s, e, ALU.mult)
                x.then_inc(kd_ready, 1)
                for d, s, e in zip(flat2(oT[:, 1, :]), slot2(g.acc[0]), flat2(oT[:, 0, :])):
                    x = V.tensor_tensor(d, s, e, ALU.mult)
                x.then_inc(free[0], 1)
                for e, (slot, t) in enumerate(((1, t1), (0, t2))):
                    dve.wait_ge(sig_ready, h * 2 + e + 1)
                    dst = g.ogT[:, bass.ds(h * 2 + e, 1), :].rearrange("p k t -> p (k t)")
                    for d, s, q in zip(flat2(dst), slot2(g.acc[slot]), flat2(t[:, 0:T])):
                        x = V.tensor_tensor(d, s, q, ALU.mult)
                    x.then_inc(free[slot], 1)
                for r in range(5):
                    dve.wait_ge(side_done, h * 8 + r + 1)
                    src = g.side[r % 2][:].rearrange("p (u v) -> p u v", u=2)
                    if r < 4:
                        x = V.tensor_copy(v[:, 2 * r:2 * r + 2, :], src)
                    else:
                        x = V.tensor_copy(v[0:TS, NT, :], src[0:TS, 0, :])
                    x.then_inc(side_free, 1)
                for r in range(3):
                    dve.wait_ge(side_done, h * 8 + 6 + r)
                    src = g.side[(r + 1) % 2][:].rearrange("p (u v) -> p u v", u=4)
                    if r < 2:
                        x = V.tensor_copy(kendT[:, 4 * r:4 * r + 4, :], src)
                    else:
                        x = V.tensor_copy(kendT[0:TS, NT, :], src[0:TS, 0, :])
                    x.then_inc(side_free, 1)
                dve.wait_ge(side_free, h * 8 + 9)
                V.tensor_tensor(km[:], kendT[0:TS, NT:NT + 1, :].to_broadcast([TS, NB, DK]),
                                seqm[:].unsqueeze(2).to_broadcast([TS, NB, DK]), ALU.mult).then_inc(km_ready, 1)
                dve.wait_ge(free[0], h * 6 + 4)
                pads = t2[:, T + 2 - TS:T + 18].rearrange("p (b c) -> p b c", b=NB)

                def gla_step(i, kind, t):
                    dve.wait_ge(gla_mm, h * NSTEP + i + 1)
                    upd = g.side[0]
                    s, n = tok(t)
                    if kind == "score":
                        x = V.tensor_tensor(scm[0:n, 0:n], upd[0:n, 0:n], (maskp if t < NT else masks)[:], ALU.mult)
                    elif kind in ("first", "second"):
                        c = kind == "second"
                        end = s + (c + 1) * CH - 1
                        if i == 1:
                            dve.wait_ge(s_reset, h + 1)
                        else:
                            dve.wait_ge(gla_v, h * NSTEP + (i + 1))
                        x = V.scalar_tensor_tensor(out=S[:, 1 - c, :], in0=S[:, int(c), :], scalar=eb[:, end:end + 1],
                                                   in1=upd[:, 0:DV], op0=ALU.mult, op1=ALU.add)
                    else:
                        for u in range(2):
                            b = 2 * t + u
                            end = TP + (b + 1) * LS - 1
                            x = V.scalar_tensor_tensor(out=s0[:, b, :], in0=s0[:, b, :], scalar=eb[:, end:end + 1],
                                                       in1=upd[:, u * DV:(u + 1) * DV], op0=ALU.mult, op1=ALU.add)
                    x.then_inc(gla_v, 1)

                def conv_tap(j, w):
                    return g.vec[:, bass.ds(h * 2 + (V_CONV + w * KD + j), 1)]

                for kind, x, y in events:
                    if kind == "gla":
                        gla_step(x, *y)
                    if kind != "block":
                        continue
                    n, j = 5 + x, x // 3
                    slot = n % 2
                    if x % 3 == 0:
                        V.memset(t2[:, 0:2], 0.0)
                        ch.step(V.tensor_copy(pads[:, :, 0:2], g.stT[:, bass.ds(h * 2 + j, 1), :].rearrange("p k (b w) -> p (k b) w", w=2)))
                    elif x % 3 == 1:
                        product(n)
                        dve.wait_ge(free[(n - 1) % 2], h * 6 + ((n - 1) // 2 + 2))
                        dst = g.ycT[:, bass.ds(h * 2 + j, 1), :].rearrange("p k t -> p (k t)")
                        for d, s, c in zip(padded3(t2), slot3(g.acc[slot]), flat3(dst)):
                            i = V.tensor_tensor(d, s, c, ALU.mult)
                        i.then_inc(free[slot], 1)
                        dve.wait_ge(free[slot], h * 6 + (n // 2 + 2))
                        W = T + 16
                        V.tensor_copy(g.lastT[:, bass.ds(h * 2 + j, 1), 0:2].rearrange("p k c -> p (k c)"), t2[:, TP:TP + 2])
                        V.tensor_copy(g.lastT[:, bass.ds(h * 2 + j, 1), 2:18].rearrange("p k (b c) -> p (k b) c", b=NB), pads[:, :, LS:LS + 2])
                        ch.step(V.tensor_scalar(t1[:, 0:W], t2[:, 0:W], conv_tap(j, 0), None, ALU.mult))
                        ch.step(V.scalar_tensor_tensor(out=t1[:, 0:W], in0=t2[:, 1:W + 1], scalar=conv_tap(j, 1), in1=t1[:, 0:W],
                                                       op0=ALU.mult, op1=ALU.add))
                        ch.step(V.scalar_tensor_tensor(out=t1[:, 0:W], in0=t2[:, 2:W + 2], scalar=conv_tap(j, 2), in1=t1[:, 0:W],
                                                       op0=ALU.mult, op1=ALU.add))
                    else:
                        product(n)
                        dst = g.ycT[:, bass.ds(h * 2 + j, 1), :].rearrange("p k t -> p (k t)")
                        out3 = [t1[:, 0:768].rearrange("p (a b) -> p a b", a=2), t1[:, 768:TP],
                                t1[:, TP + 2:T + 18].rearrange("p (b t) -> p b t", b=NB)[:, :, 0:LS]]
                        for d, s, c in zip(flat3(dst), slot3(g.acc[slot]), out3):
                            i = V.tensor_tensor(d, s, c, ALU.mult)
                        i.then_inc(free[slot], 1)
                dve.wait_ge(free[1], h * 6 + 7)
                ch.step(V.reciprocal(t1[:, 0:T], t1[:, 0:T]))
                for e in range(2):
                    dst = g.ogT[:, bass.ds(h * 2 + e, 1), :].rearrange("p k t -> p (k t)")
                    ch.step(V.tensor_tensor(oT[:, e, :], oT[:, e, :], t1[:, 0:T], ALU.mult))
                    x = V.scalar_tensor_tensor(out=dst, in0=oT[:, e, :], scalar=g.vec[:, V_GNW + e:V_GNW + e + 1], in1=dst,
                                               op0=ALU.mult, op1=ALU.mult)
                x.then_inc(og_done, 1)
                assert ch.n == ch.per, (ch.n, ch.per)


def stage3(g):
    nc, a, sem, o = g.nc, g.a, g.sem, g.o
    w_in = a["w_in"][0].rearrange("(k p) f -> p k f", p=P)
    w_oc = a["w_out_conv"][0].rearrange("(k p) f -> p k f", p=P)
    w_og = a["w_out_gla"][0].rearrange("(k p) f -> p k f", p=P)
    w_o = a["w_o"][0].rearrange("(k p) f -> p k f", p=P)
    with ExitStack() as st:
        sb = g.maker(st)
        hx = [sb(f"h_{x}", [P, KD, T], F32R) for x in ("hi", "lo")]
        bx = [sb(f"b_{x}", [P, KD, T], F32R) for x in ("hi", "lo")]
        wr = sb("wr", [P, KD, P])
        ws = [[sb(f"ws{i}{x}", [P, KD, P], F32R) for x in ("hi", "lo")] for i in range(2)]
        xb = [sb(f"xb{i}", [P, T]) for i in range(2)]
        xs = sb("xs", [P, 2, TS])
        merged = g.hT
        lrow = xb[1][0:18, 0:D]
        wr_in = sem("wr_in")
        w_hi = [sem(f"w_hi{i}") for i in range(2)]
        w_lo = [sem(f"w_lo{i}") for i in range(2)]
        prod = [sem(f"prod3_{i}") for i in range(2)]
        free = [sem(f"free3_{i}") for i in range(2)]
        x_hi, x_lo = sem("x_hi"), sem("x_lo")
        yc_in = [sem(f"yc_in{i}") for i in range(KD // 2)]
        xb_in = [sem(f"xb_in{i}") for i in range(2)]
        merged_done = sem("merged_done")
        x1_done = [sem(f"x1_done{i}") for i in range(2)]
        last_mm, lout, lready = sem("last_mm"), sem("lout"), sem("lready")
        blk = st.enter_context(nc.Block())

        @blk.sync
        def _(sp):
            def weights(p, m, w, col):
                sp.wait_ge(w_lo[1 - p], m + (1 + p))
                sp.dma_start(wr[:], w[:, :, bass.ds(col, P)]).then_inc(wr_in, 16)

            weights(0, 0, w_in, C_UA)
            for q in range(KD // 2):
                sp.wait_ge(x_lo, 2 * q + 2)
                sp.dma_start(g.hT[:, 2 * q:2 * q + 2, :], g.yc_d[2 * q:2 * q + 2].rearrange("k p t -> p k t")).then_inc(yc_in[q], 16)
            weights(1, 0, w_oc, 0)
            with sp.Fori(0, KD - 1) as j:
                weights(0, j + 1, w_in, j * P + (C_UA + P))
                weights(1, j + 1, w_oc, j * P + P)
            weights(0, KD, w_in, C_UB)
            weights(1, KD, w_og, 0)
            sp.wait_ge(lout, 32)
            for k in range(KD):
                if k >= 2:
                    sp.wait_ge(x_lo, 2 * KD + k - 1)
                sp.dma_start(xb[k % 2][:], g.og_d[k]).then_inc(xb_in[k % 2], 16)
            with sp.Fori(0, KD - 1) as j:
                weights(0, j + (KD + 1), w_in, j * P + (C_UB + P))
                weights(1, j + (KD + 1), w_og, j * P + P)
            with sp.Fori(0, KD // 2) as i:
                for r in range(2):
                    weights(r, i + 2 * KD, w_o, i * (2 * P) + r * P)
                    sp.wait_ge(merged_done, 2 * KD + 1)
                    sp.wait_ge(x1_done[r], i + 1)
                    sp.dma_start(xb[r][:], g.xT_d[bass.ds(i * 2 + r, 1)].rearrange("k p t -> p (k t)")).then_inc(xb_in[r], 16)

        @blk.gpsimd
        def _(pool):
            pool.wait_ge(lready, 1)
            pool.dma_start(o["conv_p"].rearrange("l b w d -> (l b w) d"), lrow[0:2, :]).then_inc(lout, 16)
            pool.dma_start(o["conv_s"].rearrange("l b w d -> (l b w) d"), lrow[2:18, :]).then_inc(lout, 16)
            pool.wait_ge(lout, 32)

        @blk.tensor
        def _(pe):
            for p in range(2):
                pe.sem_inc(prod[p], 1)
            out = g.acc[0][0:18, 0:2, :].rearrange("p a (b c) -> p (a b) c", b=4)
            for k in range(KD):
                mm = nc.tensor.transpose(out[:, k, :], g.lastT[:, k, :], g.ident[:])
            mm.then_inc(last_mm, 1)

            def block(p, m, x, s):
                pe.wait_ge(w_lo[p], m + 2)
                pe.wait_ge(free[p], m + 1)
                for k in range(KD):
                    pe.wait_ge(x_lo, s * KD + k + 1)
                    for n, (wi, xi) in enumerate(((0, 0), (0, 1), (1, 0))):
                        for i, (c, w) in enumerate(PIECES):
                            mm = nc.tensor.matmul(g.acc[p][:, i, 0:w], ws[p][wi][:, k, :], x[xi][:, k, c:c + w],
                                                  start=(k == 0 and n == 0), stop=(k == KD - 1 and n == 2))
                mm.then_inc(prod[p], 1)

            with pe.Fori(0, KD) as j:
                block(0, j, hx, 0)
                block(1, j, bx, 1)
            with pe.Fori(0, KD) as j:
                block(0, j + KD, hx, 0)
                block(1, j + KD, bx, 2)
            with pe.Fori(0, KD // 2) as i:
                for r in range(2):
                    block(r, i + 2 * KD, hx, 3)

        @blk.scalar
        def _(act):
            A = nc.scalar.activation

            def weights(p, m):
                act.wait_ge(wr_in, m * 32 + 16 * (p + 1))
                act.wait_ge(prod[p], m + 1)
                A(ws[p][0][:], wr[:], ACT.Copy).then_inc(w_hi[p], 1)

            def split(x, s, k):
                if s == 1:
                    act.wait_ge(yc_in[k // 2], 16)
                if s == 2:
                    act.wait_ge(xb_in[k % 2], 16 * (k // 2 + 1))
                A(x[0][:, k, :], xb[k % 2][:] if s == 2 else g.hT[:, k, :], ACT.Copy).then_inc(x_hi, 1)

            def gate(m, out):
                act.wait_ge(prod[0], m + 2)
                act.wait_ge(merged_done, m + 1)
                for d, s in zip(flat2(out), slot2(g.acc[0])):
                    x = A(d, s, ACT.Sigmoid)
                x.then_inc(free[0], 1)

            weights(0, 0)
            for k in range(KD):
                split(hx, 0, k)
            for k in range(KD):
                split(bx, 1, k)
            weights(1, 0)
            act.wait_ge(x_lo, 2 * KD)
            with act.Fori(0, KD) as j:
                weights(0, j + 1)
                gate(j, merged[:, bass.ds(j, 1), :].rearrange("p k t -> p (k t)"))
                weights(1, j + 1)
            act.wait_ge(prod[1], KD + 1)
            for k in range(KD):
                split(bx, 2, k)
            act.wait_ge(x_lo, 3 * KD)
            with act.Fori(0, KD - 1) as j:
                weights(0, j + (KD + 1))
                gate(j + KD, xb[0][:])
                weights(1, j + (KD + 1))
            weights(0, 2 * KD)
            gate(2 * KD - 1, xb[0][:])
            for k in range(KD):
                act.wait_ge(merged_done, KD + k + 2)
                split(hx, 3, k)
            weights(1, 2 * KD)
            with act.Fori(0, KD // 2 - 1) as i:
                for r in range(2):
                    weights(r, i + (2 * KD + 1))

        @blk.vector
        def _(dve):
            V = nc.vector
            for s in (*w_lo, free[1], merged_done, *x1_done):
                dve.sem_inc(s, 1)
            dve.wait_ge(last_mm, 1)
            V.tensor_copy(lrow, g.acc[0][0:18, 0:2, :].rearrange("p a c -> p (a c)")).then_inc(lready, 1)
            dve.wait_ge(lready, 1)
            dve.sem_inc(free[0], 1)

            def weights(p, m):
                dve.wait_ge(w_hi[p], m + 1)
                V.tensor_tensor(ws[p][1][:], wr[:], ws[p][0][:].bitcast(F32), ALU.subtract).then_inc(w_lo[p], 1)

            def split(x, s, k):
                dve.wait_ge(x_hi, s * KD + k + 1)
                V.tensor_tensor(x[1][:, k, :], xb[k % 2][:] if s == 2 else g.hT[:, k, :],
                                x[0][:, k, :].bitcast(F32), ALU.subtract).then_inc(x_lo, 1)

            def flat(ap, j):
                return ap[:, bass.ds(j, 1), :].rearrange("p k t -> p (k t)")

            def gla_part(j):
                dve.wait_ge(prod[1], j + (KD + 2))
                dve.wait_ge(free[0], j + (KD + 2))
                for d, s in zip(flat2(xb[0][:]), slot2(g.acc[1])):
                    x = V.tensor_tensor(d, s, d, ALU.mult)
                x.then_inc(free[1], 1)
                dve.wait_ge(free[1], j + (KD + 2))
                V.tensor_tensor(flat(merged, j), flat(merged, j), xb[0][:], ALU.add).then_inc(merged_done, 1)

            weights(0, 0)
            for k in range(KD):
                split(hx, 0, k)
            for k in range(KD):
                split(bx, 1, k)
            weights(1, 0)
            dve.wait_ge(x_lo, 2 * KD)
            with dve.Fori(0, KD) as j:
                weights(0, j + 1)
                dve.wait_ge(prod[1], j + 2)
                dve.wait_ge(free[0], j + 2)
                for d, s in zip(flat2(flat(merged, j)), slot2(g.acc[1])):
                    x = V.tensor_tensor(d, s, d, ALU.mult)
                x.then_inc(free[1], 1)
                dve.wait_ge(free[1], j + 2)
                dve.sem_inc(merged_done, 1)
                weights(1, j + 1)
            for k in range(KD):
                split(bx, 2, k)
            with dve.Fori(0, KD - 1) as j:
                weights(0, j + (KD + 1))
                gla_part(j)
                weights(1, j + (KD + 1))
            weights(0, 2 * KD)
            for k in range(KD - 1):
                split(hx, 3, k)
            gla_part(KD - 1)
            split(hx, 3, KD - 1)
            weights(1, 2 * KD)
            dve.wait_ge(x_lo, 4 * KD)

            def residual(i, last):
                for r in range(2):
                    if not last:
                        weights(r, i + (2 * KD + 1))
                    dve.wait_ge(prod[r], i + (2 * KD + 2))
                    dve.wait_ge(xb_in[r], i * 16 + 16 * (KD // 2 + 1))
                    dve.wait_ge(x1_done[r], i + 1)
                    gate = g.mod[:, bass.ds(i * 2 + (G1 * KD + r), 1), :]
                    d3, s3, x3 = flat3(flat(g.hT, i * 2 + r)), slot3(g.acc[r]), flat3(xb[r][:])
                    V.tensor_tensor(xs[:, r, :].rearrange("p (b t) -> p b t", b=NB), s3[2],
                                    gate[:, :, 1:NB + 1].rearrange("p k b -> p (k b)").unsqueeze(2).to_broadcast([P, NB, LS]), ALU.mult)
                    for e in range(2):
                        x = V.scalar_tensor_tensor(out=d3[e], in0=s3[e], scalar=gate[:, :, 0:1].rearrange("p k b -> p (k b)"),
                                                   in1=x3[e], op0=ALU.mult, op1=ALU.add)
                    x.then_inc(free[r], 1)
                    dve.wait_ge(free[r], i + (2 * KD + 2))
                    V.tensor_tensor(d3[2], xs[:, r, :].rearrange("p (b t) -> p b t", b=NB), x3[2], ALU.add).then_inc(x1_done[r], 1)

            with dve.Fori(0, KD // 2 - 1) as i:
                residual(i, False)
            with dve.Fori(KD // 2 - 1, KD // 2) as i:
                residual(i, True)


def second_norm(g):
    with ExitStack() as st:
        sb = g.maker(st)
        norm = Norm(g, "n2", 1, g.hT, g.h2T, [sb(f"sq2_{i}", [P, T]) for i in range(2)], sb("rst2", [P, T]))
        blk = st.enter_context(g.nc.Block())

        @blk.tensor
        def _(pe):
            norm.pe(pe)

        @blk.scalar
        def _(act):
            norm.act(act, None)
            norm.act_prompt(act)

        @blk.vector
        def _(dve):
            norm.dve(dve)
            norm.dve_sample(dve)


def stage4(g):
    nc, a, sem = g.nc, g.a, g.sem
    x1T, h2T = g.hT, g.h2T
    with ExitStack() as st:
        sb = g.maker(st)
        wsgu = [sb(f"ws{x}", [P, KD, FE]) for x in "gu"]
        wsd = sb("wsd", [P, 2, D])
        actT = sb("actT", [P, 2, T])
        t1 = sb("sh1", [P, T])
        gx = sb("gx", [P, KD, P + TS])
        g2 = sb("g2", [P, 2, D])
        bt = [sb(f"bt{i}", [P, D]) for i in range(2)]
        ht = [sb(f"ht{i}", [P, D]) for i in range(2)]
        rw = sb("rw", [P, KD, E])
        rb = sb("rb", [P, E])
        below = sb("below", [P, P])
        lower = sb("lower", [P, GROUPS, GROUPS])
        tokid = sb("tokid", [P, NT + 1])
        bnum = sb("bnum", [P, 2])
        zeros = sb("zeros", [P, NBLK])
        sc = sb("sc", [P, NT + 1, E])
        ch_ = sb("choice", [P, E])
        m8 = sb("m8", [P, GROUPS, 8])
        gs = sb("gs", [P, GROUPS])
        cmp = sb("cmp", [P, GROUPS, GROUPS])
        eq = sb("eq", [P, GROUPS, GROUPS])
        gr = sb("gr", [P, GROUPS])
        gmk = sb("gmk", [P, GROUPS])
        goff = sb("goff", [P, GROUPS])
        cm = sb("cm", [P, E])
        v8 = sb("v8", [P, 8])
        mr = sb("mr", [P, E])
        wsum = sb("wsum", [P, 1])
        wrec = sb("wrec", [P, 1])
        sel = sb("sel", [P, NT + 1, E])
        wn = sb("wn", [P, NT + 1, E])
        od = sb("od", [P, NT + 1, E])
        cnt_i = sb("cnt_i", [P, E], I32)
        nb_i = sb("nb_i", [P, E], I32)
        nb = sb("nb", [P, E])
        pend = sb("pend", [P, E])
        pst = sb("pst", [P, E])
        dest = sb("dest", [P, NT + 1, E])
        pick = sb("pick", [P, NT + 1, E])
        d8f = sb("d8f", [P, NT + 1, TOPK])
        be = sb("be", [P, 6])
        used = sb("used", [P, E])
        gi = sb("gi", [P, 2], I32)
        gp = sb("gp", [P, 2])
        trow = [sb(f"trow{i}", [P, P]) for i in range(2)]

        c0, c1, c2 = sem("c4_0"), sem("c4_1"), sem("c4_2")
        r_in, w_in = sem("router_in"), sem("ws_in")
        gx_ready = sem("gx_ready")
        g2_mm, g2_done, g2_out = sem("g2_mm"), sem("g2_done"), sem("g2_out")
        sh_mm = sem("sh_mm")
        sh_sig, sh_v = sem("sh_sig"), sem("sh_v")
        x_mm, y_mm, h_mm, l_mm = sem("x_mm"), sem("y_mm"), sem("h_mm"), sem("l_mm")
        bt_mul, bt_add = sem("bt_mul"), sem("bt_add")
        ht_done = sem("ht_done")
        bt_out, ht_out = [sem(f"bt_out{i}") for i in range(2)], [sem(f"ht_out{i}") for i in range(2)]
        sc_ready, sc_used = sem("sc_ready"), sem("sc_used")
        sel_done = sem("sel_done")
        rank_mm = sem("rank_mm")
        dest_done = sem("dest_done")
        be_done, be_mm, row_done = sem("be_done"), sem("be_mm"), sem("row_done")
        tok_zero, tok_out, tok_in, tok_mm, idx_done = sem("tok_zero"), sem("tok_out"), sem("tok_in"), sem("tok_mm"), sem("idx_done")
        dch = sem("dch4")
        blk = st.enter_context(nc.Block())
        NTT = NT + 1

        @blk.sync
        def _(sp):
            sp.dma_start(rw[:], a["router_w"][0].rearrange("(k p) f -> p k f", p=P)).then_inc(r_in, 16)
            sp.dma_start(rb[:], a["router_bias"].to_broadcast([P, E])).then_inc(r_in, 16)
            sp.dma_start(wsgu[0][:], a["ws_gate"][0].rearrange("(k p) f -> p k f", p=P)).then_inc(w_in, 16)
            sp.dma_start(wsgu[1][:], a["ws_up"][0].rearrange("(k p) f -> p k f", p=P)).then_inc(w_in, 16)
            sp.dma_start(wsd[:], a["ws_down"][0].rearrange("(k p) f -> p k f", p=P)).then_inc(w_in, 16)
            sp.wait_ge(g2_done, 2)
            sp.dma_start(g.g2_d.rearrange("w p d -> p w d"), g2[:]).then_inc(g2_out, 16)
            for t in range(NTT):
                s, n = tok(t)
                sp.wait_ge(ht_done, 2 * t + 2)
                sp.dma_start(g.h2_d[s:s + n, :], ht[t % 2][0:n, :]).then_inc(ht_out[t % 2], 16)
            for t in range(NTT):
                s, n = tok(t)
                sp.wait_ge(bt_add, t + 1)
                sp.dma_start(g.base_d[s:s + n, :], bt[t % 2][0:n, :]).then_inc(bt_out[t % 2], 16)
            sp.wait_ge(tok_out, 16 * NTT * TOPK)
            table = g.tok_d.rearrange("(b s) o -> b (s o)", s=B_)
            sp.dma_start(trow[0][:], table[0:P, :]).then_inc(tok_in, 16)
            sp.dma_start(trow[1][0:NBLK - P, :], table[P:NBLK, :]).then_inc(tok_in, 16)
            sp.wait_ge(g2_out, 16)
            for i in range(2):
                sp.wait_ge(ht_out[i], 16 * (5 - i))
                sp.wait_ge(bt_out[i], 16 * (5 - i))

        @blk.gpsimd
        def _(pool):
            pool.memset(below[:], 1.0).then_inc(c0, 1)
            pool.memset(lower[:], 1.0).then_inc(c0, 1)
            pool.memset(zeros[:], 0.0).then_inc(c0, 1)
            pool.wait_ge(c0, 3)
            pool.affine_select(out=below[:], in_=below[:], compare_op=ALU.is_gt, fill=0.0, base=0,
                               pattern=[[1, P]], channel_multiplier=-1).then_inc(c1, 1)
            pool.affine_select(out=lower[:], in_=lower[:], compare_op=ALU.is_gt, fill=0.0, base=0,
                               pattern=[[1, GROUPS], [-1, GROUPS]], channel_multiplier=0).then_inc(c1, 1)
            pool.iota(tokid[:], pattern=[[P, NTT]], base=0, channel_multiplier=1, allow_small_or_imprecise_dtypes=True).then_inc(c1, 1)
            pool.iota(bnum[:], pattern=[[P, 2]], base=0, channel_multiplier=1, allow_small_or_imprecise_dtypes=True).then_inc(c1, 1)
            pool.dma_start(g.tok_d.rearrange("(p b) o -> p (b o)", p=P), zeros[:]).then_inc(tok_zero, 16)
            pool.wait_ge(tok_zero, 16)
            pool.wait_ge(c1, 4)
            pool.wait_ge(dest_done, 2)
            for t in range(NTT):
                n = tok(t)[1]
                for k in range(TOPK):
                    pool.indirect_dma_start(out=g.tok_d, out_offset=bass.IndirectOffsetOnAxis(ap=g.dest8[0:n, t, k:k + 1], axis=0),
                                            in_=tokid[0:n, t:t + 1], in_offset=None).then_inc(tok_out, 16)
            pool.wait_ge(tok_out, 16 * NTT * TOPK)

        @blk.tensor
        def _(pe):
            M = nc.tensor.matmul
            pe.wait_ge(gx_ready, 2)
            for w, (lo, n) in enumerate(((0, P), (P, TS))):
                out = g.acc[w][0:n, 0:2, :].rearrange("p a (b c) -> p (a b) c", b=4)
                for k in range(KD):
                    mm = nc.tensor.transpose(out[:, k, :], gx[:, k, lo:lo + n], g.ident[:])
                mm.then_inc(g2_mm, 1)
            pe.wait_ge(r_in, 32)
            for t in range(NTT):
                s, n = tok(t)
                for i in range(2):
                    if t > 0:
                        pe.wait_ge(ht_done, 2 * t - 1 + i)
                    for k in range(4):
                        mm = nc.tensor.transpose(g.side[i][0:n, k * P:(k + 1) * P], h2T[:, 4 * i + k, s:s + n], g.ident[:])
                    mm.then_inc(h_mm, 1)
                if t > 0:
                    pe.wait_ge(sc_ready, t)
                else:
                    pe.wait_ge(g2_done, 2)
                for k in range(KD):
                    mm = M(g.acc[1][0:n, 2, 0:E], h2T[:, k, s:s + n], rw[:, k, :], start=(k == 0), stop=(k == KD - 1))
                mm.then_inc(l_mm, 1)
            pe.wait_ge(sc_ready, NTT)

            def shared(e):
                for u in range(2):
                    for k in range(KD):
                        for i, (s, n) in enumerate(PIECES):
                            mm = M(g.acc[u][:, i, 0:n], wsgu[u][:, k, e * P:(e + 1) * P], h2T[:, k, s:s + n],
                                   start=(k == 0), stop=(k == KD - 1))
                    mm.then_inc(sh_mm, 1)

            pe.wait_ge(w_in, 16 * 3)
            shared(0)
            pe.wait_ge(sel_done, NTT)
            pe.wait_ge(ht_done, 2 * NTT)
            pe.wait_ge(c1, 4)
            for t in range(NTT):
                out = g.side[t // NT][:, (t % NT) * E:(t % NT + 1) * E]
                M(out, below[:], sel[:, t, :], start=True, stop=(t == 0))
                for q in range(t):
                    M(out, g.ones[:], sel[:, q, :], start=False, stop=(q == t - 1))
            for t in range(NTT):
                mm = M(g.side[1][:, E:2 * E], g.ones[:], sel[:, t, :], start=(t == 0), stop=(t == NTT - 1))
            mm.then_inc(rank_mm, 1)
            pe.wait_ge(sh_v, 2)
            shared(1)
            pe.wait_ge(be_done, 2)
            for c in range(6):
                mm = M(g.side[c // 3][0:1, c % 3 * P:(c % 3 + 1) * P], be[:, c:c + 1], g.ident[:], start=True, stop=True)
            mm.then_inc(be_mm, 1)
            pe.wait_ge(sh_v, 4)
            for t in range(NTT):
                s, n = tok(t)
                if t > 0:
                    pe.wait_ge(bt_mul, t)
                for hf in range(2):
                    for f in range(2):
                        mm = M(g.acc[1][0:n, hf, :], actT[:, f, s:s + n], wsd[:, f, hf * 512:(hf + 1) * 512],
                               start=(f == 0), stop=(f == 1))
                mm.then_inc(y_mm, 1)
                if t > 0:
                    pe.wait_ge(bt_add, t)
                out = g.acc[0][0:n, 0:2, :].rearrange("p a (b c) -> p (a b) c", b=4)
                for k in range(KD):
                    mm = nc.tensor.transpose(out[:, k, :], x1T[:, k, s:s + n], g.ident[:])
                mm.then_inc(x_mm, 1)
            pe.wait_ge(tok_in, 32)
            pe.wait_ge(row_done, 1)
            nc.tensor.transpose(g.side[0][:, 0:P], trow[0][:], g.ident[:])
            nc.tensor.transpose(g.side[0][:, P:NBLK], trow[1][0:NBLK - P, :], g.ident[0:NBLK - P, 0:NBLK - P]).then_inc(tok_mm, 1)

        @blk.scalar
        def _(act):
            for t in range(NTT):
                s, n = tok(t)
                for i in range(2):
                    act.wait_ge(h_mm, 2 * t + 1 + i)
                    if t >= 2 and i == 0:
                        act.wait_ge(ht_out[t % 2], 16 * (t // 2))
                    nc.scalar.activation(ht[t % 2][0:n, i * 512:(i + 1) * 512], g.side[i][0:n, :], ACT.Copy).then_inc(ht_done, 1)
                act.wait_ge(l_mm, t + 1)
                nc.scalar.activation(sc[0:n, t, :], g.acc[1][0:n, 2, 0:E], ACT.Sigmoid).then_inc(sc_ready, 1)
            for e in range(2):
                act.wait_ge(sh_mm, 2 * e + 1)
                if e == 1:
                    act.wait_ge(sh_v, 2)
                for d, s in zip(flat2(t1[:]), slot2(g.acc[0])):
                    x = nc.scalar.activation(d, s, ACT.Sigmoid)
                x.then_inc(sh_sig, 1)

        @blk.vector
        def _(dve):
            V = nc.vector
            ch = Chain(dve, dch)
            V.tensor_copy(gx[:, :, 0:P], g.mod[:, G2 * KD:, 0:1].to_broadcast([P, KD, P])).then_inc(gx_ready, 1)
            V.tensor_copy(gx[:, :, P:].rearrange("p k (b t) -> p k b t", b=NB),
                          g.mod[:, G2 * KD:, 1:NB + 1].unsqueeze(3).to_broadcast([P, KD, NB, LS])).then_inc(gx_ready, 1)
            V.memset(sel[:, NT, :], 0.0)
            V.memset(wn[:, NT, :], 0.0)
            V.memset(g2[:, 1, :], 0.0)
            ch.step(V.memset(od[:, NT, :], 0.0))
            for w, n in enumerate((P, TS)):
                dve.wait_ge(g2_mm, w + 1)
                V.tensor_copy(g2[0:n, w, :], g.acc[w][0:n, 0:2, :].rearrange("p a c -> p (a c)")).then_inc(g2_done, 1)

            def shared(e):
                dve.wait_ge(sh_sig, e + 1)
                for d, s in zip(flat2(t1[:]), slot2(g.acc[0])):
                    x = V.tensor_tensor(d, s, d, ALU.mult)
                x.then_inc(sh_v, 1)
                dve.wait_ge(sh_v, 2 * e + 1)
                dve.wait_ge(sh_mm, 2 * e + 2)
                for d, s, q in zip(flat2(actT[:, e, :]), slot2(g.acc[1]), flat2(t1[:])):
                    x = V.tensor_tensor(d, s, q, ALU.mult)
                x.then_inc(sh_v, 1)

            dve.wait_ge(g2_done, 2)
            dve.wait_ge(c1, 4)
            for t in range(NTT):
                n = tok(t)[1]
                dve.wait_ge(sc_ready, t + 1)
                ch.step(V.tensor_tensor(ch_[0:n], sc[0:n, t, :], rb[0:n], ALU.add))
                for q in range(GROUPS):
                    x = V.max(m8[0:n, q, :], ch_[0:n, q * EG:(q + 1) * EG])
                ch.step(x)
                ch.step(V.tensor_tensor(gs[0:n], m8[0:n, :, 0], m8[0:n, :, 1], ALU.add))
                other = gs[0:n].unsqueeze(1).to_broadcast([n, GROUPS, GROUPS])
                own = gs[0:n].unsqueeze(2).to_broadcast([n, GROUPS, GROUPS])
                V.tensor_tensor(cmp[0:n], other, own, ALU.is_gt)
                ch.step(V.tensor_tensor(eq[0:n], other, own, ALU.is_equal))
                ch.step(V.tensor_tensor(eq[0:n], eq[0:n], lower[0:n], ALU.mult))
                ch.step(V.tensor_tensor(cmp[0:n], cmp[0:n], eq[0:n], ALU.add))
                ch.step(V.tensor_reduce(gr[0:n], cmp[0:n], AX, ALU.add))
                ch.step(V.tensor_scalar(gmk[0:n], gr[0:n], float(TOPG) - 0.5, None, ALU.is_lt))
                ch.step(V.tensor_scalar(goff[0:n], gmk[0:n], BIG, -BIG, ALU.mult, ALU.add))
                c3 = cm[0:n].rearrange("p (g e) -> p g e", g=GROUPS)
                ch.step(V.tensor_tensor(c3, ch_[0:n].rearrange("p (g e) -> p g e", g=GROUPS),
                                        gmk[0:n].unsqueeze(2).to_broadcast([n, GROUPS, EG]), ALU.mult))
                ch.step(V.tensor_tensor(c3, c3, goff[0:n].unsqueeze(2).to_broadcast([n, GROUPS, EG]), ALU.add))
                ch.step(V.max(v8[0:n], cm[0:n]))
                ch.step(V.match_replace(mr[0:n], v8[0:n], cm[0:n], 2 * BIG))
                ch.step(V.tensor_scalar(sel[0:n, t, :], mr[0:n], BIG, None, ALU.is_ge))
                V.tensor_tensor(wn[0:n, t, :], sc[0:n, t, :], sel[0:n, t, :], ALU.mult).then_inc(sc_used, 1)
                dve.wait_ge(sc_used, t + 1)
                ch.step(V.tensor_reduce(wsum[0:n], wn[0:n, t, :], AX, ALU.add))
                ch.step(V.reciprocal(wrec[0:n], wsum[0:n]))
                ch.step(V.tensor_scalar(wn[0:n, t, :], wn[0:n, t, :], wrec[0:n], SCALE_R, ALU.mult, ALU.mult))
                ch.step(V.tensor_tensor_scan(od[0:n, t, :], g.ones[0:n, 0:E], sel[0:n, t, :], 0.0, ALU.mult, ALU.add))
                V.tensor_tensor(od[0:n, t, :], od[0:n, t, :], sel[0:n, t, :], ALU.mult).then_inc(sel_done, 1)
            shared(0)
            dve.wait_ge(rank_mm, 1)
            dve.wait_ge(sel_done, NTT)
            ch.step(V.tensor_scalar(cnt_i[:], g.side[1][:, E:2 * E], float(B_ - 1), None, ALU.add))
            ch.step(V.tensor_scalar(nb_i[:], cnt_i[:], 7, None, ALU.arith_shift_right))
            ch.step(V.tensor_copy(nb[:], nb_i[:]))
            ch.step(V.tensor_tensor_scan(pend[:], g.ones[:, 0:E], nb[:], 0.0, ALU.mult, ALU.add))
            ch.step(V.tensor_tensor(pst[:], pend[:], nb[:], ALU.subtract))
            ch.step(V.tensor_scalar(pst[:], pst[:], float(B_), None, ALU.mult))
            V.tensor_tensor(dest[:, 0:NT, :], g.side[0][:].rearrange("p (t e) -> p t e", t=NT),
                            pst[:].unsqueeze(1).to_broadcast([P, NT, E]), ALU.add)
            ch.step(V.tensor_tensor(dest[:, NT, :], g.side[1][:, 0:E], pst[:], ALU.add))
            for what, out in ((dest, d8f), (wn, g.w8)):
                for k in range(TOPK):
                    ch.step(V.scalar_tensor_tensor(out=pick[:], in0=od[:], scalar=float(k + 1), in1=what[:],
                                                   op0=ALU.is_equal, op1=ALU.mult))
                    ch.step(V.tensor_reduce(out[:, :, k], pick[:], AX, ALU.add))
                if out is d8f:
                    V.tensor_copy(g.dest8[:], d8f[:]).then_inc(dest_done, 2)
            ch.step(V.tensor_scalar(used[:], nb[:], 0.5, None, ALU.is_ge))
            ch.step(V.tensor_tensor(pst[:], pend[:], nb[:], ALU.subtract))
            for c in range(2):
                b = bnum[:, c:c + 1]
                ch.step(V.tensor_scalar(cm[:], pend[:], b, None, ALU.is_le))
                ch.step(V.tensor_reduce(be[:, c:c + 1], cm[:], AX, ALU.add))
                ch.step(V.tensor_scalar(be[:, c:c + 1], be[:, c:c + 1], float(E - 1), None, ALU.min))
                ch.step(V.scalar_tensor_tensor(out=cm[:], in0=pst[:], scalar=b, in1=used[:], op0=ALU.is_le, op1=ALU.mult))
                ch.step(V.tensor_reduce(be[:, 2 + c:3 + c], cm[:], AX, ALU.add))
                ch.step(V.tensor_scalar(be[:, 2 + c:3 + c], be[:, 2 + c:3 + c], -1.0, None, ALU.add))
                ch.step(V.scalar_tensor_tensor(out=cm[:], in0=pst[:], scalar=b, in1=used[:], op0=ALU.is_equal, op1=ALU.mult))
                ch.step(V.tensor_reduce(be[:, 4 + c:5 + c], cm[:], AX, ALU.add))
            ch.step(V.tensor_copy(gi[:], be[:, 2:4]))
            ch.step(V.tensor_scalar(gi[:], gi[:], 1, None, ALU.bitwise_and))
            ch.step(V.tensor_copy(gp[:], gi[:]))
            ch.step(V.scalar_tensor_tensor(out=be[:, 4:6], in0=gp[:], scalar=1.0, in1=be[:, 4:6], op0=ALU.add, op1=ALU.mult))
            V.scalar_tensor_tensor(out=be[:, 4:6], in0=be[:, 2:4], scalar=4.0, in1=be[:, 4:6], op0=ALU.mult, op1=ALU.add).then_inc(be_done, 2)
            ch.step(V.tensor_scalar(cnt_i[0:1, 0:1], pend[0:1, E - 1:E], 1.0, None, ALU.add))
            ch.step(V.tensor_scalar(g.row[0:1, 6 * P:6 * P + 1], cnt_i[0:1, 0:1], 1, None, ALU.arith_shift_right))
            dve.wait_ge(be_mm, 1)
            for i in range(2):
                x = V.tensor_copy(g.row[0:1, i * 3 * P:(i + 1) * 3 * P], g.side[i][0:1, 0:3 * P])
            x.then_inc(row_done, 1)
            shared(1)
            for t in range(NTT):
                n = tok(t)[1]
                b = bt[t % 2][0:n, :]
                if t >= 2:
                    dve.wait_ge(bt_out[t % 2], 16 * (t // 2))
                dve.wait_ge(y_mm, t + 1)
                V.tensor_tensor(b, g.acc[1][0:n, 0:2, :].rearrange("p a c -> p (a c)"), g2[0:n, t // NT, :], ALU.mult).then_inc(bt_mul, 1)
                dve.wait_ge(bt_mul, t + 1)
                dve.wait_ge(x_mm, t + 1)
                V.tensor_tensor(b, g.acc[0][0:n, 0:2, :].rearrange("p a c -> p (a c)"), b, ALU.add).then_inc(bt_add, 1)
            dve.wait_ge(tok_mm, 1)
            V.tensor_copy(g.idx[:], g.side[0][:, 0:NBLK]).then_inc(idx_done, 1)


def stage5(g):
    nc, a, sem = g.nc, g.a, g.sem
    with ExitStack() as st:
        sb = g.maker(st)
        raw = [sb(f"raw{i}", [P, KD, 2 * FE]) for i in range(2)]
        rawd = [sb(f"rawd{i}", [P, 2, D]) for i in range(2)]
        wgu = [sb(f"wgu{x}", [P, 2, KD, 2 * FE], F32R) for x in "hl"]
        wd = [sb(f"wd{x}", [P, 2, 2, D], F32R) for x in "hl"]
        xg = [sb(f"xg{i}", [P, D]) for i in range(2)]
        xe = [[sb(f"xe{i}{x}", [P, KD, B_], F32R) for x in "hl"] for i in range(2)]
        sg = [sb(f"sg{i}", [P, FE]) for i in range(2)]
        hh = [sb(f"hh{i}", [P, FE]) for i in range(2)]
        hT = [[sb(f"hTe{i}{x}", [P, 2, B_], F32R) for x in "hl"] for i in range(2)]
        ys = [sb(f"ys{i}", [P, D]) for i in range(2)]

        def pair(name):
            return [sem(f"{name}{i}") for i in range(2)]

        raw_in, rawd_in = pair("raw_in"), pair("rawd_in")
        gu_hi, d_hi = sem("gu_hi"), sem("d_hi")
        gu_lo, d_lo = sem("gu_lo"), sem("d_lo")
        PARTS = [(0, 2), (2, 5), (5, KD)]
        NPT = len(PARTS)
        GU0, D0 = 2 * NPT, 2
        x_in = pair("xg_in")
        x_mm, xhi, xlo = pair("xe_mm"), pair("xhi"), pair("xlo")
        gu_mm = pair("gu_mm")
        sg_ready, hm, h_ready = pair("sg_ready"), pair("hm"), pair("h_ready")
        h_mm, hhi, hlo = pair("h_mm"), pair("hhi"), pair("hlo")
        y_mm, ys_ready, y_out = pair("ye_mm"), pair("ys_ready"), pair("y_out")
        blk = st.enter_context(nc.Block())
        xps = g.acc[0][:, 0:2, :]
        gps = [g.side[0], g.side[1]]
        hps = g.acc[0][:, 2, :]
        yps = g.acc[1][:, 0:2, :]
        NPAIR = NBLK // 2
        LEAST = -(-T * TOPK // (2 * B_))

        def expert(eng, b):
            return eng.value_load(g.row[0:1, bass.ds(b, 1)], min_val=0, max_val=E - 1)

        def word(eng, b):
            return eng.value_load(g.row[0:1, bass.ds(b + 4 * P, 1)], min_val=0, max_val=4 * E - 2)

        def pairs_in_use(eng):
            return eng.value_load(g.row[0:1, 6 * P:6 * P + 1], min_val=LEAST, max_val=NPAIR)

        def if_first(eng, w, part):
            for p in range(2):
                with eng.If(w % 4 == p + 1):
                    part(p, w >> 2)


        @blk.sync
        def _(sp):
            with sp.Fori(0, NBLK) as b:
                def load(p, gr):
                    e = expert(sp, b)
                    sp.wait_ge(gu_lo, gr * NPT + (GU0 - NPT))
                    for w, name in enumerate(("we_gate", "we_up")):
                        sp.dma_start(raw[p][:, :, w * FE:(w + 1) * FE],
                                     a[name][0][bass.ds(e, 1)].rearrange("e (k p) f -> p (e k) f", p=P)).then_inc(raw_in[p], 16)
                    sp.wait_ge(d_lo, gr + (D0 - 1))
                    sp.dma_start(rawd[p][:], a["we_down"][0][bass.ds(e, 1)].rearrange("e (k p) f -> p (e k) f", p=P)).then_inc(rawd_in[p], 16)

                if_first(sp, word(sp, b), load)

        @blk.gpsimd
        def _(pool):
            used = pairs_in_use(pool)

            def gather(c):
                for u in range(2):
                    pool.wait_ge(x_mm[u], c + 1)
                    b = 2 * c + u
                    pool.indirect_dma_start(out=xg[u][:], out_offset=None, in_=g.h2_d,
                                            in_offset=bass.IndirectOffsetOnAxis(ap=g.idx[:, b:b + 1], axis=0)).then_inc(x_in[u], 16)

            for c in range(NPAIR):
                if c < LEAST:
                    gather(c)
                else:
                    with pool.If(used > c):
                        gather(c)
            for u in range(2):
                pool.wait_ge(y_out[u], used * 16 + 16)

        @blk.tensor
        def _(pe):
            M = nc.tensor.matmul

            def turn(u, c):
                pe.wait_ge(x_in[u], c * 16 + 16)
                pe.wait_ge(xlo[1 - u], c + (u + 1))
                out = xps.rearrange("p a (b c) -> p (a b) c", b=4)
                for k in range(KD):
                    mm = nc.tensor.transpose(out[:, k, :], xg[u][:, k * P:(k + 1) * P], g.ident[:])
                mm.then_inc(x_mm[u], 1)

            def three(out, x, w, first, last):
                M(out, x[1], w[0], start=first, stop=False)
                M(out, x[0], w[1], start=False, stop=False)
                return M(out, x[0], w[0], start=False, stop=last)

            def gate_up_part(u, parity, ks):
                for k in ks:
                    ws = [w[:, bass.ds(parity, 1), k, :].rearrange("p g n -> p (g n)") for w in wgu]
                    mm = three(gps[u][:], [x[:, k, :] for x in xe[u]], ws, k == 0, k == KD - 1)
                return mm

            def gate_up_begin(u, c, w):
                pe.wait_ge(xlo[u], c + 2)
                pe.wait_ge(gu_lo, (w >> 2) * NPT + (GU0 + 1))
                pe.wait_ge(h_ready[u], c + 1)
                gate_up_part(u, (w >> 2) % 2, range(*PARTS[0]))

            def gate_up_end(u, w):
                pe.wait_ge(gu_lo, (w >> 2) * NPT + (GU0 + NPT))
                gate_up_part(u, (w >> 2) % 2, range(PARTS[0][1], KD)).then_inc(gu_mm[u], 1)

            def turn_h(u, c):
                pe.wait_ge(h_ready[u], c + 2)
                pe.wait_ge(hlo[1 - u], c + (u + 1))
                for f in range(2):
                    mm = nc.tensor.transpose(hps[:, f * P:(f + 1) * P], hh[u][:, f * P:(f + 1) * P], g.ident[:])
                mm.then_inc(h_mm[u], 1)

            def down(u, c, w):
                pe.wait_ge(hlo[u], c + 2)
                pe.wait_ge(d_lo, (w >> 2) + (D0 + 1))
                pe.wait_ge(ys_ready[1 - u], c + (u + 1))
                for hf in range(2):
                    for f in range(2):
                        ws = [x[:, bass.ds((w >> 2) % 2, 1), f, hf * 512:(hf + 1) * 512].rearrange("p g n -> p (g n)") for x in wd]
                        mm = three(yps[:, hf, :], [x[:, f, :] for x in hT[u]], ws, f == 0, f == 1)
                mm.then_inc(y_mm[u], 1)

            used = pairs_in_use(pe)
            turn(0, 0)
            turn(1, 0)
            w0 = word(pe, 0)
            gate_up_begin(0, 0, w0)
            gate_up_end(0, w0)
            with pe.Fori(0, NPAIR - 1) as i:
                with pe.If(used > i + 1):
                    w = [word(pe, i * 2 + d) for d in range(3)]
                    for u in range(2):
                        turn(u, i + 1)
                        gate_up_begin(1 - u, i + u, w[u + 1])
                        turn_h(u, i)
                        gate_up_end(1 - u, w[u + 1])
                        down(u, i, w[u])
            L = used - 1
            w = [word(pe, L * 2 + d) for d in range(2)]
            gate_up_begin(1, L, w[1])
            turn_h(0, L)
            gate_up_end(1, w[1])
            down(0, L, w[0])
            turn_h(1, L)
            down(1, L, w[1])

        @blk.scalar
        def _(act):
            A = nc.scalar.activation
            for u in range(2):
                act.sem_inc(xhi[u], 1)
                act.sem_inc(ys_ready[u], 1)
                act.sem_inc(y_out[u], 16)

            def split_gu(w):
                def part(p, gr):
                    act.wait_ge(raw_in[p], (gr >> 1) * 32 + 32)
                    for lo, hi in PARTS:
                        A(wgu[0][:, p, lo:hi, :], raw[p][:, lo:hi, :], ACT.Copy).then_inc(gu_hi, 1)
                if_first(act, w, part)

            def split_d(w):
                def part(p, gr):
                    act.wait_ge(rawd_in[p], (gr >> 1) * 16 + 16)
                    A(wd[0][:, p], rawd[p][:], ACT.Copy).then_inc(d_hi, 1)
                if_first(act, w, part)

            def split_x(u, c):
                act.wait_ge(x_mm[u], c + 2)
                act.wait_ge(gu_mm[u], c + 1)
                A(xe[u][0][:].rearrange("p k s -> p (k s)").rearrange("p (a c) -> p a c", a=2), xps, ACT.Copy).then_inc(xhi[u], 1)

            def sigmoid(u, c):
                act.wait_ge(gu_mm[u], c + 2)
                act.wait_ge(h_ready[u], c + 1)
                A(sg[u][:], gps[u][:, 0:FE], ACT.Sigmoid).then_inc(sg_ready[u], 1)

            def split_h(u, c):
                act.wait_ge(h_mm[u], c + 2)
                act.wait_ge(y_mm[u], c + 1)
                A(hT[u][0][:], hps[:, 0:2 * B_].rearrange("p (f s) -> p f s", f=2), ACT.Copy).then_inc(hhi[u], 1)

            def store(u, c, b):
                act.wait_ge(y_mm[u], c + 2)
                act.wait_ge(y_out[u], c * 16 + 16)
                A(ys[u][:].rearrange("p (a c) -> p a c", a=2), yps, ACT.Copy).then_inc(ys_ready[u], 1)
                act.wait_ge(ys_ready[u], c + 2)
                act.dma_start(g.y_d[bass.ds(b * B_, B_), :], ys[u][:]).then_inc(y_out[u], 16)

            used = pairs_in_use(act)
            w = [word(act, b) for b in range(2)]
            split_x(0, 0)
            split_gu(w[0])
            split_x(1, 0)
            split_gu(w[1])
            split_d(w[0])
            sigmoid(0, 0)
            with act.Fori(0, NPAIR - 1) as i:
                with act.If(used > i + 1):
                    for u in range(2):
                        split_x(u, i + 1)
                        split_h(u, i)
                        if u == 0:
                            w = [word(act, i * 2 + (1 + d)) for d in range(3)]
                        split_gu(w[u + 1])
                        sigmoid(1 - u, i + u)
                        split_d(w[u])
                        store(u, i, i * 2 + u)
            L = used - 1
            split_h(0, L)
            split_d(word(act, L * 2 + 1))
            sigmoid(1, L)
            store(0, L, L * 2)
            split_h(1, L)
            store(1, L, L * 2 + 1)

        @blk.vector
        def _(dve):
            V = nc.vector
            for u in range(2):
                dve.sem_inc(xlo[u], 1)
                dve.sem_inc(hlo[u], 1)
                dve.sem_inc(h_ready[u], 1)
                dve.sem_inc(x_mm[u], 1)
                dve.sem_inc(gu_mm[u], 1)
                dve.sem_inc(h_mm[u], 1)
                dve.sem_inc(y_mm[u], 1)
            dve.sem_inc(gu_lo, GU0)
            dve.sem_inc(d_lo, D0)

            def split_gu(w):
                def part(p, gr):
                    for k, (lo, hi) in enumerate(PARTS):
                        dve.wait_ge(gu_hi, gr * NPT + (k + 1))
                        V.tensor_tensor(wgu[1][:, p, lo:hi, :], raw[p][:, lo:hi, :],
                                        wgu[0][:, p, lo:hi, :].bitcast(F32), ALU.subtract).then_inc(gu_lo, 1)
                if_first(dve, w, part)

            def split_d(w):
                def part(p, gr):
                    dve.wait_ge(d_hi, gr + 1)
                    V.tensor_tensor(wd[1][:, p], rawd[p][:], wd[0][:, p].bitcast(F32), ALU.subtract).then_inc(d_lo, 1)
                if_first(dve, w, part)

            def split_x(u, c):
                dve.wait_ge(xhi[u], c + 2)
                V.tensor_tensor(xe[u][1][:].rearrange("p k s -> p (k s)").rearrange("p (a c) -> p a c", a=2), xps,
                                xe[u][0][:].bitcast(F32).rearrange("p k s -> p (k s)").rearrange("p (a c) -> p a c", a=2),
                                ALU.subtract).then_inc(xlo[u], 1)

            def split_h(u, c):
                dve.wait_ge(hhi[u], c + 1)
                V.tensor_tensor(hT[u][1][:], hps[:, 0:2 * B_].rearrange("p (f s) -> p f s", f=2), hT[u][0][:].bitcast(F32),
                                ALU.subtract).then_inc(hlo[u], 1)

            def swiglu(u, c):
                dve.wait_ge(sg_ready[u], c + 1)
                dve.wait_ge(h_mm[u], c + 1)
                V.tensor_tensor(sg[u][:], gps[u][:, 0:FE], sg[u][:], ALU.mult).then_inc(hm[u], 1)
                dve.wait_ge(hm[u], c + 1)
                V.tensor_tensor(hh[u][:], gps[u][:, FE:2 * FE], sg[u][:], ALU.mult).then_inc(h_ready[u], 1)

            used = pairs_in_use(dve)
            w = [word(dve, b) for b in range(2)]
            split_x(0, 0)
            split_gu(w[0])
            split_x(1, 0)
            split_gu(w[1])
            swiglu(0, 0)
            split_d(w[0])
            with dve.Fori(0, NPAIR - 1) as i:
                with dve.If(used > i + 1):
                    for u in range(2):
                        split_x(u, i + 1)
                        split_h(u, i)
                        if u == 0:
                            w = [word(dve, i * 2 + (1 + d)) for d in range(3)]
                        split_gu(w[u + 1])
                        swiglu(1 - u, i + u)
                        split_d(w[u])
            L = used - 1
            split_h(0, L)
            split_d(word(dve, L * 2 + 1))
            swiglu(1, L)
            split_h(1, L)


def stage6(g):
    nc, a, sem, o = g.nc, g.a, g.sem, g.o
    NTT = NT + 1
    with ExitStack() as st:
        sb = g.maker(st)
        R = 6
        yg = [sb(f"yg{i}", [P, D]) for i in range(R)]
        base = [sb(f"base{i}", [P, D]) for i in range(2)]
        g2 = sb("g2b", [P, 2, D])
        fw = sb("fw", [P, D])
        acc = [sb(f"ysum{i}", [P, D]) for i in range(2)]
        sqs = sb("sqs", [P, D])
        ss = sb("ss", [P, NTT])
        rt = sb("rt", [P, NTT])
        rc = sb("rc", [P, NTT])
        yo = [sb(f"yo{i}", [P, D]) for i in range(2)]
        c_in = sem("c6_in")
        b_in = [sem(f"b6_in{i}") for i in range(2)]
        y_in = [sem(f"y6_in{i}") for i in range(R)]
        add = sem("add6")
        x2m, x2_ready = sem("x2m"), sem("x2_ready")
        sum_ready, root_ready, inv_ready = sem("sum6"), sem("root6"), sem("inv6")
        yo_ready = sem("yo_ready")
        out_done = [sem(f"out{i}") for i in range(2)]
        blk = st.enter_context(nc.Block())

        @blk.gpsimd
        def _(pool):
            n_ = 0
            for t in range(NTT):
                n = tok(t)[1]
                for k in range(TOPK):
                    if n_ >= R:
                        pool.wait_ge(add, n_ - R + 1)
                    pool.indirect_dma_start(out=yg[n_ % R][0:n, :], out_offset=None, in_=g.y_d,
                                            in_offset=bass.IndirectOffsetOnAxis(ap=g.dest8[0:n, t, k:k + 1], axis=0)
                                            ).then_inc(y_in[n_ % R], 16)
                    n_ += 1

        def store(sp, t):
            s, n = tok(t)
            sp.wait_ge(yo_ready, t + 1)
            dst = o["y_p"][0, s:s + n, :] if t < NT else o["y_s"].rearrange("b t d -> (b t) d")
            sp.dma_start(dst, yo[t % 2][0:n, :]).then_inc(out_done[t % 2], 16)

        @blk.sync
        def _(sp):
            sp.dma_start(fw[:], a["final_norm_w"].rearrange("(o d) -> o d", o=1).to_broadcast([P, D])).then_inc(c_in, 16)
            sp.dma_start(g2[:], g.g2_d.rearrange("w p d -> p w d")).then_inc(c_in, 16)
            for t in range(NTT):
                s, n = tok(t)
                if t >= 2:
                    sp.wait_ge(x2_ready, t - 1)
                sp.dma_start(base[t % 2][0:n, :], g.base_d[s:s + n, :]).then_inc(b_in[t % 2], 16)
                if t >= 1:
                    store(sp, t - 1)
            store(sp, NTT - 1)
            for i in range(2):
                sp.wait_ge(out_done[i], 16 * (5 - i))

        @blk.scalar
        def _(act):
            for t in range(NTT):
                n = tok(t)[1]
                act.wait_ge(x2_ready, t + 1)
                if t > 0:
                    act.wait_ge(root_ready, t)
                nc.scalar.activation(sqs[0:n, :], acc[t % 2][0:n, :], ACT.Square, accum_out=ss[0:n, t:t + 1]).then_inc(sum_ready, 1)
                act.wait_ge(sum_ready, t + 1)
                nc.scalar.activation(rt[0:n, t:t + 1], ss[0:n, t:t + 1], ACT.Sqrt, scale=1.0 / D, bias=g.eps[0:n]).then_inc(root_ready, 1)

        @blk.vector
        def _(dve):
            V = nc.vector
            n_ = 0

            def final(t):
                n = tok(t)[1]
                dve.wait_ge(root_ready, t + 1)
                V.reciprocal(rc[0:n, t:t + 1], rt[0:n, t:t + 1]).then_inc(inv_ready, 1)
                dve.wait_ge(inv_ready, t + 1)
                if t >= 2:
                    dve.wait_ge(out_done[t % 2], 16 * (t // 2))
                V.scalar_tensor_tensor(out=yo[t % 2][0:n, :], in0=acc[t % 2][0:n, :], scalar=rc[0:n, t:t + 1], in1=fw[0:n, :],
                                       op0=ALU.mult, op1=ALU.mult).then_inc(yo_ready, 1)

            dve.wait_ge(c_in, 32)
            for t in range(NTT):
                n = tok(t)[1]
                s = acc[t % 2][0:n, :]
                for k in range(TOPK):
                    dve.wait_ge(y_in[n_ % R], 16 * (n_ // R + 1))
                    row, w = yg[n_ % R][0:n, :], g.w8[0:n, t, k:k + 1]
                    if k == 0:
                        if t >= 2:
                            dve.wait_ge(yo_ready, t - 1)
                        x = V.tensor_scalar(s, row, w, None, ALU.mult)
                    else:
                        dve.wait_ge(add, n_)
                        x = V.scalar_tensor_tensor(out=s, in0=row, scalar=w, in1=s, op0=ALU.mult, op1=ALU.add)
                    x.then_inc(add, 1)
                    n_ += 1
                dve.wait_ge(add, n_)
                V.tensor_tensor(s, s, g2[0:n, t // NT, :], ALU.mult).then_inc(x2m, 1)
                dve.wait_ge(x2m, t + 1)
                dve.wait_ge(b_in[t % 2], 16 * (t // 2 + 1))
                V.tensor_tensor(s, s, base[t % 2][0:n, :], ALU.add).then_inc(x2_ready, 1)
                if t >= 1:
                    final(t - 1)
            final(NTT - 1)


_INS = ["x_prompt", "x_sample", "state_conv", "state_gla", "c_prompt", "c_sample", "w_ada", "b_ada", "norm1_w", "w_in",
        "conv_w", "w_gk", "b_gk", "gla_norm_w", "w_out_conv", "w_out_gla", "w_o", "norm2_w", "router_w", "router_bias",
        "we_gate", "we_up", "we_down", "ws_gate", "ws_up", "ws_down", "final_norm_w"]
_OUTS = [("y_p", (1, TP, D)), ("y_s", (NB, LS, D)), ("conv_p", (1, 1, CW - 1, D)), ("gla_p", (1, 1, HEADS, DK, DV)),
         ("conv_s", (1, NB, CW - 1, D)), ("gla_s", (1, NB, HEADS, DK, DV))]


def kernel(**inputs):
    import concourse.bacc as bacc
    from concourse.bass_utils import run_bass_kernel_spmd

    nc = bacc.Bacc("TRN2", target_bir_lowering=False, num_devices=1)
    arrays = {name: np.ascontiguousarray(inputs[name]) for name in _INS}
    ins = {name: nc.dram_tensor(name, x.shape, F32, kind="ExternalInput").ap() for name, x in arrays.items()}
    outs = {name: nc.dram_tensor(f"out_{name}", shape, F32, kind="ExternalOutput").ap() for name, shape in _OUTS}
    build(nc, ins, outs)
    r = run_bass_kernel_spmd(nc, [arrays], core_ids=[0])
    return tuple(r.results[0][f"out_{name}"] for name, _ in _OUTS)
```
